# Optimizing a Trainium2 kernel written in Bass

```python
import math
import jax, jax.numpy as jnp
from jax import lax
import numpy as np

D_MODEL = 1024
BATCH = 1
SEQ = 256
DEPTH = 1

HEAD_DIM = 64
N_HEADS_FOX = 8
N_HEADS_DIL = 8
D_FOX = N_HEADS_FOX * HEAD_DIM
D_DIL = N_HEADS_DIL * HEAD_DIM
D_MIX = D_FOX + D_DIL
D_PROJ = 3 * D_FOX + 3 * D_DIL + N_HEADS_FOX
DIL_PATTERNS = ((128, 1), (512, 4), (2048, 16))
BLOCK = 128
ROPE_THETA = 10000.0
N_GROUPS = 4
EXPERTS_PER_GROUP = 8
N_EXPERTS = N_GROUPS * EXPERTS_PER_GROUP
TOP_K_INNER = 2
D_EXPERT = 512
EPS = 1e-6
NEG = -1e30
FORGET_BIAS_INIT = 3.0


def rmsnorm(x, g):
    xf = x.astype(jnp.float32)
    y = xf * lax.rsqrt(jnp.mean(xf * xf, axis=-1, keepdims=True) + EPS)
    return (y * g.astype(jnp.float32)).astype(x.dtype)

def rope(x, pos):
    dh = x.shape[-1]
    inv_freq = 1.0 / (ROPE_THETA ** (jnp.arange(0, dh, 2, dtype=jnp.float32) / dh))
    ang = pos[:, None] * inv_freq[None, :]
    cos, sin = jnp.cos(ang), jnp.sin(ang)
    xf = x.astype(jnp.float32)
    x1, x2 = xf[..., : dh // 2], xf[..., dh // 2:]
    out = jnp.concatenate([x1 * cos - x2 * sin, x2 * cos + x1 * sin], axis=-1)
    return out.astype(x.dtype)

def forgetting_attention(q, k, v, logf):
    B, H, S, dh = q.shape
    scale = 1.0 / math.sqrt(dh)
    c = jnp.cumsum(logf, axis=-1)
    nb = S // BLOCK
    qb = q.reshape(B, H, nb, BLOCK, dh).transpose(2, 0, 1, 3, 4)
    cb = c.reshape(B, H, nb, BLOCK).transpose(2, 0, 1, 3)
    kpos = jnp.arange(S)

    def one_block(args):
        qi, ci, i = args
        s = jnp.einsum('bhqd,bhkd->bhqk', qi, k).astype(jnp.float32) * scale
        s = s + ci[..., None] - c[:, :, None, :]
        qpos = i * BLOCK + jnp.arange(BLOCK)
        mask = kpos[None, :] <= qpos[:, None]
        s = jnp.where(mask, s, NEG)
        p = jax.nn.softmax(s, axis=-1)
        return jnp.einsum('bhqk,bhkd->bhqd', p.astype(v.dtype), v)

    out = lax.map(one_block, (qb, cb, jnp.arange(nb)))
    return out.transpose(1, 2, 0, 3, 4).reshape(B, H, S, dh)

def dilated_branch(q, k, v, window, dilation):
    B, H, S, dh = q.shape
    scale = 1.0 / math.sqrt(dh)
    wsub = window // dilation
    unit = dilation * BLOCK
    Sp = -(-S // unit) * unit
    L = Sp // dilation
    nb = L // BLOCK
    pad = ((0, 0), (0, 0), (0, Sp - S), (0, 0))

    def split(t):
        t = jnp.pad(t, pad).reshape(B, H, L, dilation, dh).transpose(0, 1, 3, 2, 4)
        return t.reshape(B, H, dilation, nb, BLOCK, dh)

    def with_prev(t):
        prev = jnp.pad(t, ((0, 0), (0, 0), (0, 0), (1, 0), (0, 0), (0, 0)))[:, :, :, :-1]
        return jnp.concatenate([prev, t], axis=4)

    qs = split(q)
    kw = with_prev(split(k))
    vw = with_prev(split(v))
    s = jnp.einsum('bhrnqd,bhrnkd->bhrnqk', qs, kw).astype(jnp.float32) * scale
    ql = jnp.arange(BLOCK)[:, None]
    kl = jnp.arange(2 * BLOCK)[None, :]
    dist = ql + BLOCK - kl
    kpos = jnp.arange(nb)[:, None, None] * BLOCK + kl[None] - BLOCK
    valid = (dist >= 0) & (dist <= wsub) & (kpos >= 0)
    s = jnp.where(valid, s, NEG)
    m = jnp.max(s, axis=-1, keepdims=True)
    p = jnp.exp(s - m)
    l = jnp.sum(p, axis=-1, keepdims=True)
    o = jnp.einsum('bhrnqk,bhrnkd->bhrnqd', (p / l).astype(v.dtype), vw)
    lse = (m + jnp.log(l))[..., 0]
    o = o.reshape(B, H, dilation, L, dh).transpose(0, 1, 3, 2, 4).reshape(B, H, Sp, dh)[:, :, :S]
    lse = lse.reshape(B, H, dilation, L).transpose(0, 1, 3, 2).reshape(B, H, Sp)[:, :, :S]
    return o, lse

def dilated_attention(q, k, v):
    outs, lses = [], []
    for window, dilation in DIL_PATTERNS:
        o, lse = dilated_branch(q, k, v, window, dilation)
        outs.append(o)
        lses.append(lse)
    w = jax.nn.softmax(jnp.stack(lses, axis=0), axis=0)
    o = jnp.sum(w[..., None] * jnp.stack(outs, axis=0).astype(jnp.float32), axis=0)
    return o.astype(q.dtype)

def token_mixer(xn, w_in, b_forget, q_norm_fox, k_norm_fox, q_norm_dil, k_norm_dil,
                out_norm_fox, out_norm_dil, w_out):
    B, S, _ = xn.shape
    proj = xn @ w_in
    o1 = 3 * D_FOX
    o2 = o1 + 3 * D_DIL
    qa, ka, va = jnp.split(proj[..., :o1], 3, axis=-1)
    qb, kb, vb = jnp.split(proj[..., o1:o2], 3, axis=-1)
    fa = proj[..., o2:]

    def heads(t, h):
        return t.reshape(B, S, h, HEAD_DIM).transpose(0, 2, 1, 3)

    qa = rmsnorm(heads(qa, N_HEADS_FOX), q_norm_fox)
    ka = rmsnorm(heads(ka, N_HEADS_FOX), k_norm_fox)
    va = heads(va, N_HEADS_FOX)
    logf = jax.nn.log_sigmoid(fa.astype(jnp.float32) + b_forget.astype(jnp.float32))
    logf = logf.transpose(0, 2, 1)
    oa = forgetting_attention(qa, ka, va, logf)

    pos = jnp.arange(S, dtype=jnp.float32)
    qb = rope(rmsnorm(heads(qb, N_HEADS_DIL), q_norm_dil), pos)
    kb = rope(rmsnorm(heads(kb, N_HEADS_DIL), k_norm_dil), pos)
    vb = heads(vb, N_HEADS_DIL)
    ob = dilated_attention(qb, kb, vb)

    oa = rmsnorm(oa.transpose(0, 2, 1, 3).reshape(B, S, D_FOX), out_norm_fox)
    ob = rmsnorm(ob.transpose(0, 2, 1, 3).reshape(B, S, D_DIL), out_norm_dil)
    return jnp.concatenate([oa, ob], axis=-1) @ w_out

def hierarchical_moe(xn, w_router_group, b_router_group, w_router_expert, b_router_expert,
                     w_gate, w_up, w_down):
    B, S, D = xn.shape
    t = xn.reshape(B * S, D)
    zg = (t @ w_router_group).astype(jnp.float32) + b_router_group.astype(jnp.float32)
    pg = jax.nn.softmax(zg, axis=-1)
    pg_top, g_sel = lax.top_k(pg, 1)
    ze = jnp.einsum('td,gde->tge', t, w_router_expert).astype(jnp.float32)
    ze = ze + b_router_expert.astype(jnp.float32)
    ze_sel = jnp.take_along_axis(ze, g_sel[:, :, None], axis=1)[:, 0]
    v2, i2 = lax.top_k(ze_sel, TOP_K_INNER)
    gates = jax.nn.softmax(v2, axis=-1) * pg_top
    eid = g_sel * EXPERTS_PER_GROUP + i2
    combine = jnp.sum(jax.nn.one_hot(eid, N_EXPERTS, dtype=jnp.float32) * gates[..., None], axis=1)
    y = jnp.zeros((B * S, D), jnp.float32)
    for e in range(N_EXPERTS):
        h = jax.nn.silu(t @ w_gate[e]) * (t @ w_up[e])
        y = y + combine[:, e:e + 1] * (h @ w_down[e]).astype(jnp.float32)
    return y.astype(xn.dtype).reshape(B, S, D)

def first_inputs(seed: int = 0) -> dict:
    key = jax.random.key(seed)
    ks = jax.random.split(key, 20)
    f32 = jnp.float32

    def nrm(k, shape, scale):
        return jax.random.normal(k, shape, f32) * scale

    def gain(k, shape):
        return 1.0 + 0.02 * jax.random.normal(k, shape, f32)

    return {
        "x": jax.random.normal(ks[0], (BATCH, SEQ, D_MODEL), f32),
        "norm_mix": gain(ks[1], (DEPTH, D_MODEL)),
        "w_in": nrm(ks[2], (DEPTH, D_MODEL, D_PROJ), D_MODEL ** -0.5),
        "b_forget": FORGET_BIAS_INIT + 0.1 * jax.random.normal(ks[3], (DEPTH, N_HEADS_FOX), f32),
        "q_norm_fox": gain(ks[4], (DEPTH, HEAD_DIM)),
        "k_norm_fox": gain(ks[5], (DEPTH, HEAD_DIM)),
        "q_norm_dil": gain(ks[6], (DEPTH, HEAD_DIM)),
        "k_norm_dil": gain(ks[7], (DEPTH, HEAD_DIM)),
        "out_norm_fox": gain(ks[8], (DEPTH, D_FOX)),
        "out_norm_dil": gain(ks[9], (DEPTH, D_DIL)),
        "w_out": nrm(ks[10], (DEPTH, D_MIX, D_MODEL), D_MIX ** -0.5),
        "norm_ffn": gain(ks[11], (DEPTH, D_MODEL)),
        "w_router_group": nrm(ks[12], (DEPTH, D_MODEL, N_GROUPS), D_MODEL ** -0.5),
        "b_router_group": nrm(ks[13], (DEPTH, N_GROUPS), 0.01),
        "w_router_expert": nrm(ks[14], (DEPTH, N_GROUPS, D_MODEL, EXPERTS_PER_GROUP), D_MODEL ** -0.5),
        "b_router_expert": nrm(ks[15], (DEPTH, N_GROUPS, EXPERTS_PER_GROUP), 0.01),
        "w_gate": nrm(ks[16], (DEPTH, N_EXPERTS, D_MODEL, D_EXPERT), D_MODEL ** -0.5),
        "w_up": nrm(ks[17], (DEPTH, N_EXPERTS, D_MODEL, D_EXPERT), D_MODEL ** -0.5),
        "w_down": nrm(ks[18], (DEPTH, N_EXPERTS, D_EXPERT, D_MODEL), D_EXPERT ** -0.5),
    }

def first_block(x, norm_mix, w_in, b_forget, q_norm_fox, k_norm_fox, q_norm_dil, k_norm_dil,
              out_norm_fox, out_norm_dil, w_out, norm_ffn, w_router_group, b_router_group,
              w_router_expert, b_router_expert, w_gate, w_up, w_down):
    h = x
    for l in range(DEPTH):
        xn = rmsnorm(h, norm_mix[l])
        h = h + token_mixer(xn, w_in[l], b_forget[l], q_norm_fox[l], k_norm_fox[l],
                            q_norm_dil[l], k_norm_dil[l], out_norm_fox[l], out_norm_dil[l],
                            w_out[l])
        hn = rmsnorm(h, norm_ffn[l])
        h = h + hierarchical_moe(hn, w_router_group[l], b_router_group[l], w_router_expert[l],
                                 b_router_expert[l], w_gate[l], w_up[l], w_down[l])
    return h


CHUNK = 64
MIX_WIDTH = D_MODEL
LRU_WIDTH = MIX_WIDTH // 2
LRU_BLOCKS = 8
LRU_BLOCK = LRU_WIDTH // LRU_BLOCKS
CONV_WIDTH = 4
LRU_C = 8.0
ATT_WIDTH = MIX_WIDTH - LRU_WIDTH
ATT_HEADS = 8
ATT_HEAD_DIM = ATT_WIDTH // ATT_HEADS
LEFT_CHUNKS = 8
BAND_CHUNKS = LEFT_CHUNKS + 1
REL_CLIP = 128
MEM_LEN = 256
MEM_HEADS = 4
MEM_HEAD_DIM = D_MODEL // MEM_HEADS
PEER_HEADS = 8
N_KEYS = 128
N_EXPERTS_2 = N_KEYS * N_KEYS
PEER_TOPK = 16
PEER_KEY_DIM = 128
PEER_QUERY_DIM = 2 * PEER_KEY_DIM
PEER_BLOCK = 128
IN_WIDTH = 2 * LRU_WIDTH + 3 * ATT_WIDTH
NEG_INF = -1e30


def _rmsnorm(x, g):
    xf = x.astype(jnp.float32)
    y = xf * lax.rsqrt(jnp.mean(xf * xf, axis=-1, keepdims=True) + EPS)
    return (y * g.astype(jnp.float32)).astype(x.dtype)

def _rg_lru(xr, conv_w, conv_b, gate_a_w, gate_a_b, gate_x_w, gate_x_b, lru_lambda):
    B, S, _ = xr.shape
    xc = lax.conv_general_dilated(
        xr, conv_w[:, None, :], window_strides=(1,), padding=[(CONV_WIDTH - 1, 0)],
        dimension_numbers=('NWC', 'WIO', 'NWC'), feature_group_count=LRU_WIDTH) + conv_b
    xb = xc.reshape(B, S, LRU_BLOCKS, LRU_BLOCK)
    r = jax.nn.sigmoid((jnp.einsum('bshi,hij->bshj', xb, gate_a_w).reshape(B, S, LRU_WIDTH)
                        + gate_a_b).astype(jnp.float32))
    i = jax.nn.sigmoid((jnp.einsum('bshi,hij->bshj', xb, gate_x_w).reshape(B, S, LRU_WIDTH)
                        + gate_x_b).astype(jnp.float32))
    log_a = -LRU_C * r * jax.nn.softplus(-lru_lambda.astype(jnp.float32))
    a = jnp.exp(log_a)
    mult = jnp.sqrt(jnp.maximum(-jnp.expm1(2.0 * log_a), 0.0))
    b = mult * i * xc.astype(jnp.float32)

    def combine(left, right):
        a1, b1 = left
        a2, b2 = right
        return a1 * a2, a2 * b1 + b2

    _, h = lax.associative_scan(combine, (a, b), axis=1)
    return h.astype(xr.dtype)

def _chunk_attention(q, k, v, rel_bias):
    B, S, _ = q.shape
    nc = S // CHUNK
    band = BAND_CHUNKS * CHUNK

    def split(t):
        return t.reshape(B, nc, CHUNK, ATT_HEADS, ATT_HEAD_DIM)

    q, k, v = split(q), split(k), split(v)
    pad = ((0, 0), (LEFT_CHUNKS, 0), (0, 0), (0, 0), (0, 0))
    kp, vp = jnp.pad(k, pad), jnp.pad(v, pad)
    k_band = jnp.concatenate([kp[:, j:j + nc] for j in range(BAND_CHUNKS)], axis=2)
    v_band = jnp.concatenate([vp[:, j:j + nc] for j in range(BAND_CHUNKS)], axis=2)
    s = jnp.einsum('bnqhd,bnkhd->bnhqk', q, k_band).astype(jnp.float32) * (ATT_HEAD_DIM ** -0.5)
    rel = LEFT_CHUNKS * CHUNK + np.arange(CHUNK)[:, None] - np.arange(band)[None, :]
    rel_idx = np.clip(rel, -REL_CLIP, REL_CLIP) + REL_CLIP
    bias = rel_bias[:, rel_idx].astype(jnp.float32)
    key_chunk = (np.arange(nc)[:, None] - LEFT_CHUNKS
                 + (np.arange(band) // CHUNK)[None, :])
    valid = key_chunk >= 0
    s = jnp.where(valid[None, :, None, None, :], s + bias[None, None], NEG_INF)
    p = jax.nn.softmax(s, axis=-1).astype(v.dtype)
    o = jnp.einsum('bnhqk,bnkhd->bnqhd', p, v_band)
    return o.reshape(B, S, ATT_WIDTH)

def _memory_cross_attention(h, mem_n, w_q, w_kv, w_o):
    B, S, D = h.shape
    M = mem_n.shape[1]
    q = (h @ w_q).reshape(B, S, MEM_HEADS, MEM_HEAD_DIM)
    kv = (mem_n @ w_kv).reshape(B, M, 2, MEM_HEADS, MEM_HEAD_DIM)
    k, v = kv[:, :, 0], kv[:, :, 1]
    s = jnp.einsum('bshd,bmhd->bhsm', q, k).astype(jnp.float32) * (MEM_HEAD_DIM ** -0.5)
    p = jax.nn.softmax(s, axis=-1).astype(h.dtype)
    o = jnp.einsum('bhsm,bmhd->bshd', p, v).reshape(B, S, D)
    return o @ w_o

def _peer(h, w_query, sub_keys, expert_u, expert_v):
    B, S, D = h.shape
    q = (h @ w_query).reshape(B, S, PEER_HEADS, 2, PEER_KEY_DIM)
    sc = jnp.einsum('bshpk,hpnk->bshpn', q, sub_keys).astype(jnp.float32)
    v1, i1 = lax.top_k(sc[..., 0, :], PEER_TOPK)
    v2, i2 = lax.top_k(sc[..., 1, :], PEER_TOPK)
    n_cand = PEER_TOPK * PEER_TOPK
    cand = (v1[..., :, None] + v2[..., None, :]).reshape(B, S, PEER_HEADS, n_cand)
    cand_idx = (i1[..., :, None] * N_KEYS + i2[..., None, :]).reshape(B, S, PEER_HEADS, n_cand)
    top_s, pos = lax.top_k(cand, PEER_TOPK)
    idx = jnp.take_along_axis(cand_idx, pos, axis=-1)
    g = jax.nn.softmax(top_s, axis=-1).astype(h.dtype)
    n_sel = PEER_HEADS * PEER_TOPK
    nb = (B * S) // PEER_BLOCK
    hb = h.reshape(nb, PEER_BLOCK, D)
    ib = idx.reshape(nb, PEER_BLOCK, n_sel)
    gb = g.reshape(nb, PEER_BLOCK, n_sel)

    def block(args):
        xt, it, gt = args
        u = expert_u[it]
        act = jax.nn.gelu(jnp.einsum('td,tkd->tk', xt, u))
        return jnp.einsum('tk,tkd->td', gt * act, expert_v[it])

    out = lax.map(block, (hb, ib, gb))
    return out.reshape(B, S, D)

def second_inputs(seed: int = 0) -> dict:
    key = jax.random.key(seed)
    ks = jax.random.split(key, 32)
    f32 = jnp.float32
    L = DEPTH

    def nrm(k, shape, scale):
        return jax.random.normal(k, shape, f32) * scale

    def gain(k, n):
        return 1.0 + 0.02 * jax.random.normal(k, (L, n), f32)

    a8 = jax.random.uniform(ks[10], (L, LRU_WIDTH), f32, 0.9, 0.999)
    s = a8 ** (1.0 / LRU_C)
    lru_lambda = jnp.log(s) - jnp.log1p(-s)
    return {
        "x": nrm(ks[0], (BATCH, SEQ, D_MODEL), 1.0),
        "mem": nrm(ks[1], (BATCH, MEM_LEN, D_MODEL), 1.0),
        "norm_mix": gain(ks[2], D_MODEL),
        "w_in": nrm(ks[3], (L, D_MODEL, IN_WIDTH), D_MODEL ** -0.5),
        "conv_w": nrm(ks[4], (L, CONV_WIDTH, LRU_WIDTH), CONV_WIDTH ** -0.5),
        "conv_b": nrm(ks[5], (L, LRU_WIDTH), 0.01),
        "gate_a_w": nrm(ks[6], (L, LRU_BLOCKS, LRU_BLOCK, LRU_BLOCK), LRU_BLOCK ** -0.5),
        "gate_a_b": nrm(ks[7], (L, LRU_WIDTH), 0.01),
        "gate_x_w": nrm(ks[8], (L, LRU_BLOCKS, LRU_BLOCK, LRU_BLOCK), LRU_BLOCK ** -0.5),
        "gate_x_b": nrm(ks[9], (L, LRU_WIDTH), 0.01),
        "lru_lambda": lru_lambda,
        "rel_bias": nrm(ks[11], (L, ATT_HEADS, 2 * REL_CLIP + 1), 0.5),
        "norm_grp_a": gain(ks[12], LRU_WIDTH),
        "norm_grp_b": gain(ks[13], ATT_WIDTH),
        "w_out": nrm(ks[14], (L, MIX_WIDTH, D_MODEL), MIX_WIDTH ** -0.5),
        "norm_cross": gain(ks[15], D_MODEL),
        "norm_mem": gain(ks[16], D_MODEL),
        "w_q_mem": nrm(ks[17], (L, D_MODEL, D_MODEL), D_MODEL ** -0.5),
        "w_kv_mem": nrm(ks[18], (L, D_MODEL, 2 * D_MODEL), D_MODEL ** -0.5),
        "w_o_mem": nrm(ks[19], (L, D_MODEL, D_MODEL), D_MODEL ** -0.5),
        "norm_ffn": gain(ks[20], D_MODEL),
        "w_query": nrm(ks[21], (L, D_MODEL, PEER_HEADS * PEER_QUERY_DIM), D_MODEL ** -0.5),
        "sub_keys": nrm(ks[22], (L, PEER_HEADS, 2, N_KEYS, PEER_KEY_DIM), PEER_KEY_DIM ** -0.5),
        "expert_u": nrm(ks[23], (L, N_EXPERTS_2, D_MODEL), D_MODEL ** -0.5),
        "expert_v": nrm(ks[24], (L, N_EXPERTS_2, D_MODEL), PEER_HEADS ** -0.5),
        "norm_final": 1.0 + 0.02 * jax.random.normal(ks[25], (D_MODEL,), f32),
    }

def second_block(x, mem, norm_mix, w_in, conv_w, conv_b, gate_a_w, gate_a_b, gate_x_w, gate_x_b,
              lru_lambda, rel_bias, norm_grp_a, norm_grp_b, w_out, norm_cross, norm_mem,
              w_q_mem, w_kv_mem, w_o_mem, norm_ffn, w_query, sub_keys, expert_u, expert_v,
              norm_final):
    splits = [LRU_WIDTH, 2 * LRU_WIDTH, 2 * LRU_WIDTH + ATT_WIDTH, 2 * LRU_WIDTH + 2 * ATT_WIDTH]
    for l in range(DEPTH):
        hn = _rmsnorm(x, norm_mix[l])
        z = hn @ w_in[l]
        x_lru, gate, q, k, v = jnp.split(z, splits, axis=-1)
        y_a = _rg_lru(x_lru, conv_w[l], conv_b[l], gate_a_w[l], gate_a_b[l],
                      gate_x_w[l], gate_x_b[l], lru_lambda[l]) * jax.nn.gelu(gate)
        y_b = _chunk_attention(q, k, v, rel_bias[l])
        y = jnp.concatenate([_rmsnorm(y_a, norm_grp_a[l]), _rmsnorm(y_b, norm_grp_b[l])], axis=-1)
        x = x + y @ w_out[l]
        x = x + _memory_cross_attention(_rmsnorm(x, norm_cross[l]), _rmsnorm(mem, norm_mem[l]),
                                        w_q_mem[l], w_kv_mem[l], w_o_mem[l])
        x = x + _peer(_rmsnorm(x, norm_ffn[l]), w_query[l], sub_keys[l], expert_u[l], expert_v[l])
    return _rmsnorm(x, norm_final)


def setup_inputs(seed=0):
    out = dict(first_inputs(seed))
    for name, value in second_inputs(seed + 1).items():
        if name != "x":
            out[name + "_2"] = value
    return out


def reference(
    x, norm_mix, w_in, b_forget, q_norm_fox, k_norm_fox, q_norm_dil, k_norm_dil, out_norm_fox,
    out_norm_dil, w_out, norm_ffn, w_router_group, b_router_group, w_router_expert,
    b_router_expert, w_gate, w_up, w_down, mem_2, norm_mix_2, w_in_2, conv_w_2, conv_b_2,
    gate_a_w_2, gate_a_b_2, gate_x_w_2, gate_x_b_2, lru_lambda_2, rel_bias_2, norm_grp_a_2,
    norm_grp_b_2, w_out_2, norm_cross_2, norm_mem_2, w_q_mem_2, w_kv_mem_2, w_o_mem_2,
    norm_ffn_2, w_query_2, sub_keys_2, expert_u_2, expert_v_2, norm_final_2,
):
    x = first_block(
        x, norm_mix, w_in, b_forget, q_norm_fox, k_norm_fox, q_norm_dil, k_norm_dil,
        out_norm_fox, out_norm_dil, w_out, norm_ffn, w_router_group, b_router_group,
        w_router_expert, b_router_expert, w_gate, w_up, w_down,
    )
    return second_block(
        x, mem_2, norm_mix_2, w_in_2, conv_w_2, conv_b_2, gate_a_w_2, gate_a_b_2, gate_x_w_2,
        gate_x_b_2, lru_lambda_2, rel_bias_2, norm_grp_a_2, norm_grp_b_2, w_out_2, norm_cross_2,
        norm_mem_2, w_q_mem_2, w_kv_mem_2, w_o_mem_2, norm_ffn_2, w_query_2, sub_keys_2,
        expert_u_2, expert_v_2, norm_final_2,
    )


_drawn_inputs = setup_inputs


def setup_inputs(seed=0):
    import zlib

    import numpy as np

    out = dict(_drawn_inputs(seed))
    spreads = {}
    factors = {'q_norm_fox': 3.856,
     'k_norm_fox': 2.754,
     'k_norm_dil': 3.004,
     'b_router_group': 8.0,
     'b_router_expert': 4.252,
     'norm_mix_2': 2.795,
     'conv_b_2': 3.351,
     'gate_a_b_2': 8.0,
     'gate_x_b_2': 8.0,
     'norm_grp_a_2': 4.079,
     'norm_grp_b_2': 4.422,
     'norm_cross_2': 8.0,
     'norm_mem_2': 8.0,
     'norm_ffn_2': 23.165,
     'norm_final_2': 7.89}
    for name, (base, spread) in spreads.items():
        noise = np.random.default_rng([zlib.crc32(name.encode()), seed]).standard_normal(out[name].shape)
        drawn = base * np.exp(spread * noise) if base else spread * noise
        out[name] = __import__('jax').numpy.asarray(drawn.astype(out[name].dtype))
    for name, factor in factors.items():
        out[name] = (out[name] * factor).astype(out[name].dtype)
    return out
```

```python
import math

import numpy as np

import concourse.bass as bass
from concourse import mybir

F32 = mybir.dt.float32
U32 = mybir.dt.uint32
I32 = mybir.dt.int32
ALU = mybir.AluOpType
ACT = mybir.ActivationFunctionType
AX = mybir.AxisListType.X

EPS = 1e-6
NEG = -1e30
P = 128
D = 1024
CAP = 64
NSLOT = 5


class Lane:

    def __init__(self, nc, eng, name):
        self.eng, self.name = eng, name
        self.sem = nc.alloc_semaphore(name)
        self.n = 0
        self.seen = {}

    def wait(self, *marks):
        for m in marks:
            if m is None:
                continue
            if isinstance(m, list):
                self.wait(*m)
                continue
            sem, v = m
            if self.seen.get(sem.name, 0) < v:
                self.eng.wait_ge(sem, v)
                self.seen[sem.name] = v

    def mark(self, ins):
        self.n += 1
        ins.then_inc(self.sem, 1)
        return (self.sem, self.n)

    def last(self):
        return (self.sem, self.n)

    def op(self, build, *args, after=(), chain=True, **kw):
        self.wait(*after)
        if chain and self.n:
            self.wait(self.last())
        return self.mark(build(*args, **kw))


class Load:

    def __init__(self, nc, name):
        self.sem, self.n = nc.alloc_semaphore(name), 0

    def start(self, lane, dst, src, after=()):
        lane.wait(*after)
        lane.eng.dma_start(dst, src).then_inc(self.sem, 16)
        self.n += 16
        return (self.sem, self.n)

    def mark(self):
        return (self.sem, self.n)


class Ring:

    def __init__(self, nc, lane, buf, plan):
        self.lane, self.buf, self.plan = lane, buf, plan
        self.sems = [nc.alloc_semaphore(f"s_ring{i}") for i in range(NSLOT)]
        self.issued = self.taken = self.freed = 0
        while self.issued < min(NSLOT, len(plan)):
            self._issue(())

    def _issue(self, after):
        i = self.issued
        n, pat, kw, src = self.plan[i]
        dst = self.buf[:, i % NSLOT, 0:n]
        if pat:
            dst = dst.rearrange(pat, **kw)
        self.lane.wait(*after)
        self.lane.eng.dma_start(dst, src).then_inc(self.sems[i % NSLOT], 16)
        self.issued += 1

    def take(self):
        i = self.taken
        self.taken += 1
        return self.buf[:, i % NSLOT, :], (self.sems[i % NSLOT], 16 * (i // NSLOT + 1))

    def free(self, *marks):
        self.freed += 1
        if self.issued < len(self.plan):
            self._issue(marks)


def program(nc, a, out, dbg=None):
    sb = lambda name, shape, dt=F32: nc.alloc_sbuf_tensor(name, shape, dt)
    V = Lane(nc, nc.vector, "s_dve")
    A = Lane(nc, nc.scalar, "s_act")
    T = Lane(nc, nc.tensor, "s_pe")
    G = Lane(nc, nc.gpsimd, "s_pool")
    S = Lane(nc, nc.sync, "s_sp")
    mm = nc.tensor.matmul

    ring_buf = sb("ring", [P, NSLOT, 4096])
    ACTS = sb("acts", [P, 16384])
    DS = sb("ds", [P, 8192])
    X = sb("x", [P, 2, D])
    HT = sb("ht", [P, 8, 256])
    Y = sb("y", [P, 2, D])
    ident = sb("ident", [P, P])
    iota = sb("iota", [P, P])
    tri = sb("tri", [P, 2, 256])
    small = sb("small", [P, 900])
    PS = nc.alloc_psum_tensor("ps", [P, 8, 512], F32)
    bank_free = [None] * 8
    small_at = [0]

    def sm(n):
        s = small[:, small_at[0]:small_at[0] + n]
        small_at[0] += n
        return s

    K512 = ("p (k n) -> p k n", dict(k=8))

    def cols(w, n0, n=512):
        return (8 * n, *K512, w.rearrange("(p k) n -> p k n", k=8)[:, :, n0:n0 + n])

    def whole(src):
        return (4096, None, None, src)

    plan = [cols(a["w_in"][0], 512 * i) for i in range(6)]
    plan += [cols(a["w_out"][0], 512 * i) for i in range(2)]
    for e in range(0, 32, 2):
        for w, k in (("w_gate", 8), ("w_up", 8), ("w_down", 4)):
            for i in (e, e + 1):
                plan.append(whole(a[w][0, i].rearrange("(p k) n -> p (k n)", k=k)))
    plan += [cols(a["w_in_2"][0], 512 * i) for i in range(4)]
    plan.append((3072, None, None, a["bias_2"]))
    plan.append(cols(a["w_in_2"][0], 2048))
    plan += [cols(a["w_out_2"][0], 512 * i) for i in range(2)]
    plan += [cols(a["w_kv_mem_2"][0], 512 * i) for i in range(4)]
    plan += [cols(a["w_q_mem_2"][0], 512 * i) for i in range(2)]
    plan += [cols(a["w_o_mem_2"][0], 512 * i) for i in range(2)]
    plan += [cols(a["w_query_2"][0], 512 * i) for i in range(4)]
    plan.append((2048, None, None, a["sub_keys_2"]))
    for hf in range(2):
        plan += [whole(a["expert_u_2"][hf * 16 + i]) for i in range(16)]
        plan += [whole(a["expert_v_2"][hf * 16 + i]) for i in range(16)]

    l_x = Load(nc, "l_x")
    for b in range(2):
        l_x.start(A, X[:, b, :], a["x"][0, b * P:(b + 1) * P, :])
    l_c = Load(nc, "l_c")
    l_c.start(A, ident[:, :], a["c_ident"])
    ring = Ring(nc, S, ring_buf, plan)
    l_s = Load(nc, "l_s")
    PROJ = ACTS[:, 0:6144].rearrange("p (b n) -> p b n", b=2)
    QK = ACTS[:, 6144:10240].rearrange("p (j c t) -> p j c t", j=4, c=4)
    PB = ACTS[:, 10240:12288].rearrange("p (h k) -> p h k", h=8)
    PT = ACTS[:, 12288:14336].rearrange("p (b h q) -> p b h q", b=2, h=8)
    MF = ACTS[:, 14336:14848].rearrange("p (b k) -> p b k", b=2)
    MD = ACTS[:, 14848:15360].rearrange("p (b k) -> p b k", b=2)
    ROPE = ACTS[:, 15360:15488].rearrange("p (s b f) -> p s b f", s=2, b=2)
    GDIL = ACTS[:, 15488:15616].rearrange("p (s d) -> p s d", s=2)
    WF = ACTS[:, 15616:15680].rearrange("p (k n) -> p k n", k=8)
    WR = ACTS[:, 15680:15968].rearrange("p (k n) -> p k n", k=8)
    CT = ACTS[0:8, 15968:16224]
    SEL = DS[0:8, 7168:8192].rearrange("p (h q) -> p h q", h=8)

    def vec8(name):
        g = sm(8)
        l_s.start(A, g, a[name].rearrange("a (p k) -> (a p) k", k=8))
        return g

    g_mix = vec8("norm_mix")
    g_out = sm(8)
    l_s.start(A, g_out[0:64, :], a["out_norm_fox"].rearrange("a (p k) -> (a p) k", k=8))
    l_s.start(A, g_out[64:128, :], a["out_norm_dil"].rearrange("a (p k) -> (a p) k", k=8))
    gq, gk = sm(1), sm(1)
    for g, name in ((gq, "q_norm_fox"), (gk, "k_norm_fox")):
        for i in range(2):
            l_s.start(A, g[64 * i:64 * i + 64, :], a[name].rearrange("a (p k) -> (a p) k", k=1))
    bf = sm(8)
    l_s.start(A, bf, a["b_forget"].broadcast_to((P, 8)))
    l_s.start(A, WF, a["w_in"][0].rearrange("(p k) n -> p k n", k=8)[:, :, 3072:3080])
    l_s.start(A, GDIL[:, 0, :], a["q_norm_dil"].broadcast_to((P, 64)))
    l_s.start(A, GDIL[:, 1, :], a["k_norm_dil"].broadcast_to((P, 64)))
    l_s.start(A, ROPE, a["c_rope"])
    l_s.start(A, MF, a["c_fox"])
    l_s.start(A, MD, a["c_dil"])
    l_s.start(A, SEL, a["c_sel"])
    l_s.start(A, tri[:, :, :], a["c_tri"])
    l_s.start(A, iota[:, :], a["c_iota"])
    g_ffn = vec8("norm_ffn")
    l_s.start(A, WR, a["w_router"])
    br = sm(36)
    l_s.start(A, br[:, 0:4], a["b_router_group"].broadcast_to((P, 4)))
    l_s.start(A, br[:, 4:36], a["b_router_expert"].rearrange("a g e -> a (g e)").broadcast_to((P, 32)))
    g_mix2, g_cross, g_mem, g_ffn2 = (vec8(n) for n in ("norm_mix_2", "norm_cross_2", "norm_mem_2", "norm_ffn_2"))
    g_grp = sm(8)
    l_s.start(A, g_grp[0:64, :], a["norm_grp_a_2"].rearrange("a (p k) -> (a p) k", k=8))
    l_s.start(A, g_grp[64:128, :], a["norm_grp_b_2"].rearrange("a (p k) -> (a p) k", k=8))
    cw = sm(16).rearrange("p (c w) -> p c w", c=4)
    l_s.start(A, cw, a["conv_w_2"])
    cb, gab, gxb, lam = (sm(4) for _ in range(4))
    for t, n in ((cb, "conv_b_2"), (gab, "gate_a_b_2"), (gxb, "gate_x_b_2"), (lam, "lru_lambda_2")):
        l_s.start(A, t, a[n])
    consts = [l_c.mark(), l_s.mark()]

    def rstd_of(ss, n, width, scale=None):
        V.op(V.eng.tensor_scalar, ss, ss, 1.0 / width, EPS, ALU.mult, ALU.add, after=(A.last(),))
        A.op(A.eng.activation, ss, ss, ACT.Sqrt, after=(V.last(),))
        m = V.op(V.eng.reciprocal, ss, ss, after=(A.last(),))
        if scale is not None:
            m = V.op(V.eng.tensor_scalar, ss, ss, scale, None, ALU.mult)
        return m

    def transposed(xs, gain, dst, after):
        ready = [None] * 8
        for bank in range(4):
            T.wait(bank_free[bank], *after)
            for k in (2 * bank, 2 * bank + 1):
                for b in range(2):
                    ins = nc.tensor.transpose(
                        PS[:, bank, (k % 2) * 256 + b * P:(k % 2) * 256 + (b + 1) * P],
                        xs[:, b, :].rearrange("p (c k) -> p k c", k=8)[:, k, :], ident[:, :])
            m = T.mark(ins)
            for k in (2 * bank, 2 * bank + 1):
                src = PS[:, bank, (k % 2) * 256:(k % 2) * 256 + 256]
                if bank % 2:
                    ready[k] = A.op(A.eng.activation, dst[:, k, :], src, ACT.Copy,
                                    scale=1.0 if gain is None else gain[:, k:k + 1], after=(m,), chain=False)
                elif gain is None:
                    ready[k] = V.op(V.eng.tensor_copy, dst[:, k, :], src, after=(m,), chain=False)
                else:
                    ready[k] = V.op(V.eng.tensor_scalar, dst[:, k, :], src, gain[:, k:k + 1], None, ALU.mult,
                                    after=(m,), chain=False)
            bank_free[bank] = [ready[2 * bank], ready[2 * bank + 1]]
        return [V.last(), A.last()]

    ss = sm(4)

    def norm(src, xs, after=()):
        for b in range(2):
            A.op(A.eng.activation, xs[:, b, :], src[:, b, :], ACT.Square, accum_out=ss[:, b:b + 1],
                 after=(*after, V.last(), T.last()))
        rstd_of(ss[:, 0:2], 2, D)
        for b in range(2):
            V.op(V.eng.tensor_scalar, xs[:, b, :], src[:, b, :], ss[:, b:b + 1], None, ALU.mult)
        return V.last()

    def tokens_by(w, ht, b, bank, n=512, after=(), k_of=8):
        T.wait(bank_free[bank], *after)
        for k in range(k_of):
            ins = mm(PS[:, bank, 0:n], ht[:, k, b * P:(b + 1) * P], w[:, k, 0:n],
                     start=(k == 0), stop=(k == k_of - 1))
        return T.mark(ins)

    def features_by(w, ht, c, bank, half, after=()):
        T.wait(bank_free[bank], *after)
        o = PS[:, bank, half * 256:half * 256 + 256]
        for k in range(8):
            ins = mm(o, w[:, k, c * P:(c + 1) * P], ht[:, k, :], start=(k == 0), stop=(k == 7))
        return T.mark(ins)

    def w8(tile, n=512):
        return tile[:, 0:8 * n].rearrange("p (k n) -> p k n", k=8)

    T.wait(*consts)
    V.wait(*consts)
    A.wait(*consts)
    m = norm(X, Y, after=(l_x.mark(),))
    ht_ready = transposed(Y, g_mix, HT, (m,))

    def project(n_tiles, dst, ready, bank0=4):
        turn = 0
        for i in range(n_tiles):
            tile, landed = ring.take()
            for b in range(2):
                bank = bank0 + turn % 4
                m = tokens_by(w8(tile), HT, b, bank, after=(landed, *ready))
                lane = A if turn % 2 else V
                if turn % 2:
                    d = A.op(A.eng.activation, dst(i, b), PS[:, bank, :], ACT.Copy, after=(m,), chain=False)
                else:
                    d = V.op(V.eng.tensor_copy, dst(i, b), PS[:, bank, :], after=(m,), chain=False)
                bank_free[bank] = d
                turn += 1
            ring.free(m)
        return [V.last(), A.last()]

    logf, cum = sm(16), sm(16)
    for b in range(2):
        m = tokens_by(WF, HT, b, 4 + b, n=8, after=ht_ready)
        bank_free[4 + b] = V.op(V.eng.tensor_tensor, logf[:, 8 * b:8 * b + 8], PS[:, 4 + b, 0:8], bf, ALU.add, after=(m,))
    t0, t1, t2, t3 = (sm(16) for _ in range(4))

    def log1p_exp_neg_abs(x, n, e, s, s2, q):
        V.op(V.eng.tensor_scalar, e[:, 0:n], x, -1.0, None, ALU.mult)
        V.op(V.eng.tensor_tensor, e[:, 0:n], e[:, 0:n], x, ALU.min)
        A.op(A.eng.activation, e[:, 0:n], e[:, 0:n], ACT.Exp, after=(V.last(),))
        V.op(V.eng.tensor_scalar, s[:, 0:n], e[:, 0:n], 2.0, None, ALU.add, after=(A.last(),))
        V.op(V.eng.reciprocal, s[:, 0:n], s[:, 0:n])
        V.op(V.eng.tensor_tensor, s[:, 0:n], s[:, 0:n], e[:, 0:n], ALU.mult)
        V.op(V.eng.tensor_tensor, s2[:, 0:n], s[:, 0:n], s[:, 0:n], ALU.mult)
        V.op(V.eng.tensor_scalar, q[:, 0:n], s2[:, 0:n], 1.0 / 17, 1.0 / 15, ALU.mult, ALU.add)
        for c in (13, 11, 9, 7, 5, 3, 1):
            V.op(V.eng.tensor_tensor, q[:, 0:n], q[:, 0:n], s2[:, 0:n], ALU.mult)
            V.op(V.eng.tensor_scalar, q[:, 0:n], q[:, 0:n], 1.0 / c, None, ALU.add)
        V.op(V.eng.tensor_tensor, e[:, 0:n], q[:, 0:n], s[:, 0:n], ALU.mult)
        return V.op(V.eng.tensor_scalar, e[:, 0:n], e[:, 0:n], 2.0, None, ALU.mult)

    log1p_exp_neg_abs(logf, 16, t0, t1, t2, t3)
    V.op(V.eng.tensor_scalar, logf, logf, 0.0, None, ALU.min)
    m = V.op(V.eng.tensor_tensor, logf, logf, t0, ALU.subtract)
    T.wait(m, bank_free[6], bank_free[7])
    mm(PS[:, 6, 0:8], tri[:, 0, 0:P], logf[:, 0:8], start=True, stop=True)
    mm(PS[:, 6, 8:16], tri[:, 0, P:256], logf[:, 0:8], start=True, stop=False)
    mm(PS[:, 6, 8:16], tri[:, 1, P:256], logf[:, 8:16], start=False, stop=True)
    for b in range(2):
        ins = mm(PS[0:8, 7, 0:256], logf[:, 8 * b:8 * b + 8], tri[:, b, :], start=(b == 0), stop=(b == 1))
    m = T.mark(ins)
    V.op(V.eng.tensor_copy, cum, PS[:, 6, 0:16], after=(m,))
    ct_ready = V.op(V.eng.tensor_scalar, CT, PS[0:8, 7, 0:256], -1.0, None, ALU.mult)
    bank_free[6] = bank_free[7] = V.last()

    proj_ready = project(6, lambda i, b: PROJ[:, b, 512 * i:512 * i + 512], ht_ready)

    nrm = sm(64).rearrange("p (b j n) -> p b j n", b=2, j=2)
    SQ = DS[:, 0:4096].rearrange("p (b j n d) -> p b j n d", b=2, j=2, d=64)
    V.wait(*proj_ready)
    A.wait(*proj_ready)
    for b in range(2):
        for j in range(2):
            qk = PROJ[:, b, 1536 * j:1536 * j + 1024].rearrange("p (n d) -> p n d", d=64)
            m = A.op(A.eng.activation, SQ[:, b, j], qk, ACT.Square, chain=False)
            V.op(V.eng.tensor_reduce, nrm[:, b, j, :], SQ[:, b, j], AX, ALU.add, after=(m,), chain=False)
    rstd_of(nrm.rearrange("p b j n -> p (b j n)"), 64, 64)
    for b in range(2):
        V.op(V.eng.tensor_scalar, nrm[:, b, :, 0:8], nrm[:, b, :, 0:8], 0.125, None, ALU.mult)
    for b in range(2):
        for j in range(2):
            qk = PROJ[:, b, 1536 * j:1536 * j + 1024].rearrange("p (n d) -> p n d", d=64)
            m = V.op(V.eng.tensor_tensor, qk, qk, nrm[:, b, j, :].rearrange("p (n o) -> p n o", o=1).broadcast_to((P, 16, 64)), ALU.mult)
            if j == 0:
                qk_fox = m
                continue
            q4 = qk.rearrange("p (s n) d -> p s n d", s=2)
            for s in range(2):
                V.op(V.eng.tensor_tensor, q4[:, s], q4[:, s],
                     GDIL[:, s:s + 1, :].broadcast_to((P, 8, 64)), ALU.mult)
            cos = ROPE[:, 0, b:b + 1, :].broadcast_to((P, 16, 32))
            sin = ROPE[:, 1, b:b + 1, :].broadcast_to((P, 16, 32))
            x1, x2 = qk[:, :, 0:32], qk[:, :, 32:64]
            tmp = [DS[:, 4096 + 512 * i:4608 + 512 * i].rearrange("p (n d) -> p n d", d=32) for i in range(4)]
            g0 = G.op(G.eng.tensor_tensor, tmp[0], x1, sin, ALU.mult, after=(V.last(),))
            g1 = G.op(G.eng.tensor_tensor, tmp[1], x2, sin, ALU.mult)
            V.op(V.eng.tensor_tensor, tmp[2], x1, cos, ALU.mult)
            V.op(V.eng.tensor_tensor, tmp[3], x2, cos, ALU.mult)
            V.op(V.eng.tensor_tensor, x1, tmp[2], tmp[1], ALU.subtract, after=(g1,))
            V.op(V.eng.tensor_tensor, x2, tmp[3], tmp[0], ALU.add)
    qk_dil = V.last()
    turn = 0
    qk_ready = []
    for j in range(4):
        off = (0, 512, 1536, 2048)[j]
        for half in range(2):
            bank = turn % 4
            T.wait(bank_free[bank], qk_fox if j < 2 else qk_dil)
            for c in (2 * half, 2 * half + 1):
                for b in range(2):
                    ins = nc.tensor.transpose(PS[:, bank, (c % 2) * 256 + b * P:(c % 2) * 256 + (b + 1) * P],
                                              PROJ[:, b, off + c * P:off + (c + 1) * P], ident[:, :])
            m = T.mark(ins)
            dst = QK[:, j, 2 * half:2 * half + 2, :].rearrange("p c t -> p (c t)")
            scale = (gq, gk, None, None)[j]
            if half:
                d = A.op(A.eng.activation, dst, PS[:, bank, :], ACT.Copy,
                         scale=1.0 if scale is None else scale, after=(m,), chain=False)
            elif scale is None:
                d = V.op(V.eng.tensor_copy, dst, PS[:, bank, :], after=(m,), chain=False)
            else:
                d = V.op(V.eng.tensor_scalar, dst, PS[:, bank, :], scale, None, ALU.mult, after=(m,), chain=False)
            bank_free[bank] = d
            qk_ready.append(d)
            turn += 1

    mx, nm, lsum, rl = (sm(8) for _ in range(4))

    def head_slot(h):
        return (h % 2) * 4 + h // 2

    S8 = PS[:, 0:4, :].rearrange("p a (c k) -> p (a c) k", k=256)

    def score_mms(qt, kt, b, K, after):
        T.wait(*[bank_free[i] for i in range(4)], *after)
        for h in range(8):
            o = 64 * (h % 2)
            ins = mm(S8[:, head_slot(h), 0:K], qt[o:o + 64, h // 2, b * P:(b + 1) * P],
                     kt[o:o + 64, h // 2, 0:K], start=True, stop=True)
        return T.mark(ins)

    def head_of(s):
        return 2 * (s % 4) + s // 4

    oss = sm(4).rearrange("p (j b) -> p j b", j=2)
    for j in range(2):
        for b in range(2):
            K = P * (b + 1)
            m = score_mms(QK[:, 2 * j], QK[:, 2 * j + 1], b, K, qk_ready)
            pb = PB[:, :, 0:K]
            if j == 0:
                T.wait(ct_ready, *[bank_free[i] for i in range(4, 8)])
                C8 = PS[:, 4:8, :].rearrange("p a (c k) -> p (a c) k", k=256)
                for s in range(8):
                    ins = mm(C8[:, s, 0:K], SEL[:, head_of(s), :], CT[:, 0:K], start=True, stop=True)
                mc = T.mark(ins)
                d = V.op(V.eng.tensor_tensor, pb, C8[:, :, 0:K], MF[:, b:b + 1, 0:K].broadcast_to((P, 8, K)), ALU.add,
                         after=(mc, T.last()))
                for i in range(4, 8):
                    bank_free[i] = d
                for s in range(8):
                    h = head_of(s)
                    m = V.op(V.eng.scalar_tensor_tensor, pb[:, s, :], S8[:, s, 0:K], cum[:, 8 * b + h:8 * b + h + 1],
                             pb[:, s, :], ALU.add, ALU.add, after=(m, d), chain=False)
            else:
                m = V.op(V.eng.tensor_tensor, pb, S8[:, :, 0:K], MD[:, b:b + 1, 0:K].broadcast_to((P, 8, K)), ALU.add,
                         after=(m, T.last()))
            for i in range(4):
                bank_free[i] = m
            dst = Y[:, b, 512 * j:512 * j + 512].rearrange("p (h i d) -> p i h d", h=4, i=2)
            voff = 1024 + 1536 * j
            V.op(V.eng.tensor_reduce, mx, pb, AX, ALU.max)
            V.op(V.eng.tensor_scalar, nm, mx, -1.0, None, ALU.mult)
            e = []
            for s in range(8):
                e.append(A.op(A.eng.activation, pb[:, s, :], pb[:, s, :], ACT.Exp, bias=nm[:, s:s + 1],
                              accum_out=lsum[:, s:s + 1], after=(V.last(),), chain=False))
            rec = V.op(V.eng.reciprocal, rl, lsum, after=(e[-1],))
            for kb in range(b + 1):
                for g in range(2):
                    bank = 4 + (kb * 2 + g) % 3
                    T.wait(bank_free[bank], e[4 * g + 3])
                    for i in range(4):
                        ins = nc.tensor.transpose(PS[:, bank, i * P:(i + 1) * P],
                                                  pb[:, 4 * g + i, kb * P:(kb + 1) * P], ident[:, :])
                    m = T.mark(ins)
                    d = PT[:, kb, 4 * g:4 * g + 4, :].rearrange("p h q -> p (h q)")
                    if g:
                        m = A.op(A.eng.activation, d, PS[:, bank, :], ACT.Copy, after=(m,), chain=False)
                    else:
                        m = V.op(V.eng.tensor_copy, d, PS[:, bank, :], after=(m,), chain=False)
                    bank_free[bank] = m
            T.wait(V.last(), A.last(), bank_free[7])
            for s in range(8):
                h = head_of(s)
                for kb in range(b + 1):
                    ins = mm(PS[:, 7, s * 64:(s + 1) * 64], PT[:, kb, s, :],
                             PROJ[:, kb, voff + 64 * h:voff + 64 * h + 64], start=(kb == 0), stop=(kb == b))
            m = T.mark(ins)
            for i in range(2):
                m2 = V.op(V.eng.tensor_tensor, dst[:, i], PS[:, 7, 256 * i:256 * i + 256].rearrange("p (h d) -> p h d", h=4),
                          rl[:, 4 * i:4 * i + 4].rearrange("p (n o) -> p n o", o=1).broadcast_to((P, 4, 64)),
                          ALU.mult, after=(m, rec))
            bank_free[7] = m2
            A.op(A.eng.activation, DS[:, 0:512], Y[:, b, 512 * j:512 * j + 512], ACT.Square,
                 accum_out=oss[:, j, b:b + 1], after=(m2,))

    def group_norm_out(oss, gain, dst_bank_add):
        rstd_of(oss.rearrange("p j b -> p (j b)"), 4, 512)
        for b in range(2):
            for j in range(2):
                V.op(V.eng.tensor_scalar, Y[:, b, 512 * j:512 * j + 512], Y[:, b, 512 * j:512 * j + 512],
                     oss[:, j, b:b + 1], None, ALU.mult)
        ready = transposed(Y, gain, HT, (V.last(),))
        return add_product(ready)

    def add_product(ready):
        for i in range(2):
            tile, landed = ring.take()
            for b in range(2):
                bank = 4 + 2 * i + b
                m = tokens_by(w8(tile), HT, b, bank, after=(landed, *ready))
                xb = X[:, b, 512 * i:512 * i + 512]
                bank_free[bank] = V.op(V.eng.tensor_tensor, xb, xb, PS[:, bank, :], ALU.add, after=(m,), chain=False)
            ring.free(m)
        return V.last()

    group_norm_out(oss, g_out, None)
    if dbg == "h":
        return finish_debug(nc, S, X, V, out)

    m = norm(X, Y)
    ht_ready = transposed(Y, g_ffn, HT, (m,))
    Z = sm(72).rearrange("p (b n) -> p b n", b=2)
    for b in range(2):
        m = tokens_by(WR, HT, b, 4 + b, n=36, after=ht_ready)
        bank_free[4 + b] = V.op(V.eng.tensor_tensor, Z[:, b, :], PS[:, 4 + b, 0:36], br, ALU.add, after=(m,))
    gmx, gsum, ge, goh, gidx = sm(2), sm(2), sm(8), sm(8), sm(2)
    b2 = lambda x: x.rearrange("p (b n) -> p b n", b=2)
    ge, goh = b2(ge), b2(goh)
    col = lambda x, n: x.rearrange("p (b o) -> p b o", o=1).broadcast_to((P, 2, n))
    V.op(V.eng.tensor_reduce, gmx, Z[:, :, 0:4], AX, ALU.max)
    V.op(V.eng.tensor_tensor, ge, Z[:, :, 0:4], col(gmx, 4), ALU.subtract)
    m = A.op(A.eng.activation, ge, ge, ACT.Exp, after=(V.last(),))
    V.op(V.eng.tensor_tensor, goh, Z[:, :, 0:4], col(gmx, 4), ALU.is_equal)
    iota4 = iota[:, 0:4].rearrange("p (o n) -> p o n", o=1).broadcast_to((P, 2, 4))
    V.op(V.eng.scalar_tensor_tensor, goh, goh, -1000.0, iota4, ALU.mult, ALU.add)
    V.op(V.eng.tensor_reduce, gidx, goh, AX, ALU.min)
    V.op(V.eng.tensor_scalar, gidx, gidx, 1000.0, None, ALU.add)
    V.op(V.eng.tensor_tensor, goh, iota4, col(gidx, 4), ALU.is_equal)
    V.op(V.eng.tensor_reduce, gsum, ge, AX, ALU.add, after=(m,))
    V.op(V.eng.reciprocal, gsum, gsum)
    zsel, prod, top8 = b2(sm(16)), DS[:, 4096:4160].rearrange("p (b e g) -> p b e g", b=2, e=8), b2(sm(16))
    for b in range(2):
        V.op(V.eng.tensor_tensor, prod[:, b], Z[:, b, 4:36].rearrange("p (g e) -> p e g", g=4),
             goh[:, b:b + 1, :].broadcast_to((P, 8, 4)), ALU.mult)
    V.op(V.eng.tensor_reduce, zsel.rearrange("p b e -> p (b e)"), prod.rearrange("p b e g -> p (b e) g"), AX, ALU.add)
    ti = nc.alloc_sbuf_tensor("ti", [P, 16], U32)
    tf = b2(sm(16))
    for b in range(2):
        V.op(V.eng.max, top8[:, b, :], zsel[:, b, :])
        V.op(V.eng.max_index, ti[:, 8 * b:8 * b + 8], top8[:, b, :], zsel[:, b, :])
    V.op(V.eng.tensor_copy, tf.rearrange("p b e -> p (b e)"), ti[:, :])
    w1, w2, wt = sm(2), sm(2), sm(2)
    V.op(V.eng.tensor_tensor, w2, top8[:, :, 1], top8[:, :, 0], ALU.subtract)
    A.op(A.eng.activation, w2, w2, ACT.Exp, after=(V.last(),))
    V.op(V.eng.tensor_scalar, wt, w2, 1.0, None, ALU.add, after=(A.last(),))
    V.op(V.eng.reciprocal, wt, wt)
    V.op(V.eng.tensor_tensor, w1, wt, gsum, ALU.mult)
    V.op(V.eng.tensor_tensor, w2, w2, w1, ALU.mult)
    e1, e2 = b2(sm(16)), b2(sm(16))
    iota8 = iota[:, 0:8].rearrange("p (o n) -> p o n", o=1).broadcast_to((P, 2, 8))
    V.op(V.eng.tensor_tensor, e1, iota8, tf[:, :, 0:1].broadcast_to((P, 2, 8)), ALU.is_equal)
    V.op(V.eng.tensor_tensor, e2, iota8, tf[:, :, 1:2].broadcast_to((P, 2, 8)), ALU.is_equal)
    MK, CB, RM = b2(sm(64)), b2(sm(64)), b2(sm(64))
    ee, ew = b2(sm(16)), b2(sm(16))
    V.op(V.eng.tensor_tensor, ee, e1, e2, ALU.add)
    V.op(V.eng.tensor_tensor, e1, e1, col(w1, 8), ALU.mult)
    V.op(V.eng.tensor_tensor, e2, e2, col(w2, 8), ALU.mult)
    V.op(V.eng.tensor_tensor, ew, e1, e2, ALU.add)
    for b in range(2):
        g4 = goh[:, b, :].rearrange("p (g o) -> p g o", o=1).broadcast_to((P, 4, 8))
        for dst, src in ((MK, ee), (CB, ew)):
            V.op(V.eng.tensor_tensor, dst[:, b, :].rearrange("p (g e) -> p g e", g=4), g4,
                 src[:, b:b + 1, :].broadcast_to((P, 4, 8)), ALU.mult)
    T.wait(V.last(), bank_free[6])
    mm(PS[:, 6, 0:32], tri[:, 0, 0:P], MK[:, 0, :], start=True, stop=True)
    mm(PS[:, 6, 32:64], tri[:, 0, P:256], MK[:, 0, :], start=True, stop=False)
    m = T.mark(mm(PS[:, 6, 32:64], tri[:, 1, P:256], MK[:, 1, :], start=False, stop=True))
    V.op(V.eng.tensor_tensor, RM.rearrange("p b e -> p (b e)"), MK.rearrange("p b e -> p (b e)"), PS[:, 6, 0:64],
         ALU.mult, after=(m,))
    bank_free[6] = V.last()
    OV, ovn = b2(sm(64)), sm(1)
    V.op(V.eng.tensor_scalar, OV.rearrange("p b e -> p (b e)"), RM.rearrange("p b e -> p (b e)"), float(CAP) + 0.5, None, ALU.is_gt)
    V.op(V.eng.tensor_reduce, ovn, OV.rearrange("p b e -> p (b e)"), AX, ALU.add)
    V.op(V.eng.tensor_tensor, OV.rearrange("p b e -> p (b e)"), OV.rearrange("p b e -> p (b e)"),
         CB.rearrange("p b e -> p (b e)"), ALU.mult)
    T.wait(V.last(), bank_free[7])
    m = T.mark(mm(PS[0:1, 7, 0:1], ovn, tri[:, 0, 127:128], start=True, stop=True))
    flag = nc.alloc_sbuf_tensor("flag", [1, 1], I32)
    flag_ready = V.op(V.eng.tensor_copy, flag[:, :], PS[0:1, 7, 0:1], after=(m,))
    bank_free[7] = flag_ready

    SD = DS[:, 0:4096].rearrange("p (b e s) -> p b e s", b=2, e=32)
    SCT = DS[:, 4096:8192].rearrange("p (g t) -> p g t", g=16)
    XG = ACTS[:, :].rearrange("p (g k s) -> p g k s", g=16, k=8)
    iota_s = iota[:, 1:1 + CAP].rearrange("p (o s) -> p o s", o=1).broadcast_to((P, 32, CAP))
    for b in range(2):
        m = V.op(V.eng.tensor_tensor, SD[:, b], iota_s, RM[:, b, :].rearrange("p (e o) -> p e o", o=1).broadcast_to((P, 32, CAP)),
                 ALU.is_equal)
    turn = 0
    for k in range(8):
        for q in range(4):
            bank = 4 + turn % 4
            T.wait(bank_free[bank], m)
            for b in range(2):
                ins = mm(PS[:, bank, :], Y[:, b, :].rearrange("p (c k) -> p k c", k=8)[:, k, :],
                         SD[:, b, 8 * q:8 * q + 8, :].rearrange("p e s -> p (e s)"), start=(b == 0), stop=(b == 1))
            mt = T.mark(ins)
            src = PS[:, bank, :].rearrange("p (g s) -> p g s", g=4)
            dst = XG[:, 4 * q:4 * q + 4, k, :]
            if turn % 2:
                d = A.op(A.eng.activation, dst, src, ACT.Copy, scale=g_ffn[:, k:k + 1], after=(mt,), chain=False)
            else:
                d = V.op(V.eng.tensor_scalar, dst, src, g_ffn[:, k:k + 1], None, ALU.mult, after=(mt,), chain=False)
            bank_free[bank] = d
            turn += 1
    xg_ready = [V.last(), A.last()]
    for b in range(2):
        V.op(V.eng.tensor_tensor, SD[:, b], SD[:, b], CB[:, b, :].rearrange("p (e o) -> p e o", o=1).broadcast_to((P, 32, CAP)),
             ALU.mult, after=(T.last(),))
    for q in range(8):
        bank = 4 + q % 4
        T.wait(bank_free[bank], V.last())
        for g in (2 * q, 2 * q + 1):
            for b in range(2):
                ins = nc.tensor.transpose(PS[:, bank, (g % 2) * 256 + b * P:(g % 2) * 256 + (b + 1) * P],
                                          SD[:, b, 2 * g:2 * g + 2, :].rearrange("p e s -> p (e s)"), ident[:, :])
        mt = T.mark(ins)
        dst = SCT[:, 2 * q:2 * q + 2, :].rearrange("p g t -> p (g t)")
        if q % 2:
            d = A.op(A.eng.activation, dst, PS[:, bank, :], ACT.Copy, after=(mt,), chain=False)
        else:
            d = V.op(V.eng.tensor_copy, dst, PS[:, bank, :], after=(mt,), chain=False)
        bank_free[bank] = d
    sct_ready = [V.last(), A.last()]

    HB = DS[:, 0:512]
    HTB = DS[:, 512:1024].rearrange("p (c s) -> p c s", c=4)
    YG = DS[:, 1024:2048]
    T.wait(*xg_ready, *sct_ready)
    A.wait(T.last())
    y_last = yg_ready = None

    def scatter(g, ready):
        T.wait(ready, *[bank_free[i] for i in range(4)])
        for b in range(2):
            for half in range(2):
                ins = mm(PS[:, 2 * b + half, :], SCT[:, g, b * P:(b + 1) * P], YG[:, 512 * half:512 * half + 512],
                         start=(g == 0), stop=(g == 15), skip_group_check=True)
        return T.mark(ins)

    for g in range(16):
        for bank in (4, 5):
            t0_, l0 = ring.take()
            t1_, l1 = ring.take()
            T.wait(l0, l1, bank_free[bank])
            for k in range(8):
                for i, t in enumerate((t0_, t1_)):
                    ins = mm(PS[64 * i:64 * i + 64, bank, :], XG[:, g, k, 64 * i:64 * i + 64], w8(t)[:, k, :],
                             start=(k == 0), stop=(k == 7), skip_group_check=True)
            m = T.mark(ins)
            ring.free(m)
            ring.free(m)
            if bank == 4:
                m4 = m
        mh = A.op(A.eng.activation, HB, PS[:, 4, :], ACT.Silu, after=(m4, T.last() if g == 0 else None, y_last))
        mh = V.op(V.eng.tensor_tensor, HB, HB, PS[:, 5, :], ALU.mult, after=(mh, m))
        bank_free[5] = mh
        if g:
            y_last = scatter(g - 1, yg_ready)
        T.wait(mh)
        for c in range(4):
            ins = nc.tensor.transpose(PS[:, 4, c * P:(c + 1) * P],
                                      HB.rearrange("p (f c) -> p c f", c=4)[:, c, :], ident[:, :])
        m = T.mark(ins)
        m = V.op(V.eng.tensor_copy, HTB.rearrange("p c s -> p (c s)"), PS[:, 4, :], after=(m,))
        bank_free[4] = m
        t0_, l0 = ring.take()
        t1_, l1 = ring.take()
        T.wait(l0, l1, m)
        yg_ready = []
        for half in range(2):
            T.wait(bank_free[6 + half])
            for c in range(4):
                for i, t in enumerate((t0_, t1_)):
                    ins = mm(PS[64 * i:64 * i + 64, 6 + half, :], HTB[:, c, 64 * i:64 * i + 64],
                             t.rearrange("p (c n) -> p c n", c=4)[:, c, 512 * half:512 * half + 512],
                             start=(c == 0), stop=(c == 3), skip_group_check=True)
            md = T.mark(ins)
            dst = YG[:, 512 * half:512 * half + 512]
            if half:
                d = A.op(A.eng.activation, dst, PS[:, 7, :], ACT.Copy, after=(md, y_last))
            else:
                d = V.op(V.eng.tensor_copy, dst, PS[:, 6, :], after=(md, y_last))
            bank_free[6 + half] = d
            yg_ready.append(d)
        ring.free(md)
        ring.free(md)
    m = scatter(15, yg_ready)
    for b in range(2):
        for half in range(2):
            xb = X[:, b, 512 * half:512 * half + 512]
            bank_free[2 * b + half] = V.op(V.eng.tensor_tensor, xb, xb, PS[:, 2 * b + half, :], ALU.add, after=(m,),
                                           chain=False)

    for lane in (G, S):
        lane.wait(flag_ready)
    overflow(nc, a, (V, A, T), flag, flag_ready, X, HT, OV, ACTS, PS)
    joined = V.op(V.eng.tensor_scalar, ss[:, 0:2], ss[:, 0:2], 1.0, None, ALU.mult)
    for lane in (A, T, G, S):
        lane.wait(joined)
    for i in range(8):
        bank_free[i] = None
    if dbg == "h2":
        return finish_debug(nc, S, X, V, out)

    R = lambda i: ACTS[:, 1024 * i:1024 * i + 1024].rearrange("p (c t) -> p c t", c=4)
    XR, XC, GT, RR, II, AA, BB, HH, QT, KT = (R(i) for i in range(10))
    VT = ACTS[:, 10240:11264].rearrange("p (b n) -> p b n", b=2)
    PB2 = ACTS[:, 11264:13312].rearrange("p (h k) -> p h k", h=8)
    PT2 = ACTS[:, 13312:15360].rearrange("p (b h q) -> p b h q", b=2, h=8)
    GW = ACTS[:, 15360:15872].rearrange("p (s c j) -> p s c j", s=2, c=4)
    l_g = Load(nc, "l_g")
    l_g.start(A, GW[:, 0], a["gate_a_w_2"])
    l_g.start(A, GW[:, 1], a["gate_x_w_2"])
    m = norm(X, Y)
    ht_ready = transposed(Y, g_mix2, HT, (m,))
    fm_ready = []
    turn = 0
    for i, dst in enumerate((XR, GT, QT, KT)):
        tile, landed = ring.take()
        for c2 in range(2):
            bank = 4 + turn % 4
            turn += 1
            features_by(w8(tile), HT, 2 * c2, bank, 0, after=(landed, *ht_ready))
            m = features_by(w8(tile), HT, 2 * c2 + 1, bank, 1)
            d = dst[:, 2 * c2:2 * c2 + 2, :].rearrange("p c t -> p (c t)")
            if i == 1:
                e = A.op(A.eng.activation, d, PS[:, bank, :], ACT.Gelu_apprx_tanh, after=(m,), chain=False)
            elif i == 2:
                e = V.op(V.eng.tensor_scalar, d, PS[:, bank, :], 0.125, None, ALU.mult, after=(m,), chain=False)
            else:
                e = V.op(V.eng.tensor_copy, d, PS[:, bank, :], after=(m,), chain=False)
            bank_free[bank] = e
        ring.free(m)
    fm_ready = [V.last(), A.last()]
    btile, bias_landed = ring.take()
    vtile, landed = ring.take()
    for b in range(2):
        m = tokens_by(w8(vtile), HT, b, 4 + b, after=(landed,))
        bank_free[4 + b] = A.op(A.eng.activation, VT[:, b, :], PS[:, 4 + b, :], ACT.Copy, after=(m,), chain=False)
    v_ready = A.last()
    v_done = m

    oss2 = sm(4).rearrange("p (j b) -> p j b", j=2)
    for b in range(2):
        K = P * (b + 1)
        m = score_mms(QT, KT, b, K, fm_ready)
        pb = PB2[:, :, 0:K]
        bias = btile[:, 1024 * b:1024 * b + 8 * K].rearrange("p (s k) -> p s k", s=8)
        m = V.op(V.eng.tensor_tensor, pb, S8[:, :, 0:K], bias, ALU.add, after=(m, bias_landed))
        for i in range(4):
            bank_free[i] = m
        V.op(V.eng.tensor_reduce, mx, pb, AX, ALU.max)
        V.op(V.eng.tensor_scalar, nm, mx, -1.0, None, ALU.mult)
        e = []
        for s in range(8):
            e.append(A.op(A.eng.activation, pb[:, s, :], pb[:, s, :], ACT.Exp, bias=nm[:, s:s + 1],
                          accum_out=lsum[:, s:s + 1], after=(V.last(),), chain=False))
        rec = V.op(V.eng.reciprocal, rl, lsum, after=(e[-1],))
        for kb in range(b + 1):
            for g in range(2):
                bank = 4 + (kb * 2 + g) % 3
                T.wait(bank_free[bank], e[4 * g + 3])
                for i in range(4):
                    ins = nc.tensor.transpose(PS[:, bank, i * P:(i + 1) * P],
                                              pb[:, 4 * g + i, kb * P:(kb + 1) * P], ident[:, :])
                m = T.mark(ins)
                d = PT2[:, kb, 4 * g:4 * g + 4, :].rearrange("p h q -> p (h q)")
                if g:
                    m = A.op(A.eng.activation, d, PS[:, bank, :], ACT.Copy, after=(m,), chain=False)
                else:
                    m = V.op(V.eng.tensor_copy, d, PS[:, bank, :], after=(m,), chain=False)
                bank_free[bank] = m
        T.wait(V.last(), A.last(), v_ready, bank_free[7])
        for s in range(8):
            h = head_of(s)
            for kb in range(b + 1):
                ins = mm(PS[:, 7, s * 64:(s + 1) * 64], PT2[:, kb, s, :],
                         VT[:, kb, 64 * h:64 * h + 64], start=(kb == 0), stop=(kb == b))
        m = T.mark(ins)
        dst = Y[:, b, 512:1024].rearrange("p (h i d) -> p i h d", h=4, i=2)
        for i in range(2):
            m2 = V.op(V.eng.tensor_tensor, dst[:, i], PS[:, 7, 256 * i:256 * i + 256].rearrange("p (h d) -> p h d", h=4),
                      rl[:, 4 * i:4 * i + 4].rearrange("p (n o) -> p n o", o=1).broadcast_to((P, 4, 64)),
                      ALU.mult, after=(m, rec))
        bank_free[7] = m2
        A.op(A.eng.activation, DS[:, 0:512], Y[:, b, 512:1024], ACT.Square, accum_out=oss2[:, 1, b:b + 1], after=(m2,))
    ring.free(V.last())
    ring.free(v_done)

    sp, u0, u1, u2 = (sm(4) for _ in range(4))
    log1p_exp_neg_abs(lam, 4, sp, u0, u1, u2)
    V.op(V.eng.tensor_scalar, u0, lam, -1.0, 0.0, ALU.mult, ALU.max)
    V.op(V.eng.tensor_tensor, sp, sp, u0, ALU.add)
    V.op(V.eng.tensor_scalar, sp, sp, 4.0, None, ALU.mult)
    for c in range(4):
        V.op(V.eng.tensor_scalar, XC[:, c, :], XR[:, c, :], cw[:, c, 3:4], cb[:, c:c + 1], ALU.mult, ALU.add)
        for w in (2, 1, 0):
            s = 3 - w
            V.op(V.eng.scalar_tensor_tensor, XC[:, c, s:256], XR[:, c, 0:256 - s], cw[:, c, w:w + 1], XC[:, c, s:256],
                 ALU.mult, ALU.add)
    m = V.last()
    for s, (dst, bias) in enumerate(((RR, gab), (II, gxb))):
        for c in range(4):
            bank = 4 * s + c
            T.wait(m, bank_free[bank], l_g.mark())
            for o in (0, 64):
                ins = mm(PS[o:o + 64, bank, 0:256], GW[o:o + 64, s, c, :],
                         XC[o:o + 64, c, :], start=True, stop=True, skip_group_check=True)
            mt = T.mark(ins)
            d = A.op(A.eng.activation, dst[:, c, :], PS[:, bank, 0:256], ACT.Sigmoid,
                     bias=bias[:, c:c + 1], after=(mt,), chain=False)
            bank_free[bank] = d
    for c in range(4):
        A.op(A.eng.activation, RR[:, c, :], RR[:, c, :], ACT.Tanh, scale=sp[:, c:c + 1], after=(V.last(),))
    rf, aaf, bbf = (x.rearrange("p c t -> p (c t)") for x in (RR, AA, BB))
    V.op(V.eng.tensor_scalar, bbf, rf, 1.3e-35, None, ALU.max, after=(A.last(),))
    ms = A.op(A.eng.activation, bbf, bbf, ACT.Sqrt, after=(V.last(),))
    hhf, xcf, iif = (x.rearrange("p c t -> p (c t)") for x in (HH, XC, II))
    V.op(V.eng.tensor_scalar, hhf, rf, 1.0, None, ALU.add)
    V.op(V.eng.reciprocal, hhf, hhf)
    V.op(V.eng.tensor_scalar, aaf, rf, -1.0, 1.0, ALU.mult, ALU.add)
    V.op(V.eng.tensor_tensor, aaf, aaf, hhf, ALU.mult)
    V.op(V.eng.tensor_tensor, xcf, xcf, iif, ALU.mult)
    V.op(V.eng.scalar_tensor_tensor, xcf, xcf, 2.0, hhf, ALU.mult, ALU.mult)
    V.op(V.eng.tensor_tensor, bbf, bbf, xcf, ALU.mult, after=(ms,))
    for c in range(4):
        V.op(V.eng.tensor_tensor_scan, HH[:, c, :], AA[:, c, :], BB[:, c, :], 0.0, ALU.mult, ALU.add)
    m = V.op(V.eng.tensor_tensor, hhf, hhf, GT.rearrange("p c t -> p (c t)"), ALU.mult)
    for b in range(2):
        T.wait(m, bank_free[4 + b])
        for c in range(4):
            ins = nc.tensor.transpose(PS[:, 4 + b, c * P:(c + 1) * P], HH[:, c, b * P:(b + 1) * P], ident[:, :])
        mt = T.mark(ins)
        d = V.op(V.eng.tensor_copy, Y[:, b, 0:512], PS[:, 4 + b, :], after=(mt,))
        bank_free[4 + b] = d
        A.op(A.eng.activation, DS[:, 0:512], Y[:, b, 0:512], ACT.Square, accum_out=oss2[:, 0, b:b + 1], after=(d,))
    group_norm_out(oss2, g_grp, None)
    if dbg == "x1":
        return finish_debug(nc, S, X, V, out)

    MEM = DS[:, 0:2048].rearrange("p (b n) -> p b n", b=2)
    MT = ACTS[:, 0:2048].rearrange("p (k t) -> p k t", k=8)
    KM = ACTS[:, 2048:4096].rearrange("p (c t) -> p c t", c=8)
    VM = ACTS[:, 4096:6144].rearrange("p (b n) -> p b n", b=2)
    QM = ACTS[:, 6144:8192].rearrange("p (c t) -> p c t", c=8)
    PM = ACTS[:, 8192:9216].rearrange("p (h k) -> p h k", h=4)
    PTM = ACTS[:, 9216:10240].rearrange("p (b h q) -> p b h q", b=2, h=4)
    l_m = Load(nc, "l_m")
    for b in range(2):
        l_m.start(A, MEM[:, b, :], a["mem_2"][0, b * P:(b + 1) * P, :], after=(A.last(), V.last(), T.last()))
    m = norm(MEM, Y, after=(l_m.mark(),))
    mt_ready = transposed(Y, g_mem, MT, (m,))
    turn = 0
    for i in range(2):
        tile, landed = ring.take()
        for c2 in range(2):
            bank = 4 + turn % 4
            turn += 1
            features_by(w8(tile), MT, 2 * c2, bank, 0, after=(landed, *mt_ready))
            m = features_by(w8(tile), MT, 2 * c2 + 1, bank, 1)
            d = KM[:, 4 * i + 2 * c2:4 * i + 2 * c2 + 2, :].rearrange("p c t -> p (c t)")
            bank_free[bank] = V.op(V.eng.tensor_copy, d, PS[:, bank, :], after=(m,), chain=False)
        ring.free(m)
    for i in range(2):
        tile, landed = ring.take()
        for b in range(2):
            bank = 4 + turn % 4
            turn += 1
            m = tokens_by(w8(tile), MT, b, bank, after=(landed,))
            bank_free[bank] = A.op(A.eng.activation, VM[:, b, 512 * i:512 * i + 512], PS[:, bank, :], ACT.Copy,
                                   after=(m,), chain=False)
        ring.free(m)
    m = norm(X, Y)
    ht_ready = transposed(Y, g_cross, HT, (m,))
    for i in range(2):
        tile, landed = ring.take()
        for c2 in range(2):
            bank = 4 + turn % 4
            turn += 1
            features_by(w8(tile), HT, 2 * c2, bank, 0, after=(landed, *ht_ready))
            m = features_by(w8(tile), HT, 2 * c2 + 1, bank, 1)
            d = QM[:, 4 * i + 2 * c2:4 * i + 2 * c2 + 2, :].rearrange("p c t -> p (c t)")
            bank_free[bank] = V.op(V.eng.tensor_scalar, d, PS[:, bank, :], 1.0 / 16, None, ALU.mult, after=(m,),
                                   chain=False)
        ring.free(m)
    q_ready = [V.last(), A.last()]
    S4 = PS[:, 0:2, :].rearrange("p a (c k) -> p (a c) k", k=256)
    for b in range(2):
        T.wait(*q_ready, bank_free[0], bank_free[1])
        for h in range(4):
            for c in range(2):
                ins = mm(S4[:, h, :], QM[:, 2 * h + c, b * P:(b + 1) * P], KM[:, 2 * h + c, :],
                         start=(c == 0), stop=(c == 1))
        m = T.mark(ins)
        V.op(V.eng.tensor_reduce, mx[:, 0:4], S4, AX, ALU.max, after=(m, A.last()))
        V.op(V.eng.tensor_scalar, nm[:, 0:4], mx[:, 0:4], -1.0, None, ALU.mult)
        for h in range(4):
            e = A.op(A.eng.activation, PM[:, h, :], S4[:, h, :], ACT.Exp, bias=nm[:, h:h + 1],
                     accum_out=lsum[:, h:h + 1], after=(V.last(), T.last()), chain=False)
        bank_free[0] = bank_free[1] = e
        rec = V.op(V.eng.reciprocal, rl[:, 0:4], lsum[:, 0:4], after=(e,))
        for kb in range(2):
            T.wait(bank_free[4 + kb], e)
            for h in range(4):
                ins = nc.tensor.transpose(PS[:, 4 + kb, h * P:(h + 1) * P], PM[:, h, kb * P:(kb + 1) * P], ident[:, :])
            mt = T.mark(ins)
            bank_free[4 + kb] = V.op(V.eng.tensor_copy, PTM[:, kb].rearrange("p h q -> p (h q)"), PS[:, 4 + kb, :],
                                     after=(mt,), chain=False)
        T.wait(V.last(), bank_free[6], bank_free[7])
        for h in range(4):
            for kb in range(2):
                ins = mm(PS[:, 6 + h // 2, (h % 2) * 256:(h % 2) * 256 + 256], PTM[:, kb, h, :],
                         VM[:, kb, 256 * h:256 * h + 256], start=(kb == 0), stop=(kb == 1))
        m = T.mark(ins)
        for i in range(2):
            d = V.op(V.eng.tensor_tensor, Y[:, b, 512 * i:512 * i + 512].rearrange("p (h d) -> p h d", h=2),
                     PS[:, 6 + i, :].rearrange("p (h d) -> p h d", h=2),
                     rl[:, 2 * i:2 * i + 2].rearrange("p (n o) -> p n o", o=1).broadcast_to((P, 2, 256)), ALU.mult,
                     after=(m, rec))
            bank_free[6 + i] = d
    ready = transposed(Y, None, HT, (V.last(),))
    add_product(ready)
    if dbg == "x2":
        return finish_debug(nc, S, X, V, out)

    m = norm(X, Y)
    ht_ready = transposed(Y, g_ffn2, HT, (m,))
    QP = DS[:, 0:4096].rearrange("p (j t) -> p j t", j=16)
    SC = DS[:, 4096:8192].rearrange("p (b j n) -> p b j n", b=2, j=16)
    turn = 0
    for i in range(4):
        tile, landed = ring.take()
        for c2 in range(2):
            bank = 4 + turn % 4
            turn += 1
            features_by(w8(tile), HT, 2 * c2, bank, 0, after=(landed, *ht_ready))
            m = features_by(w8(tile), HT, 2 * c2 + 1, bank, 1)
            d = QP[:, 4 * i + 2 * c2:4 * i + 2 * c2 + 2, :].rearrange("p c t -> p (c t)")
            bank_free[bank] = V.op(V.eng.tensor_copy, d, PS[:, bank, :], after=(m,), chain=False)
        ring.free(m)
    tile, landed = ring.take()
    SK = tile[:, 0:2048].rearrange("p (j n) -> p j n", j=16)
    q_ready = V.last()
    for b in range(2):
        for q in range(4):
            bank = 4 * b + q
            T.wait(bank_free[bank], q_ready, landed)
            for j in range(4 * q, 4 * q + 4):
                ins = mm(PS[:, bank, (j % 4) * P:(j % 4 + 1) * P], QP[:, j, b * P:(b + 1) * P], SK[:, j, :],
                         start=True, stop=True)
            m = T.mark(ins)
            bank_free[bank] = A.op(A.eng.activation, SC[:, b, 4 * q:4 * q + 4, :].rearrange("p j n -> p (j n)"),
                                   PS[:, bank, :], ACT.Copy, after=(m,), chain=False)
    ring.free(m)
    sc_ready = A.last()

    ROUTED = routing(nc, V, A, G, T, SC, DS, Y, iota, ident, PS, bank_free, sm, sc_ready)

    W = ACTS[:, :].rearrange("p (n t) -> p n t", n=64)
    y_started = False
    v_last = [None]
    for hf in range(2):
        act_ready = up_phase(nc, ring, T, A, W, HT, PS, bank_free, ht_ready, v_last[0])
        if hf == 0:
            I1T, I2T, GTT, r_ready = ROUTED()
        w_ready = gate_phase(nc, V, G, T, W, I1T, I2T, GTT, iota, DS, PS, bank_free, hf, act_ready, r_ready)
        for i in range(16):
            tile, landed = ring.take()
            vt = tile.rearrange("p (j d) -> p j d", j=4)
            T.wait(landed, w_ready, *[bank_free[q] for q in range(4)])
            for j in range(4):
                n = 4 * i + j
                for b in range(2):
                    for half in range(2):
                        ins = mm(PS[:, 2 * b + half, :], W[:, n, b * P:(b + 1) * P], vt[:, j, 512 * half:512 * half + 512],
                                 start=(hf == 0 and n == 0), stop=(hf == 1 and n == 63), skip_group_check=True)
            m = T.mark(ins)
            ring.free(m)
        v_last[0] = m
    gf = DS[:, 0:1024]
    l_f = Load(nc, "l_f")
    l_f.start(A, gf, a["norm_final_2"].rearrange("(o n) -> o n", o=1).broadcast_to((P, D)), after=(m, V.last()))
    for b in range(2):
        for half in range(2):
            xb = X[:, b, 512 * half:512 * half + 512]
            V.op(V.eng.tensor_tensor, xb, xb, PS[:, 2 * b + half, :], ALU.add, after=(m,), chain=False)
    norm(X, Y)
    for b in range(2):
        V.op(V.eng.tensor_tensor, Y[:, b, :], Y[:, b, :], gf, ALU.mult, after=(l_f.mark(),))
    l_o = Load(nc, "l_o")
    for b in range(2):
        l_o.start(S, out[0, b * P:(b + 1) * P, :], Y[:, b, :], after=(V.last(),))
    S.wait(l_o.mark())


def finish_debug(nc, S, X, V, out):
    l_o = Load(nc, "l_o")
    for b in range(2):
        l_o.start(S, out[0, b * P:(b + 1) * P, :], X[:, b, :], after=(V.last(),))
    S.wait(l_o.mark())


def overflow(nc, a, lanes, flag, flag_ready, X, HT, OV, ACTS, PS):
    mains = lanes
    for lane in mains:
        lane.wait(flag_ready, *[o.last() for o in mains])
    V, A, T = (Lane(nc, o.eng, f"{o.name}_ov") for o in mains)
    WG, WU, WD = (ACTS[:, 4096 * i:4096 * i + 4096] for i in range(3))
    wg, wu = (w.rearrange("p (k n) -> p k n", k=8) for w in (WG, WU))
    wd = WD.rearrange("p (c n) -> p c n", c=4)
    HU = ACTS[:, 12288:13312].rearrange("p (c t) -> p c t", c=4)
    l_w = Load(nc, "l_ov")

    per_t, per_a, per_v = 4 * 2 + 2, 4, 4 + 4

    def t_mark(e, i):
        return (T.sem, per_t * e + i + 1)

    def a_mark(e, i):
        return (A.sem, per_a * e + i + 1)

    def v_mark(e, i):
        return (V.sem, per_v * e + i + 1)

    def body_tensor():
        for e in range(32):
            T.wait((l_w.sem, 48 * (e + 1)))
            for c in range(4):
                for s, w in enumerate((wg, wu)):
                    bank = 2 * (c % 2) + s
                    if c >= 2:
                        T.wait(v_mark(e, c - 2))
                    elif e:
                        T.wait(v_mark(e - 1, 2 + c))
                    for k in range(8):
                        ins = nc.tensor.matmul(
                            PS[:, bank, 0:256],
                            w.rearrange("p k (f c) -> p k c f", c=4)[:, k, c, :], HT[:, k, :],
                            start=(k == 0), stop=(k == 7))
                    T.mark(ins)
            T.wait(v_mark(e, 3))
            if e:
                T.wait(v_mark(e - 1, 7))
            for b in range(2):
                for half in range(2):
                    for c in range(4):
                        ins = nc.tensor.matmul(PS[:, 4 + 2 * b + half, :], HU[:, c, b * P:(b + 1) * P],
                                               wd[:, c, 512 * half:512 * half + 512], start=(c == 0), stop=(c == 3))
                T.mark(ins)

    def body_scalar():
        for e in range(32):
            if e:
                A.wait(t_mark(e - 1, 9))
            for dst, n, k in ((WG, "w_gate", 8), (WU, "w_up", 8), (WD, "w_down", 4)):
                l_w.start(A, dst, a[n][0, e].rearrange("(p k) n -> p (k n)", k=k))
            for c in range(4):
                A.wait(t_mark(e, 2 * c))
                A.mark(nc.scalar.activation(HU[:, c, :], PS[:, 2 * (c % 2), 0:256], ACT.Silu))

    def body_vector():
        for e in range(32):
            for c in range(4):
                V.wait(a_mark(e, c), t_mark(e, 2 * c + 1))
                V.mark(nc.vector.tensor_tensor(HU[:, c, :], HU[:, c, :], PS[:, 2 * (c % 2) + 1, 0:256], ALU.mult))
            for b in range(2):
                V.wait(t_mark(e, 8 + b))
                if e:
                    V.wait(v_mark(e - 1, 4 + 2 * b + 1))
                for half in range(2):
                    xb = X[:, b, 512 * half:512 * half + 512]
                    V.mark(nc.vector.scalar_tensor_tensor(xb, PS[:, 4 + 2 * b + half, :], OV[:, b, e:e + 1], xb,
                                                          ALU.mult, ALU.add))
        V.wait(V.last(), (A.sem, per_a * 32), (T.sem, per_t * 32))

    value = nc.values_load(flag[0:1, 0:1], min_val=0, max_val=8192)
    with nc.If(value > 0):
        body_tensor()
        body_scalar()
        body_vector()


def routing(nc, V, A, G, T, SC, DS, Y, iota, ident, PS, bank_free, sm, sc_ready):
    HK = 128
    at = [0]
    yf = Y[:, :, :].rearrange("p b n -> p (b n)")

    def part(n):
        s = yf[:, at[0]:at[0] + n]
        at[0] += n
        return s

    v, ixf, tv, pa, pb_, i1s, i2s, gg = (part(n) for n in (256, 256, 128, 128, 128, 128, 128, 128))
    ix = part(256).bitcast(U32)
    T3 = part(512).rearrange("p (j t) -> p j t", j=2)
    GTT = nc.alloc_sbuf_tensor("gtt", [P, 256], F32)[:, :]
    I1T, I2T = T3[:, 0, :], T3[:, 1, :]
    S2 = DS[:, 0:2048].rearrange("p (j n) -> p j n", j=16)
    CAND = DS[:, 0:2048].rearrange("p (h n) -> p h n", h=8)
    TMP = DS[:, 2048:4096]
    hm, hs = sm(8), sm(8)
    pos = pa.bitcast(U32)
    posb = pb_.bitcast(U32)

    def emit():
        V.wait(sc_ready, T.last())
        for b in range(2):
            for j in range(16):
                s, s2 = SC[:, b, j, :], S2[:, j, :]
                vj, ij = v[:, 16 * j:16 * j + 16], ix[:, 16 * j:16 * j + 16]
                V.op(V.eng.max, vj[:, 0:8], s)
                V.op(V.eng.match_replace, s2, vj[:, 0:8], s, -3.0e38)
                V.op(V.eng.max, vj[:, 8:16], s2)
                V.op(V.eng.max_index, ij[:, 0:8], vj[:, 0:8], s, chain=False)
                V.op(V.eng.max_index, ij[:, 8:16], vj[:, 8:16], s2)
            V.op(V.eng.tensor_copy, ixf, ix)
            vv = v.rearrange("p (h s n) -> p h s n", h=8, s=2)
            for h in range(8):
                V.op(V.eng.tensor_tensor, CAND[:, h, :].rearrange("p (x y) -> p x y", x=16),
                     vv[:, h, 0, :].rearrange("p (n o) -> p n o", o=1).broadcast_to((P, 16, 16)),
                     vv[:, h, 1:2, :].broadcast_to((P, 16, 16)), ALU.add)
            C2 = SC[:, b, :, :].rearrange("p (h j) n -> p h (j n)", h=8)
            for h in range(8):
                th, ph = tv[:, 16 * h:16 * h + 16], pos[:, 16 * h:16 * h + 16]
                V.op(V.eng.max, th[:, 0:8], CAND[:, h, :])
                V.op(V.eng.match_replace, C2[:, h, :], th[:, 0:8], CAND[:, h, :], -3.0e38)
                V.op(V.eng.max, th[:, 8:16], C2[:, h, :])
                V.op(V.eng.max_index, ph[:, 0:8], th[:, 0:8], CAND[:, h, :], chain=False)
                V.op(V.eng.max_index, ph[:, 8:16], th[:, 8:16], C2[:, h, :])
            t8 = tv.rearrange("p (h k) -> p h k", h=8)
            g8 = gg.rearrange("p (h k) -> p h k", h=8)
            V.op(V.eng.tensor_tensor, g8, t8, t8[:, :, 0:1].broadcast_to((P, 8, 16)), ALU.subtract)
            m = A.op(A.eng.activation, gg, gg, ACT.Exp, after=(V.last(),))
            V.op(V.eng.tensor_scalar, posb, pos, 15, None, ALU.bitwise_and)
            V.op(V.eng.tensor_scalar, pos, pos, 4, None, ALU.logical_shift_right)
            V.op(V.eng.tensor_copy, i1s, pos)
            V.op(V.eng.tensor_copy, i2s, posb)
            xf = ixf.rearrange("p (h s n) -> p h s n", h=8, s=2)
            T4 = TMP.rearrange("p (h k n) -> p h k n", h=8, k=16)
            i16 = iota[:, 0:16].rearrange("p (o n) -> p o n", o=1).broadcast_to((P, HK, 16))
            for s, sel in enumerate((i1s, i2s)):
                V.op(V.eng.tensor_tensor, TMP.rearrange("p (k n) -> p k n", n=16), i16,
                     sel.rearrange("p (k o) -> p k o", o=1).broadcast_to((P, HK, 16)), ALU.is_equal)
                for h in range(8):
                    V.op(V.eng.tensor_tensor, T4[:, h], T4[:, h], xf[:, h, s:s + 1, :].broadcast_to((P, 16, 16)),
                         ALU.mult, chain=(h == 0))
                V.op(V.eng.tensor_reduce, sel, TMP.rearrange("p (k n) -> p k n", n=16), AX, ALU.add)
            V.op(V.eng.tensor_reduce, hs, g8, AX, ALU.add, after=(m,))
            V.op(V.eng.reciprocal, hs, hs)
            mg = V.op(V.eng.tensor_tensor, g8, g8, hs.rearrange("p (h o) -> p h o", o=1).broadcast_to((P, 8, 16)), ALU.mult)
            T.wait(mg, bank_free[6])
            for i, src in enumerate((i1s, i2s, gg)):
                ins = nc.tensor.transpose(PS[:, 6, i * P:(i + 1) * P], src, ident[:, :])
            mt = T.mark(ins)
            for i, dst in enumerate((I1T, I2T, GTT)):
                d = V.op(V.eng.tensor_copy, dst[:, b * P:(b + 1) * P], PS[:, 6, i * P:(i + 1) * P], after=(mt,))
            bank_free[6] = d
        return I1T, I2T, GTT, V.last()

    return emit


def up_phase(nc, ring, T, A, W, HT, PS, bank_free, ht_ready, v_last):
    for i in range(16):
        tile, landed = ring.take()
        u = tile.rearrange("p (j k n) -> p j k n", j=4, k=8)
        T.wait(landed, *ht_ready)
        for j2 in range(2):
            bank = 4 + j2
            T.wait(bank_free[bank])
            for j in (2 * j2, 2 * j2 + 1):
                for k in range(8):
                    ins = nc.tensor.matmul(PS[:, bank, (j % 2) * 256:(j % 2) * 256 + 256], u[:, j, k, :], HT[:, k, :],
                                           start=(k == 0), stop=(k == 7))
            m = T.mark(ins)
            n = 4 * i + 2 * j2
            bank_free[bank] = A.op(A.eng.activation, W[:, n:n + 2, :].rearrange("p n t -> p (n t)"), PS[:, bank, :],
                                   ACT.Gelu_apprx_tanh, after=(m, v_last), chain=False)
        ring.free(m)
    return A.last()


def gate_phase(nc, V, G, T, W, I1T, I2T, GTT, iota, DS, PS, bank_free, hf, act_ready, r_ready):
    NB = 2
    E1 = DS[:, 0:NB * 1024].rearrange("p (i t n) -> p i t n", i=NB, t=8)
    E2 = DS[:, 2048:2048 + NB * 512].rearrange("p (i t n) -> p i t n", i=NB, t=8)
    used = [None] * NB
    for q in range(32):
        i = q % NB
        bank = 6 + q % 2
        for t in range(8):
            tt = 8 * q + t
            g = G.op(G.eng.tensor_scalar, E1[:, i, t, :], iota[:, :], I1T[:, tt:tt + 1], None, ALU.is_equal,
                     after=(r_ready, T.last() if q < 2 else None, used[i]), chain=False)
        for t in range(8):
            tt = 8 * q + t
            v = V.op(V.eng.tensor_scalar, E2[:, i, t, :], iota[:, 64 * hf:64 * hf + 64], I2T[:, tt:tt + 1],
                     GTT[:, tt:tt + 1], ALU.is_equal, ALU.mult,
                     after=(T.last() if q < 2 else None, used[i]), chain=False)
        T.wait(g, v, bank_free[bank])
        for t in range(8):
            ins = nc.tensor.matmul(PS[:, bank, 64 * t:64 * t + 64], E1[:, i, t, :], E2[:, i, t, :],
                                   start=True, stop=True)
        used[i] = T.mark(ins)
        if q:
            _weigh(V, W, PS, bank_free, q - 1, last, act_ready)
        last = used[i]
    _weigh(V, W, PS, bank_free, 31, last, act_ready)
    return V.last()


def _weigh(V, W, PS, bank_free, q, ready, act_ready):
    bank = 6 + q % 2
    w = W[:, :, 8 * q:8 * q + 8]
    bank_free[bank] = V.op(V.eng.tensor_tensor, w, PS[:, bank, :].rearrange("p (t n) -> p n t", t=8), w, ALU.mult,
                           after=(ready, act_ready), chain=False)


_RAW = ["x", "norm_mix", "w_in", "b_forget", "q_norm_fox", "k_norm_fox", "q_norm_dil", "k_norm_dil",
        "out_norm_fox", "out_norm_dil", "w_out", "norm_ffn", "b_router_group", "b_router_expert", "w_gate",
        "w_up", "w_down", "mem_2", "norm_mix_2", "w_in_2", "norm_grp_a_2", "norm_grp_b_2", "w_out_2",
        "norm_cross_2", "norm_mem_2", "w_q_mem_2", "w_kv_mem_2", "w_o_mem_2", "norm_ffn_2", "w_query_2",
        "norm_final_2"]


def _constants():
    t = np.arange(256)
    q, k = t[:, None], t[None, :]
    by_tile = lambda m: np.ascontiguousarray(m.reshape(2, 128, -1).transpose(1, 0, 2), dtype=np.float32)
    causal = k <= q
    count = (causal & (q - k <= 128)).astype(int) + (causal & ((q - k) % 4 == 0)) + (causal & ((q - k) % 16 == 0))
    inv = 1.0 / (np.float32(10000.0) ** (np.arange(0, 64, 2, dtype=np.float32) / np.float32(64)))
    ang = t.astype(np.float32)[:, None] * inv.astype(np.float32)[None, :]
    rope = np.stack([by_tile(np.cos(ang)), by_tile(np.sin(ang))], axis=1)
    sel = np.zeros((8, 8, 128), np.float32)
    for h in range(8):
        sel[h, h] = 1.0
    return {
        "c_ident": np.eye(128, dtype=np.float32),
        "c_iota": np.tile(np.arange(128, dtype=np.float32), (128, 1)),
        "c_tri": by_tile((q <= k).astype(np.float32)),
        "c_fox": by_tile(np.where(causal, 0.0, NEG)),
        "c_dil": by_tile(np.where(count > 0, np.log(np.maximum(count, 1)), NEG)),
        "c_rope": np.ascontiguousarray(rope, dtype=np.float32),
        "c_sel": sel,
    }


def _laid_out(i):
    c = np.ascontiguousarray
    out = {n: c(i[n]) for n in _RAW}
    out |= _constants()
    we = i["w_router_expert"][0].transpose(1, 0, 2).reshape(1024, 32)
    out["w_router"] = c(np.concatenate([i["w_router_group"][0], we], axis=1).reshape(128, 8, 36))
    chunks = lambda v: c(v.reshape(4, 128).T)
    out["conv_w_2"] = c(i["conv_w_2"][0].reshape(4, 4, 128).transpose(2, 1, 0))
    for n in ("conv_b_2", "gate_a_b_2", "gate_x_b_2", "lru_lambda_2"):
        out[n] = chunks(i[n][0])
    for n in ("gate_a_w_2", "gate_x_w_2"):
        out[n] = c(i[n][0].reshape(4, 2, 64, 64).transpose(1, 2, 0, 3).reshape(128, 4, 64))
    t = np.arange(256)
    rel = np.clip(t[:, None] - t[None, :], -128, 128) + 128
    rel = np.where(t[None, :] // 64 <= t[:, None] // 64, rel, 257)
    ext = np.concatenate([i["rel_bias_2"][0], np.full((8, 1), NEG, np.float32)], axis=1)
    slots = [2 * (s % 4) + s // 4 for s in range(8)]
    bias = ext[slots][:, rel].transpose(1, 0, 2)
    out["bias_2"] = c(np.concatenate([bias[:128, :, :128].reshape(128, -1), bias[128:].reshape(128, -1)], axis=1))
    out["sub_keys_2"] = c(i["sub_keys_2"][0].transpose(3, 0, 1, 2).reshape(128, 2048))
    u = i["expert_u_2"][0].reshape(128, 32, 4, 128, 8)
    out["expert_u_2"] = c(u.transpose(1, 3, 2, 4, 0).reshape(32, 128, 4096))
    v = i["expert_v_2"][0].reshape(128, 32, 4096)
    out["expert_v_2"] = c(v.transpose(1, 0, 2))
    return out


def kernel(**inputs):
    import concourse.bacc as _bacc
    from concourse.bass_utils import run_bass_kernel_spmd as _run

    nc = _bacc.Bacc("TRN2", target_bir_lowering=False, num_devices=1)
    arrays = _laid_out({k: np.asarray(v) for k, v in inputs.items()})
    aps, send = {}, {}
    for name, v in arrays.items():
        send[f"in_{name}"] = v
        aps[name] = nc.dram_tensor(f"in_{name}", v.shape, mybir.dt.from_np(v.dtype), kind="ExternalInput").ap()
    out = nc.dram_tensor("out_0", (1, 256, 1024), F32, kind="ExternalOutput").ap()
    program(nc, aps, out)
    r = _run(nc, [send], core_ids=[0])
    return r.results[0]["out_0"]
```

```python
import math

import numpy as np

import concourse.bass as bass
from concourse import mybir

F32 = mybir.dt.float32
FR = mybir.dt.float32r
U32 = mybir.dt.uint32
I32 = mybir.dt.int32
ALU = mybir.AluOpType
ACT = mybir.ActivationFunctionType
AX = mybir.AxisListType.X

EPS = 1e-6
NEG = -1e30
P = 128
D = 1024
CAP = 64
NPACK = 142


class Lane:

    def __init__(self, nc, eng, name):
        self.eng, self.name = eng, name
        self.sem = nc.alloc_semaphore(name)
        self.n = 0
        self.seen = {}

    def wait(self, *marks):
        for m in marks:
            if m is None:
                continue
            if isinstance(m, list):
                self.wait(*m)
                continue
            sem, v = m
            if self.seen.get(sem.name, 0) < v:
                self.eng.wait_ge(sem, v)
                self.seen[sem.name] = v

    def mark(self, ins):
        self.n += 1
        ins.then_inc(self.sem, 1)
        return (self.sem, self.n)

    def last(self):
        return (self.sem, self.n)

    def op(self, build, *args, after=(), chain=True, **kw):
        self.wait(*after)
        if chain and self.n:
            self.wait(self.last())
        return self.mark(build(*args, **kw))


class Load:

    def __init__(self, nc, name):
        self.sem, self.n = nc.alloc_semaphore(name), 0

    def start(self, lane, dst, src, after=()):
        lane.wait(*after)
        lane.eng.dma_start(dst, src).then_inc(self.sem, 16)
        self.n += 16
        return (self.sem, self.n)

    def mark(self):
        return (self.sem, self.n)


class Ring:

    def __init__(self, nc, lane, slots, plan, slot_of):
        self.lane, self.slots, self.plan, self.slot_of = lane, slots, plan, slot_of
        self.sems = [nc.alloc_semaphore(f"s_ring{i}") for i in range(len(slots))]
        self.before, self.turn, last, count = [], [], {}, {}
        for i, s in enumerate(slot_of):
            self.before.append(last.get(s))
            count[s] = count.get(s, 0) + 1
            self.turn.append(count[s])
            last[s] = i
        self.issued = self.taken = self.freed = 0
        self.marks = {}
        self._issue()

    def _issue(self):
        while self.issued < len(self.plan):
            i = self.issued
            before = self.before[i]
            if before is not None and before not in self.marks:
                return
            n, pat, kw, src = self.plan[i]
            dst = self.slots[self.slot_of[i]][:, 0:n]
            if pat:
                dst = dst.rearrange(pat, **kw)
            if before is not None:
                self.lane.wait(*self.marks[before])
            self.lane.eng.dma_start(dst, src).then_inc(self.sems[self.slot_of[i]], 16)
            self.issued += 1

    def take(self):
        i = self.taken
        self.taken += 1
        assert i < self.issued
        return self.slots[self.slot_of[i]], (self.sems[self.slot_of[i]], 16 * self.turn[i])

    def hold(self, n):
        held = list(range(self.freed, self.freed + n))
        self.freed += n
        return held

    def free_held(self, i, *marks):
        self.marks[i] = marks
        self._issue()

    def free(self, *marks):
        self.marks[self.freed] = marks
        self.freed += 1
        self._issue()


class Halves:

    def __init__(self, V, A, bufs, fr):
        self.V, self.A, self.bufs, self.fr = V, A, bufs, fr
        self.used = [None] * len(bufs)
        self.n = 0

    def split(self, tile, landed, n=2048, after=()):
        V, A = self.V, self.A
        i = self.n % len(self.bufs)
        self.n += 1
        hi = self.bufs[i][:, 0:n]
        raw = tile[:, 0:n]
        m = A.op(A.eng.activation, self.fr(hi), raw, ACT.Copy, after=(landed, self.used[i], *after), chain=False)
        m = V.op(V.eng.tensor_tensor, self.fr(raw), raw, self.fr(hi).bitcast(F32), ALU.subtract, after=(m, landed), chain=False)
        return self.fr(hi), self.fr(raw), m, i

    def free(self, i, mark):
        self.used[i] = mark


def program(nc, a, out, dbg=None):
    sb = lambda name, shape, dt=F32: nc.alloc_sbuf_tensor(name, shape, dt)
    twins = {}

    def twin(name, shape, piece=None):
        t = sb(name, shape)
        row = math.prod(shape[1:])
        piece = piece or row
        start = nc.sbuf_base - 4 * row
        twins[name] = piece, [nc.alloc_sbuf_tensor_at(f"{name}_parts{i}", [P, piece], FR, offset=start + 4 * piece * i)
                              for i in range(row // piece)]
        return t

    def fr(x):
        piece, names = twins[x.tensor.name]
        (_, rows), *rest = x.ap
        assert rows == P
        return bass.AP(names[x.offset // piece], x.offset % piece, [[piece, P], *rest])

    V = Lane(nc, nc.vector, "s_dve")
    A = Lane(nc, nc.scalar, "s_act")
    T = Lane(nc, nc.tensor, "s_pe")
    G = Lane(nc, nc.gpsimd, "s_pool")
    S = Lane(nc, nc.sync, "s_sp")
    mm = nc.tensor.matmul

    BIG = twin("big", [P, 32768], 8192)
    FIX = twin("fix", [P, 5, 2048])
    ACTS, DS = BIG[:, 0:16384], BIG[:, 24576:32768]
    X = twin("x", [P, 2, D])
    HH = twin("hh", [P, 8, 256])
    HL = twin("hl", [P, 8, 256])
    HT = (fr(HH[:, :, :]), fr(HL[:, :, :]))
    Y = twin("y", [P, 2, D])
    ii = sb("ii", [P, 2, P])
    ident, iota = ii[:, 0, :], ii[:, 1, :]
    tig = sb("tig", [P, 768])
    tri = tig[:, 0:512].rearrange("p (b k) -> p b k", b=2)
    small = sb("small", [P, 880])
    PS = nc.alloc_psum_tensor("ps", [P, 8, 512], F32)
    bank_free = [None] * 8
    small_at = [0]

    def sm(n):
        s = small[:, small_at[0]:small_at[0] + n]
        small_at[0] += n
        return s

    def cols(w, n0, n=512):
        w = w.rearrange("(p k) n -> p k n", k=8)
        return [(4 * n, "p (k n) -> p k n", dict(k=4), w[:, 4 * h:4 * h + 4, n0:n0 + n]) for h in range(2)]

    def whole(src):
        return [(2048, None, None, src[:, 2048 * h:2048 * h + 2048]) for h in range(2)]

    def product(w, n):
        return [t for i in range(n) for t in cols(w, 512 * i)]

    plan = product(a["w_in"][0], 6) + product(a["w_out"][0], 2)
    for e in range(0, 32, 2):
        for w, k in (("w_gate", 8), ("w_up", 8), ("w_down", 4)):
            one, two = (whole(a[w][0, i].rearrange("(p k) n -> p (k n)", k=k)) for i in (e, e + 1))
            plan += [one[0], two[0], one[1], two[1]]
    plan += product(a["w_in_2"][0], 4)
    plan += [(1024, None, None, a["bias_2"][:, 0:1024]), (2048, None, None, a["bias_2"][:, 1024:3072])]
    plan += cols(a["w_in_2"][0], 2048)
    plan += product(a["w_out_2"][0], 2)
    plan += product(a["w_kv_mem_2"][0], 4) + product(a["w_q_mem_2"][0], 2) + product(a["w_o_mem_2"][0], 2)
    plan += product(a["w_query_2"][0], 4)
    plan.append((2048, None, None, a["sub_keys_2"]))
    slot_of = [i % 7 for i in range(len(plan))]
    for w in ("expert_u_2", "expert_v_2"):
        for i in range(32):
            plan += whole(a[w][i])
    slot_of += [i % 3 for i in range(128)]
    slots = [FIX[:, i, :] for i in range(3)] + [BIG[:, 16384 + 2048 * i:18432 + 2048 * i] for i in range(4)]
    split_bufs = [FIX[:, 3, :], FIX[:, 4, :]]

    l_x = Load(nc, "l_x")
    for b in range(2):
        l_x.start(S, X[:, b, :], a["x"][0, b * P:(b + 1) * P, :])
    l_c = Load(nc, "l_c")
    l_c.start(A, ii[:, :, :], a["c_ii"])
    l_c.start(A, small[:, 0:NPACK], a["pack"])
    l_s = Load(nc, "l_s")
    l_s.start(A, ACTS[:, 14336:15968], a["pack_acts"])
    l_s.start(A, tri, a["c_tri"])
    l_s.start(A, DS[0:8, 7168:8192], a["c_sel"].rearrange("h a q -> h (a q)"))
    ring = Ring(nc, S, slots, plan, slot_of)
    PROJ = ACTS[:, 0:6144].rearrange("p (b n) -> p b n", b=2)
    QK = ACTS[:, 6144:10240].rearrange("p (j c t) -> p j c t", j=4, c=4)
    PB = ACTS[:, 10240:12288].rearrange("p (h k) -> p h k", h=8)
    PT = ACTS[:, 12288:14336].rearrange("p (b h q) -> p b h q", b=2, h=8)
    MF = ACTS[:, 14336:14848].rearrange("p (b k) -> p b k", b=2)
    MD = ACTS[:, 14848:15360].rearrange("p (b k) -> p b k", b=2)
    ROPE = ACTS[:, 15360:15488].rearrange("p (s b f) -> p s b f", s=2, b=2)
    GDIL = ACTS[:, 15488:15616].rearrange("p (s d) -> p s d", s=2)
    CT = ACTS[0:8, 15968:16224]
    SEL = DS[0:8, 7168:8192].rearrange("p (h q) -> p h q", h=8)

    def packed(n):
        small_at[0] += n
        return small[:, small_at[0] - n:small_at[0]]

    g_mix, g_out, g_ffn, g_mix2, g_cross, g_mem, g_ffn2, g_grp = (packed(8) for _ in range(8))
    gq, gk, bf, br, cw, cb, gab, gxb, lam = (packed(n) for n in (1, 1, 8, 36, 16, 4, 4, 4, 4))
    cw = cw.rearrange("p (c w) -> p c w", c=4)
    assert small_at[0] == NPACK
    consts = [l_c.mark()]
    halves = Halves(V, A, split_bufs, fr)

    def rstd_of(ss, n, width, scale=None):
        V.op(V.eng.tensor_scalar, ss, ss, 1.0 / width, EPS, ALU.mult, ALU.add, after=(A.last(),))
        A.op(A.eng.activation, ss, ss, ACT.Sqrt, after=(V.last(),))
        m = V.op(V.eng.reciprocal, ss, ss, after=(A.last(),))
        if scale is not None:
            m = V.op(V.eng.tensor_scalar, ss, ss, scale, None, ALU.mult)
        return m

    def transposed(xs, gain, dst, after):
        hi, lo = dst
        for bank in range(4):
            T.wait(bank_free[bank], *after)
            for k in (2 * bank, 2 * bank + 1):
                for b in range(2):
                    ins = nc.tensor.transpose(
                        PS[:, bank, (k % 2) * 256 + b * P:(k % 2) * 256 + (b + 1) * P],
                        xs[:, b, :].rearrange("p (c k) -> p k c", k=8)[:, k, :], ident)
            m = T.mark(ins)
            for k in (2 * bank, 2 * bank + 1):
                src = PS[:, bank, (k % 2) * 256:(k % 2) * 256 + 256]
                ma = A.op(A.eng.activation, hi[:, k, :], src, ACT.Copy,
                          scale=1.0 if gain is None else gain[:, k:k + 1], after=(m,), chain=False)
            for k in (2 * bank, 2 * bank + 1):
                src = PS[:, bank, (k % 2) * 256:(k % 2) * 256 + 256]
                mv = V.op(V.eng.scalar_tensor_tensor, lo[:, k, :], src, 1.0 if gain is None else gain[:, k:k + 1],
                          hi[:, k, :].bitcast(F32), ALU.mult, ALU.subtract, after=(ma,), chain=False)
            bank_free[bank] = mv
        return [V.last(), A.last()]

    ss = sm(4)

    def norm(src, xs, after=()):
        for b in range(2):
            A.op(A.eng.activation, xs[:, b, :], src[:, b, :], ACT.Square, accum_out=ss[:, b:b + 1],
                 after=(*after, V.last(), T.last()))
        rstd_of(ss[:, 0:2], 2, D)
        for b in range(2):
            V.op(V.eng.tensor_scalar, xs[:, b, :], src[:, b, :], ss[:, b:b + 1], None, ALU.mult)
        return V.last()

    def pass3(o, l, r, first, last):
        mm(o, l[0], r[0], start=first, stop=False)
        mm(o, l[0], r[1], start=False, stop=False)
        return mm(o, l[1], r[0], start=False, stop=last)

    def tokens_by(w, ht, b, bank, n, after=(), k0=0, k_of=8):
        T.wait(bank_free[bank], *after)
        for k in range(k_of):
            ins = pass3(PS[:, bank, 0:n], [x[:, k0 + k, b * P:(b + 1) * P] for x in ht], [x[:, k, 0:n] for x in w],
                        k0 + k == 0, k0 + k == 7)
        return T.mark(ins)

    def by_k(x, n=512, k=4):
        return x[:, 0:k * n].rearrange("p (k n) -> p k n", k=k)

    def tokens_product(ht, banks, after=()):
        for h in range(2):
            tile, landed = ring.take()
            hi, lo, m, i = halves.split(tile, landed)
            for b in range(2):
                mt = tokens_by((by_k(hi), by_k(lo)), ht, b, banks[b], 512, after=(m, *after), k0=4 * h, k_of=4)
                if h and b == 0:
                    first = mt
            halves.free(i, mt)
            ring.free(mt)
        return first, mt

    def features_product(ht, banks, after=()):
        marks = []
        for h in range(2):
            tile, landed = ring.take()
            hi, lo, m, i = halves.split(tile, landed)
            T.wait(m, *after)
            for c in range(4):
                T.wait(bank_free[banks[c]])
                for k in range(4):
                    ins = pass3(PS[:, banks[c], 0:256], [by_k(x)[:, k, c * P:(c + 1) * P] for x in (hi, lo)],
                                [x[:, 4 * h + k, :] for x in ht], h + k == 0, h == 1 and k == 3)
                mt = T.mark(ins)
                if h:
                    marks.append(mt)
            halves.free(i, mt)
            ring.free(mt)
        return marks

    T.wait(*consts)
    V.wait(*consts)
    A.wait(*consts)
    m = norm(X, Y, after=(l_x.mark(),))
    ht_ready = transposed(Y, g_mix, HT, (m,))

    def project(n_tiles, dst, ready, ht=HT, bank0=4):
        for i in range(n_tiles):
            banks = [bank0 + 2 * (i % 2), bank0 + 2 * (i % 2) + 1]
            m = tokens_product(ht, banks, ready)
            bank_free[banks[0]] = V.op(V.eng.tensor_copy, dst(i, 0), PS[:, banks[0], :], after=(m[0],), chain=False)
            bank_free[banks[1]] = A.op(A.eng.activation, dst(i, 1), PS[:, banks[1], :], ACT.Copy, after=(m[1],),
                                       chain=False)
        return [V.last(), A.last()]

    logf, cum = sm(16), sm(16)
    V.wait(l_s.mark())
    A.wait(l_s.mark())
    T.wait(l_s.mark())
    WS = ACTS[:, 15616:15968]
    WSH, WSL = DS[:, 6144:6496], DS[:, 6528:6880]
    m = A.op(A.eng.activation, fr(WSH), WS, ACT.Copy)
    ws_ready = V.op(V.eng.tensor_tensor, fr(WSL), WS, fr(WSH).bitcast(F32), ALU.subtract, after=(m,))
    WF = [fr(x[:, 0:64]).rearrange("p (k n) -> p k n", k=8) for x in (WSH, WSL)]
    WR = [fr(x[:, 64:352]).rearrange("p (k n) -> p k n", k=8) for x in (WSH, WSL)]
    for b in range(2):
        m = tokens_by(WF, HT, b, 4 + b, n=8, after=(ws_ready, *ht_ready))
        bank_free[4 + b] = V.op(V.eng.tensor_tensor, logf[:, 8 * b:8 * b + 8], PS[:, 4 + b, 0:8], bf, ALU.add, after=(m,))
    t0, t1, t2, t3 = (sm(16) for _ in range(4))

    def log1p_exp_neg_abs(x, n, e, s, s2, q):
        V.op(V.eng.tensor_scalar, e[:, 0:n], x, -1.0, None, ALU.mult)
        V.op(V.eng.tensor_tensor, e[:, 0:n], e[:, 0:n], x, ALU.min)
        A.op(A.eng.activation, e[:, 0:n], e[:, 0:n], ACT.Exp, after=(V.last(),))
        V.op(V.eng.tensor_scalar, s[:, 0:n], e[:, 0:n], 2.0, None, ALU.add, after=(A.last(),))
        V.op(V.eng.reciprocal, s[:, 0:n], s[:, 0:n])
        V.op(V.eng.tensor_tensor, s[:, 0:n], s[:, 0:n], e[:, 0:n], ALU.mult)
        V.op(V.eng.tensor_tensor, s2[:, 0:n], s[:, 0:n], s[:, 0:n], ALU.mult)
        V.op(V.eng.tensor_scalar, q[:, 0:n], s2[:, 0:n], 1.0 / 17, 1.0 / 15, ALU.mult, ALU.add)
        for c in (13, 11, 9, 7, 5, 3, 1):
            V.op(V.eng.tensor_tensor, q[:, 0:n], q[:, 0:n], s2[:, 0:n], ALU.mult)
            V.op(V.eng.tensor_scalar, q[:, 0:n], q[:, 0:n], 1.0 / c, None, ALU.add)
        V.op(V.eng.tensor_tensor, e[:, 0:n], q[:, 0:n], s[:, 0:n], ALU.mult)
        return V.op(V.eng.tensor_scalar, e[:, 0:n], e[:, 0:n], 2.0, None, ALU.mult)

    log1p_exp_neg_abs(logf, 16, t0, t1, t2, t3)
    V.op(V.eng.tensor_scalar, logf, logf, 0.0, None, ALU.min)
    m = V.op(V.eng.tensor_tensor, logf, logf, t0, ALU.subtract)
    T.wait(m, bank_free[6], bank_free[7])
    mm(PS[:, 6, 0:8], tri[:, 0, 0:P], logf[:, 0:8], start=True, stop=True)
    mm(PS[:, 6, 8:16], tri[:, 0, P:256], logf[:, 0:8], start=True, stop=False)
    mm(PS[:, 6, 8:16], tri[:, 1, P:256], logf[:, 8:16], start=False, stop=True)
    for b in range(2):
        ins = mm(PS[0:8, 7, 0:256], logf[:, 8 * b:8 * b + 8], tri[:, b, :], start=(b == 0), stop=(b == 1))
    m = T.mark(ins)
    V.op(V.eng.tensor_copy, cum, PS[:, 6, 0:16], after=(m,))
    ct_ready = V.op(V.eng.tensor_scalar, CT, PS[0:8, 7, 0:256], -1.0, None, ALU.mult)
    bank_free[6] = bank_free[7] = V.last()

    proj_ready = project(6, lambda i, b: PROJ[:, b, 512 * i:512 * i + 512], ht_ready)

    nrm = sm(64).rearrange("p (b j n) -> p b j n", b=2, j=2)
    SQ = DS[:, 0:4096].rearrange("p (b j n d) -> p b j n d", b=2, j=2, d=64)
    V.wait(*proj_ready)
    A.wait(*proj_ready)
    for b in range(2):
        for j in range(2):
            qk = PROJ[:, b, 1536 * j:1536 * j + 1024].rearrange("p (n d) -> p n d", d=64)
            m = A.op(A.eng.activation, SQ[:, b, j], qk, ACT.Square, chain=False)
            V.op(V.eng.tensor_reduce, nrm[:, b, j, :], SQ[:, b, j], AX, ALU.add, after=(m,), chain=False)
    rstd_of(nrm.rearrange("p b j n -> p (b j n)"), 64, 64)
    for b in range(2):
        V.op(V.eng.tensor_scalar, nrm[:, b, :, 0:8], nrm[:, b, :, 0:8], 0.125, None, ALU.mult)
    for b in range(2):
        for j in range(2):
            qk = PROJ[:, b, 1536 * j:1536 * j + 1024].rearrange("p (n d) -> p n d", d=64)
            m = V.op(V.eng.tensor_tensor, qk, qk, nrm[:, b, j, :].rearrange("p (n o) -> p n o", o=1).broadcast_to((P, 16, 64)), ALU.mult)
            if j == 0:
                qk_fox = m
                continue
            q4 = qk.rearrange("p (s n) d -> p s n d", s=2)
            for s in range(2):
                V.op(V.eng.tensor_tensor, q4[:, s], q4[:, s],
                     GDIL[:, s:s + 1, :].broadcast_to((P, 8, 64)), ALU.mult)
            cos = ROPE[:, 0, b:b + 1, :].broadcast_to((P, 16, 32))
            sin = ROPE[:, 1, b:b + 1, :].broadcast_to((P, 16, 32))
            x1, x2 = qk[:, :, 0:32], qk[:, :, 32:64]
            tmp = [DS[:, 4096 + 512 * i:4608 + 512 * i].rearrange("p (n d) -> p n d", d=32) for i in range(4)]
            g0 = G.op(G.eng.tensor_tensor, tmp[0], x1, sin, ALU.mult, after=(V.last(),))
            g1 = G.op(G.eng.tensor_tensor, tmp[1], x2, sin, ALU.mult)
            V.op(V.eng.tensor_tensor, tmp[2], x1, cos, ALU.mult)
            V.op(V.eng.tensor_tensor, tmp[3], x2, cos, ALU.mult)
            V.op(V.eng.tensor_tensor, x1, tmp[2], tmp[1], ALU.subtract, after=(g1,))
            V.op(V.eng.tensor_tensor, x2, tmp[3], tmp[0], ALU.add)
    qk_dil = V.last()
    turn = 0
    qk_ready = []
    for j in range(4):
        off = (0, 512, 1536, 2048)[j]
        for half in range(2):
            bank = turn % 4
            T.wait(bank_free[bank], qk_fox if j < 2 else qk_dil)
            for c in (2 * half, 2 * half + 1):
                for b in range(2):
                    ins = nc.tensor.transpose(PS[:, bank, (c % 2) * 256 + b * P:(c % 2) * 256 + (b + 1) * P],
                                              PROJ[:, b, off + c * P:off + (c + 1) * P], ident)
            m = T.mark(ins)
            dst = QK[:, j, 2 * half:2 * half + 2, :].rearrange("p c t -> p (c t)")
            scale = (gq, gk, None, None)[j]
            if half:
                d = A.op(A.eng.activation, dst, PS[:, bank, :], ACT.Copy,
                         scale=1.0 if scale is None else scale, after=(m,), chain=False)
            elif scale is None:
                d = V.op(V.eng.tensor_copy, dst, PS[:, bank, :], after=(m,), chain=False)
            else:
                d = V.op(V.eng.tensor_scalar, dst, PS[:, bank, :], scale, None, ALU.mult, after=(m,), chain=False)
            bank_free[bank] = d
            qk_ready.append(d)
            turn += 1

    mx, nm, lsum, rl = (sm(8) for _ in range(4))

    def head_slot(h):
        return (h % 2) * 4 + h // 2

    S8 = PS[:, 0:4, :].rearrange("p a (c k) -> p (a c) k", k=256)

    def score_mms(qt, kt, b, K, after):
        T.wait(*[bank_free[i] for i in range(4)], *after)
        for h in range(8):
            o = 64 * (h % 2)
            ins = mm(S8[:, head_slot(h), 0:K], qt[o:o + 64, h // 2, b * P:(b + 1) * P],
                     kt[o:o + 64, h // 2, 0:K], start=True, stop=True)
        return T.mark(ins)

    def head_of(s):
        return 2 * (s % 4) + s // 4

    oss = sm(4).rearrange("p (j b) -> p j b", j=2)
    for j in range(2):
        for b in range(2):
            K = P * (b + 1)
            m = score_mms(QK[:, 2 * j], QK[:, 2 * j + 1], b, K, qk_ready)
            pb = PB[:, :, 0:K]
            if j == 0:
                T.wait(ct_ready, *[bank_free[i] for i in range(4, 8)])
                C8 = PS[:, 4:8, :].rearrange("p a (c k) -> p (a c) k", k=256)
                for s in range(8):
                    ins = mm(C8[:, s, 0:K], SEL[:, head_of(s), :], CT[:, 0:K], start=True, stop=True)
                mc = T.mark(ins)
                d = V.op(V.eng.tensor_tensor, pb, C8[:, :, 0:K], MF[:, b:b + 1, 0:K].broadcast_to((P, 8, K)), ALU.add,
                         after=(mc, T.last()))
                for i in range(4, 8):
                    bank_free[i] = d
                for s in range(8):
                    h = head_of(s)
                    m = V.op(V.eng.scalar_tensor_tensor, pb[:, s, :], S8[:, s, 0:K], cum[:, 8 * b + h:8 * b + h + 1],
                             pb[:, s, :], ALU.add, ALU.add, after=(m, d), chain=False)
            else:
                m = V.op(V.eng.tensor_tensor, pb, S8[:, :, 0:K], MD[:, b:b + 1, 0:K].broadcast_to((P, 8, K)), ALU.add,
                         after=(m, T.last()))
            for i in range(4):
                bank_free[i] = m
            dst = Y[:, b, 512 * j:512 * j + 512].rearrange("p (h i d) -> p i h d", h=4, i=2)
            voff = 1024 + 1536 * j
            V.op(V.eng.tensor_reduce, mx, pb, AX, ALU.max)
            V.op(V.eng.tensor_scalar, nm, mx, -1.0, None, ALU.mult)
            e = []
            for s in range(8):
                e.append(A.op(A.eng.activation, pb[:, s, :], pb[:, s, :], ACT.Exp, bias=nm[:, s:s + 1],
                              accum_out=lsum[:, s:s + 1], after=(V.last(),), chain=False))
            rec = V.op(V.eng.reciprocal, rl, lsum, after=(e[-1],))
            for kb in range(b + 1):
                for g in range(2):
                    bank = 4 + (kb * 2 + g) % 3
                    T.wait(bank_free[bank], e[4 * g + 3])
                    for i in range(4):
                        ins = nc.tensor.transpose(PS[:, bank, i * P:(i + 1) * P],
                                                  pb[:, 4 * g + i, kb * P:(kb + 1) * P], ident)
                    m = T.mark(ins)
                    d = PT[:, kb, 4 * g:4 * g + 4, :].rearrange("p h q -> p (h q)")
                    if g:
                        m = A.op(A.eng.activation, d, PS[:, bank, :], ACT.Copy, after=(m,), chain=False)
                    else:
                        m = V.op(V.eng.tensor_copy, d, PS[:, bank, :], after=(m,), chain=False)
                    bank_free[bank] = m
            T.wait(V.last(), A.last(), bank_free[7])
            for s in range(8):
                h = head_of(s)
                for kb in range(b + 1):
                    ins = mm(PS[:, 7, s * 64:(s + 1) * 64], PT[:, kb, s, :],
                             PROJ[:, kb, voff + 64 * h:voff + 64 * h + 64], start=(kb == 0), stop=(kb == b))
            m = T.mark(ins)
            for i in range(2):
                m2 = V.op(V.eng.tensor_tensor, dst[:, i], PS[:, 7, 256 * i:256 * i + 256].rearrange("p (h d) -> p h d", h=4),
                          rl[:, 4 * i:4 * i + 4].rearrange("p (n o) -> p n o", o=1).broadcast_to((P, 4, 64)),
                          ALU.mult, after=(m, rec))
            bank_free[7] = m2
            A.op(A.eng.activation, DS[:, 0:512], Y[:, b, 512 * j:512 * j + 512], ACT.Square,
                 accum_out=oss[:, j, b:b + 1], after=(m2,))

    def group_norm_out(oss, gain, dst_bank_add):
        rstd_of(oss.rearrange("p j b -> p (j b)"), 4, 512)
        for b in range(2):
            for j in range(2):
                V.op(V.eng.tensor_scalar, Y[:, b, 512 * j:512 * j + 512], Y[:, b, 512 * j:512 * j + 512],
                     oss[:, j, b:b + 1], None, ALU.mult)
        ready = transposed(Y, gain, HT, (V.last(),))
        return add_product(ready)

    def add_product(ready):
        for i in range(2):
            m = tokens_product(HT, [4 + 2 * i, 5 + 2 * i], ready)
            for b in range(2):
                xb = X[:, b, 512 * i:512 * i + 512]
                bank_free[4 + 2 * i + b] = V.op(V.eng.tensor_tensor, xb, xb, PS[:, 4 + 2 * i + b, :], ALU.add,
                                                after=(m[b],), chain=False)
        return V.last()

    group_norm_out(oss, g_out, None)
    if dbg == "h":
        return finish_debug(nc, S, X, V, out)

    m = norm(X, Y)
    ht_ready = transposed(Y, g_ffn, HT, (m,))
    Z = sm(72).rearrange("p (b n) -> p b n", b=2)
    for b in range(2):
        m = tokens_by(WR, HT, b, 4 + b, n=36, after=ht_ready)
        bank_free[4 + b] = V.op(V.eng.tensor_tensor, Z[:, b, :], PS[:, 4 + b, 0:36], br, ALU.add, after=(m,))
    gmx, gsum, ge, goh, gidx = sm(2), sm(2), sm(8), sm(8), sm(2)
    b2 = lambda x: x.rearrange("p (b n) -> p b n", b=2)
    ge, goh = b2(ge), b2(goh)
    col = lambda x, n: x.rearrange("p (b o) -> p b o", o=1).broadcast_to((P, 2, n))
    V.op(V.eng.tensor_reduce, gmx, Z[:, :, 0:4], AX, ALU.max)
    V.op(V.eng.tensor_tensor, ge, Z[:, :, 0:4], col(gmx, 4), ALU.subtract)
    m = A.op(A.eng.activation, ge, ge, ACT.Exp, after=(V.last(),))
    V.op(V.eng.tensor_tensor, goh, Z[:, :, 0:4], col(gmx, 4), ALU.is_equal)
    iota4 = iota[:, 0:4].rearrange("p (o n) -> p o n", o=1).broadcast_to((P, 2, 4))
    V.op(V.eng.scalar_tensor_tensor, goh, goh, -1000.0, iota4, ALU.mult, ALU.add)
    V.op(V.eng.tensor_reduce, gidx, goh, AX, ALU.min)
    V.op(V.eng.tensor_scalar, gidx, gidx, 1000.0, None, ALU.add)
    V.op(V.eng.tensor_tensor, goh, iota4, col(gidx, 4), ALU.is_equal)
    V.op(V.eng.tensor_reduce, gsum, ge, AX, ALU.add, after=(m,))
    V.op(V.eng.reciprocal, gsum, gsum)
    zsel, prod, top8 = b2(sm(16)), DS[:, 4096:4160].rearrange("p (b e g) -> p b e g", b=2, e=8), b2(sm(16))
    for b in range(2):
        V.op(V.eng.tensor_tensor, prod[:, b], Z[:, b, 4:36].rearrange("p (g e) -> p e g", g=4),
             goh[:, b:b + 1, :].broadcast_to((P, 8, 4)), ALU.mult)
    V.op(V.eng.tensor_reduce, zsel.rearrange("p b e -> p (b e)"), prod.rearrange("p b e g -> p (b e) g"), AX, ALU.add)
    ti = nc.alloc_sbuf_tensor("ti", [P, 16], U32)
    tf = b2(sm(16))
    for b in range(2):
        V.op(V.eng.max, top8[:, b, :], zsel[:, b, :])
        V.op(V.eng.max_index, ti[:, 8 * b:8 * b + 8], top8[:, b, :], zsel[:, b, :])
    V.op(V.eng.tensor_copy, tf.rearrange("p b e -> p (b e)"), ti[:, :])
    w1, w2, wt = sm(2), sm(2), sm(2)
    V.op(V.eng.tensor_tensor, w2, top8[:, :, 1], top8[:, :, 0], ALU.subtract)
    A.op(A.eng.activation, w2, w2, ACT.Exp, after=(V.last(),))
    V.op(V.eng.tensor_scalar, wt, w2, 1.0, None, ALU.add, after=(A.last(),))
    V.op(V.eng.reciprocal, wt, wt)
    V.op(V.eng.tensor_tensor, w1, wt, gsum, ALU.mult)
    V.op(V.eng.tensor_tensor, w2, w2, w1, ALU.mult)
    e1, e2 = b2(sm(16)), b2(sm(16))
    iota8 = iota[:, 0:8].rearrange("p (o n) -> p o n", o=1).broadcast_to((P, 2, 8))
    V.op(V.eng.tensor_tensor, e1, iota8, tf[:, :, 0:1].broadcast_to((P, 2, 8)), ALU.is_equal)
    V.op(V.eng.tensor_tensor, e2, iota8, tf[:, :, 1:2].broadcast_to((P, 2, 8)), ALU.is_equal)
    MK, CB, RM = b2(sm(64)), b2(sm(64)), b2(sm(64))
    ee, ew = b2(sm(16)), b2(sm(16))
    V.op(V.eng.tensor_tensor, ee, e1, e2, ALU.add)
    V.op(V.eng.tensor_tensor, e1, e1, col(w1, 8), ALU.mult)
    V.op(V.eng.tensor_tensor, e2, e2, col(w2, 8), ALU.mult)
    V.op(V.eng.tensor_tensor, ew, e1, e2, ALU.add)
    for b in range(2):
        g4 = goh[:, b, :].rearrange("p (g o) -> p g o", o=1).broadcast_to((P, 4, 8))
        for dst, src in ((MK, ee), (CB, ew)):
            V.op(V.eng.tensor_tensor, dst[:, b, :].rearrange("p (g e) -> p g e", g=4), g4,
                 src[:, b:b + 1, :].broadcast_to((P, 4, 8)), ALU.mult)
    T.wait(V.last(), bank_free[6])
    mm(PS[:, 6, 0:32], tri[:, 0, 0:P], MK[:, 0, :], start=True, stop=True)
    mm(PS[:, 6, 32:64], tri[:, 0, P:256], MK[:, 0, :], start=True, stop=False)
    m = T.mark(mm(PS[:, 6, 32:64], tri[:, 1, P:256], MK[:, 1, :], start=False, stop=True))
    V.op(V.eng.tensor_tensor, RM.rearrange("p b e -> p (b e)"), MK.rearrange("p b e -> p (b e)"), PS[:, 6, 0:64],
         ALU.mult, after=(m,))
    bank_free[6] = V.last()
    OV, ovn = b2(sm(64)), sm(1)
    V.op(V.eng.tensor_scalar, OV.rearrange("p b e -> p (b e)"), RM.rearrange("p b e -> p (b e)"), float(CAP) + 0.5, None, ALU.is_gt)
    V.op(V.eng.tensor_reduce, ovn, OV.rearrange("p b e -> p (b e)"), AX, ALU.add)
    V.op(V.eng.tensor_tensor, OV.rearrange("p b e -> p (b e)"), OV.rearrange("p b e -> p (b e)"),
         CB.rearrange("p b e -> p (b e)"), ALU.mult)
    T.wait(V.last(), bank_free[7])
    m = T.mark(mm(PS[0:1, 7, 0:1], ovn, tri[:, 0, 127:128], start=True, stop=True))
    flag = nc.alloc_sbuf_tensor("flag", [1, 1], I32)
    flag_ready = V.op(V.eng.tensor_copy, flag[:, :], PS[0:1, 7, 0:1], after=(m,))
    bank_free[7] = flag_ready

    XSH = ACTS[:, 14336:16384].rearrange("p (b n) -> p b n", b=2)
    for b in range(2):
        m = A.op(A.eng.activation, fr(XSH[:, b, :]), Y[:, b, :], ACT.Copy, after=(V.last(), T.last()))
        xs_ready = V.op(V.eng.tensor_tensor, fr(Y[:, b, :]), Y[:, b, :], fr(XSH[:, b, :]).bitcast(F32), ALU.subtract, after=(m,))
    two = lambda o, n: [ACTS[:, o + n * i:o + n * i + n] for i in range(2)]
    XGS = [x.rearrange("p (g k s) -> p g k s", g=4, k=8) for x in two(0, 4096)]
    SDS = [x.rearrange("p (b e s) -> p b e s", b=2, e=8) for x in two(8192, 1024)]
    DWS = [x.rearrange("p (b e s) -> p b e s", b=2, e=8) for x in two(10240, 1024)]
    SCS = [x.rearrange("p (g t) -> p g t", g=4) for x in two(12288, 1024)]
    iota_s = iota[:, 1:1 + CAP].rearrange("p (o s) -> p o s", o=1).broadcast_to((P, 8, CAP))
    moe_marks = {}

    def slots_of(q):
        sd, dw = SDS[q % 2], DWS[q % 2]
        wide = lambda x, b: x[:, b, 8 * q:8 * q + 8].rearrange("p (e o) -> p e o", o=1).broadcast_to((P, 8, CAP))
        for b in range(2):
            V.op(V.eng.tensor_tensor, fr(sd[:, b]), iota_s, wide(RM, b), ALU.is_equal,
                 after=(moe_marks.get(("gathered", q - 2)),))
        for b in range(2):
            V.op(V.eng.tensor_tensor, dw[:, b], fr(sd[:, b]).bitcast(F32), wide(CB, b), ALU.mult, after=(moe_marks.get(("turned", q - 2)),))
        return V.last()

    def gather(q, ready):
        sd, dw, xg = SDS[q % 2], DWS[q % 2], XGS[q % 2]
        for k in range(8):
            bank = 6 + k % 2
            T.wait(bank_free[bank], ready, xs_ready)
            for b in range(2):
                r = fr(sd[:, b].rearrange("p e s -> p (e s)"))
                for i, x in enumerate((XSH, Y)):
                    ins = mm(PS[:, bank, :], fr(x[:, b, :].rearrange("p (c k) -> p k c", k=8)[:, k, :]), r,
                             start=(b + i == 0), stop=(b + i == 2))
            mt = T.mark(ins)
            src = PS[:, bank, :].rearrange("p (g s) -> p g s", g=4)
            done = (moe_marks.get(("pairs", q - 2)),)
            if k % 2:
                d = A.op(A.eng.activation, xg[:, :, k, :], src, ACT.Copy, scale=g_ffn[:, k:k + 1],
                         after=(mt, *done), chain=False)
            else:
                d = V.op(V.eng.tensor_scalar, xg[:, :, k, :], src, g_ffn[:, k:k + 1], None, ALU.mult,
                         after=(mt, *done), chain=False)
            bank_free[bank] = d
        moe_marks[("gathered", q)] = mt
        for c in range(2):
            bank = 6 + c
            T.wait(bank_free[bank])
            for g in (2 * c, 2 * c + 1):
                for b in range(2):
                    ins = nc.tensor.transpose(PS[:, bank, (g % 2) * 256 + b * P:(g % 2) * 256 + (b + 1) * P],
                                              dw[:, b, 2 * g:2 * g + 2, :].rearrange("p e s -> p (e s)"), ident)
            mt = T.mark(ins)
            dst = SCS[q % 2][:, 2 * c:2 * c + 2, :].rearrange("p g t -> p (g t)")
            done = (moe_marks.get(("scattered", q - 2)),)
            if c:
                d = A.op(A.eng.activation, dst, PS[:, bank, :], ACT.Copy, after=(mt, *done), chain=False)
            else:
                d = V.op(V.eng.tensor_copy, dst, PS[:, bank, :], after=(mt, *done), chain=False)
            bank_free[bank] = d
        moe_marks[("turned", q)] = mt
        return [V.last(), A.last()]

    HB = [DS[:, 0:512], DS[:, 512:1024]]
    HTB = DS[:, 1024:1536].rearrange("p (c s) -> p c s", c=4)
    YG = [DS[:, 2048:3072], DS[:, 3072:4096]]
    y_last = [None, None]
    yg_ready = None

    def scatter(g, ready):
        T.wait(ready, *[bank_free[i] for i in range(4)])
        sc = SCS[(g // 4) % 2]
        for b in range(2):
            for half in range(2):
                ins = mm(PS[:, 2 * b + half, :], sc[:, g % 4, b * P:(b + 1) * P],
                         YG[g % 2][:, 512 * half:512 * half + 512],
                         start=(g == 0), stop=(g == 15), skip_group_check=True)
        m = T.mark(ins)
        if g % 4 == 3:
            moe_marks[("scattered", g // 4)] = m
        return m

    def pair_product(lhs, banks_of, view, k_of):
        for h in range(2):
            (t0_, l0), (t1_, l1) = ring.take(), ring.take()
            T.wait(l0, l1)
            for k in range(k_of // 2):
                for bank, c0 in banks_of:
                    for i, t in enumerate((t0_, t1_)):
                        ins = mm(PS[64 * i:64 * i + 64, bank, :], lhs(h * k_of // 2 + k, i), view(t)[:, k, c0:c0 + 512],
                                 start=(h + k == 0), stop=(h == 1 and k == k_of // 2 - 1), skip_group_check=True)
            m = T.mark(ins)
            ring.free(m)
            ring.free(m)
        return m

    xg_ready = gather(0, slots_of(0))
    for g in range(16):
        xg = XGS[(g // 4) % 2]
        hb = HB[g % 2]
        T.wait(*xg_ready)
        T.wait(bank_free[4])
        lhs = lambda k, i: xg[:, g % 4, k, 64 * i:64 * i + 64]
        m4 = pair_product(lhs, [(4, 0)], by_k, 8)
        T.wait(bank_free[5])
        m = pair_product(lhs, [(5, 0)], by_k, 8)
        if g % 4 == 3:
            moe_marks[("pairs", g // 4)] = m
        mh = A.op(A.eng.activation, hb, PS[:, 4, :], ACT.Silu, after=(m4, T.last() if g < 2 else None))
        mh = V.op(V.eng.tensor_tensor, hb, hb, PS[:, 5, :], ALU.mult, after=(mh, m))
        bank_free[5] = mh
        if g:
            y_last[(g - 1) % 2] = scatter(g - 1, yg_ready)
        if g % 4 == 1 and g < 12:
            sd_ready = slots_of(g // 4 + 1)
        T.wait(mh)
        for c in range(4):
            ins = nc.tensor.transpose(PS[:, 4, c * P:(c + 1) * P],
                                      hb.rearrange("p (f c) -> p c f", c=4)[:, c, :], ident)
        m = T.mark(ins)
        m = V.op(V.eng.tensor_copy, HTB.rearrange("p c s -> p (c s)"), PS[:, 4, :], after=(m,))
        bank_free[4] = m
        T.wait(m, bank_free[6], bank_free[7])
        md = pair_product(lambda c, i: HTB[:, c, 64 * i:64 * i + 64], [(6, 0), (7, 512)],
                          lambda t: by_k(t, 1024, 2), 4)
        yg = YG[g % 2]
        d0 = V.op(V.eng.tensor_copy, yg[:, 0:512], PS[:, 6, :], after=(md, y_last[g % 2]))
        d1 = A.op(A.eng.activation, yg[:, 512:1024], PS[:, 7, :], ACT.Copy, after=(md, y_last[g % 2]))
        bank_free[6], bank_free[7] = d0, d1
        yg_ready = [d0, d1]
        if g % 4 == 1 and g < 12:
            xg_ready = gather(g // 4 + 1, sd_ready)
    m = scatter(15, yg_ready)
    for b in range(2):
        for half in range(2):
            xb = X[:, b, 512 * half:512 * half + 512]
            bank_free[2 * b + half] = V.op(V.eng.tensor_tensor, xb, xb, PS[:, 2 * b + half, :], ALU.add, after=(m,),
                                           chain=False)

    for lane in (G, S):
        lane.wait(flag_ready)
    overflow(nc, a, (V, A, T), flag, flag_ready, X, HT, OV, ACTS, PS)
    joined = V.op(V.eng.tensor_scalar, ss[:, 0:2], ss[:, 0:2], 1.0, None, ALU.mult)
    for lane in (A, T, G, S):
        lane.wait(joined)
    for i in range(8):
        bank_free[i] = None
    if dbg == "h2":
        return finish_debug(nc, S, X, V, out)

    R = lambda i: ACTS[:, 1024 * i:1024 * i + 1024].rearrange("p (c t) -> p c t", c=4)
    XR, XC, GT, RR, II, AA, BB, HS, QT, KT = (R(i) for i in range(10))
    VT = ACTS[:, 10240:11264].rearrange("p (b n) -> p b n", b=2)
    PB2 = ACTS[:, 11264:13312].rearrange("p (h k) -> p h k", h=8)
    PT2 = ACTS[:, 13312:15360].rearrange("p (b h q) -> p b h q", b=2, h=8)
    GW = ACTS[:, 15360:15872].rearrange("p (s c j) -> p s c j", s=2, c=4)
    l_g = Load(nc, "l_g")
    l_g.start(A, GW[:, 0], a["gate_a_w_2"])
    l_g.start(A, GW[:, 1], a["gate_x_w_2"])
    m = norm(X, Y)
    ht_ready = transposed(Y, g_mix2, HT, (m,))
    fm_ready = []
    turn = 0
    for i, dst in enumerate((XR, GT, QT, KT)):
        banks = [4 * (i % 2) + c for c in range(4)]
        ms = features_product(HT, banks, ht_ready)
        for c, m in enumerate(ms):
            src = PS[:, banks[c], 0:256]
            if i == 1:
                e = A.op(A.eng.activation, dst[:, c, :], src, ACT.Gelu_apprx_tanh, after=(m,), chain=False)
            elif i == 2:
                e = V.op(V.eng.tensor_scalar, dst[:, c, :], src, 0.125, None, ALU.mult, after=(m,), chain=False)
            else:
                e = V.op(V.eng.tensor_copy, dst[:, c, :], src, after=(m,), chain=False)
            bank_free[banks[c]] = e
    fm_ready = [V.last(), A.last()]
    biases = [ring.take(), ring.take()]
    hold = ring.hold(2)
    project(1, lambda i, b: VT[:, b, :], ())
    v_ready = [V.last(), A.last()]

    oss2 = sm(4).rearrange("p (j b) -> p j b", j=2)
    for b in range(2):
        K = P * (b + 1)
        m = score_mms(QT, KT, b, K, fm_ready)
        pb = PB2[:, :, 0:K]
        btile, bias_landed = biases[b]
        bias = btile[:, 0:8 * K].rearrange("p (s k) -> p s k", s=8)
        m = V.op(V.eng.tensor_tensor, pb, S8[:, :, 0:K], bias, ALU.add, after=(m, bias_landed))
        ring.free_held(hold[b], m)
        for i in range(4):
            bank_free[i] = m
        V.op(V.eng.tensor_reduce, mx, pb, AX, ALU.max)
        V.op(V.eng.tensor_scalar, nm, mx, -1.0, None, ALU.mult)
        e = []
        for s in range(8):
            e.append(A.op(A.eng.activation, pb[:, s, :], pb[:, s, :], ACT.Exp, bias=nm[:, s:s + 1],
                          accum_out=lsum[:, s:s + 1], after=(V.last(),), chain=False))
        rec = V.op(V.eng.reciprocal, rl, lsum, after=(e[-1],))
        for kb in range(b + 1):
            for g in range(2):
                bank = 4 + (kb * 2 + g) % 3
                T.wait(bank_free[bank], e[4 * g + 3])
                for i in range(4):
                    ins = nc.tensor.transpose(PS[:, bank, i * P:(i + 1) * P],
                                              pb[:, 4 * g + i, kb * P:(kb + 1) * P], ident)
                m = T.mark(ins)
                d = PT2[:, kb, 4 * g:4 * g + 4, :].rearrange("p h q -> p (h q)")
                if g:
                    m = A.op(A.eng.activation, d, PS[:, bank, :], ACT.Copy, after=(m,), chain=False)
                else:
                    m = V.op(V.eng.tensor_copy, d, PS[:, bank, :], after=(m,), chain=False)
                bank_free[bank] = m
        T.wait(V.last(), A.last(), *v_ready, bank_free[7])
        for s in range(8):
            h = head_of(s)
            for kb in range(b + 1):
                ins = mm(PS[:, 7, s * 64:(s + 1) * 64], PT2[:, kb, s, :],
                         VT[:, kb, 64 * h:64 * h + 64], start=(kb == 0), stop=(kb == b))
        m = T.mark(ins)
        dst = Y[:, b, 512:1024].rearrange("p (h i d) -> p i h d", h=4, i=2)
        for i in range(2):
            m2 = V.op(V.eng.tensor_tensor, dst[:, i], PS[:, 7, 256 * i:256 * i + 256].rearrange("p (h d) -> p h d", h=4),
                      rl[:, 4 * i:4 * i + 4].rearrange("p (n o) -> p n o", o=1).broadcast_to((P, 4, 64)),
                      ALU.mult, after=(m, rec))
        bank_free[7] = m2
        A.op(A.eng.activation, DS[:, 0:512], Y[:, b, 512:1024], ACT.Square, accum_out=oss2[:, 1, b:b + 1], after=(m2,))
    sp, u0, u1, u2 = (sm(4) for _ in range(4))
    log1p_exp_neg_abs(lam, 4, sp, u0, u1, u2)
    V.op(V.eng.tensor_scalar, u0, lam, -1.0, 0.0, ALU.mult, ALU.max)
    V.op(V.eng.tensor_tensor, sp, sp, u0, ALU.add)
    V.op(V.eng.tensor_scalar, sp, sp, 4.0, None, ALU.mult)
    for c in range(4):
        V.op(V.eng.tensor_scalar, XC[:, c, :], XR[:, c, :], cw[:, c, 3:4], cb[:, c:c + 1], ALU.mult, ALU.add)
        for w in (2, 1, 0):
            s = 3 - w
            V.op(V.eng.scalar_tensor_tensor, XC[:, c, s:256], XR[:, c, 0:256 - s], cw[:, c, w:w + 1], XC[:, c, s:256],
                 ALU.mult, ALU.add)
    m = V.last()
    for s, (dst, bias) in enumerate(((RR, gab), (II, gxb))):
        for c in range(4):
            bank = 4 * s + c
            T.wait(m, bank_free[bank], l_g.mark())
            for o in (0, 64):
                ins = mm(PS[o:o + 64, bank, 0:256], GW[o:o + 64, s, c, :],
                         XC[o:o + 64, c, :], start=True, stop=True, skip_group_check=True)
            mt = T.mark(ins)
            d = A.op(A.eng.activation, dst[:, c, :], PS[:, bank, 0:256], ACT.Sigmoid,
                     bias=bias[:, c:c + 1], after=(mt,), chain=False)
            bank_free[bank] = d
    for c in range(4):
        A.op(A.eng.activation, RR[:, c, :], RR[:, c, :], ACT.Tanh, scale=sp[:, c:c + 1], after=(V.last(),))
    rf, aaf, bbf = (x.rearrange("p c t -> p (c t)") for x in (RR, AA, BB))
    V.op(V.eng.tensor_scalar, bbf, rf, 1.3e-35, None, ALU.max, after=(A.last(),))
    ms = A.op(A.eng.activation, bbf, bbf, ACT.Sqrt, after=(V.last(),))
    hhf, xcf, iif = (x.rearrange("p c t -> p (c t)") for x in (HS, XC, II))
    V.op(V.eng.tensor_scalar, hhf, rf, 1.0, None, ALU.add)
    V.op(V.eng.reciprocal, hhf, hhf)
    V.op(V.eng.tensor_scalar, aaf, rf, -1.0, 1.0, ALU.mult, ALU.add)
    V.op(V.eng.tensor_tensor, aaf, aaf, hhf, ALU.mult)
    V.op(V.eng.tensor_tensor, xcf, xcf, iif, ALU.mult)
    V.op(V.eng.scalar_tensor_tensor, xcf, xcf, 2.0, hhf, ALU.mult, ALU.mult)
    V.op(V.eng.tensor_tensor, bbf, bbf, xcf, ALU.mult, after=(ms,))
    for c in range(4):
        V.op(V.eng.tensor_tensor_scan, HS[:, c, :], AA[:, c, :], BB[:, c, :], 0.0, ALU.mult, ALU.add)
    m = V.op(V.eng.tensor_tensor, hhf, hhf, GT.rearrange("p c t -> p (c t)"), ALU.mult)
    for b in range(2):
        T.wait(m, bank_free[4 + b])
        for c in range(4):
            ins = nc.tensor.transpose(PS[:, 4 + b, c * P:(c + 1) * P], HS[:, c, b * P:(b + 1) * P], ident)
        mt = T.mark(ins)
        d = V.op(V.eng.tensor_copy, Y[:, b, 0:512], PS[:, 4 + b, :], after=(mt,))
        bank_free[4 + b] = d
        A.op(A.eng.activation, DS[:, 0:512], Y[:, b, 0:512], ACT.Square, accum_out=oss2[:, 0, b:b + 1], after=(d,))
    group_norm_out(oss2, g_grp, None)
    if dbg == "x1":
        return finish_debug(nc, S, X, V, out)

    MEM = DS[:, 0:2048].rearrange("p (b n) -> p b n", b=2)
    MT = [fr(ACTS[:, o:o + 2048]).rearrange("p (k t) -> p k t", k=8) for o in (0, 10240)]
    KM = ACTS[:, 2048:4096].rearrange("p (c t) -> p c t", c=8)
    VM = ACTS[:, 4096:6144].rearrange("p (b n) -> p b n", b=2)
    QM = ACTS[:, 6144:8192].rearrange("p (c t) -> p c t", c=8)
    PM = ACTS[:, 8192:9216].rearrange("p (h k) -> p h k", h=4)
    PTM = ACTS[:, 9216:10240].rearrange("p (b h q) -> p b h q", b=2, h=4)
    l_m = Load(nc, "l_m")
    for b in range(2):
        l_m.start(A, MEM[:, b, :], a["mem_2"][0, b * P:(b + 1) * P, :], after=(A.last(), V.last(), T.last()))
    m = norm(MEM, Y, after=(l_m.mark(),))
    mt_ready = transposed(Y, g_mem, MT, (m,))
    def features_to(ht, dst, n, scale, after):
        for i in range(n):
            banks = [4 * (i % 2) + c for c in range(4)]
            for c, m in enumerate(features_product(ht, banks, after)):
                bank_free[banks[c]] = V.op(V.eng.tensor_scalar, dst[:, 4 * i + c, :], PS[:, banks[c], 0:256], scale,
                                           None, ALU.mult, after=(m,), chain=False)

    features_to(MT, KM, 2, 1.0, mt_ready)
    project(2, lambda i, b: VM[:, b, 512 * i:512 * i + 512], (), ht=MT)
    m = norm(X, Y)
    ht_ready = transposed(Y, g_cross, HT, (m,))
    features_to(HT, QM, 2, 1.0 / 16, ht_ready)
    q_ready = [V.last(), A.last()]
    S4 = PS[:, 0:2, :].rearrange("p a (c k) -> p (a c) k", k=256)
    for b in range(2):
        T.wait(*q_ready, bank_free[0], bank_free[1])
        for h in range(4):
            for c in range(2):
                ins = mm(S4[:, h, :], QM[:, 2 * h + c, b * P:(b + 1) * P], KM[:, 2 * h + c, :],
                         start=(c == 0), stop=(c == 1))
        m = T.mark(ins)
        V.op(V.eng.tensor_reduce, mx[:, 0:4], S4, AX, ALU.max, after=(m, A.last()))
        V.op(V.eng.tensor_scalar, nm[:, 0:4], mx[:, 0:4], -1.0, None, ALU.mult)
        for h in range(4):
            e = A.op(A.eng.activation, PM[:, h, :], S4[:, h, :], ACT.Exp, bias=nm[:, h:h + 1],
                     accum_out=lsum[:, h:h + 1], after=(V.last(), T.last()), chain=False)
        bank_free[0] = bank_free[1] = e
        rec = V.op(V.eng.reciprocal, rl[:, 0:4], lsum[:, 0:4], after=(e,))
        for kb in range(2):
            T.wait(bank_free[4 + kb], e)
            for h in range(4):
                ins = nc.tensor.transpose(PS[:, 4 + kb, h * P:(h + 1) * P], PM[:, h, kb * P:(kb + 1) * P], ident)
            mt = T.mark(ins)
            bank_free[4 + kb] = V.op(V.eng.tensor_copy, PTM[:, kb].rearrange("p h q -> p (h q)"), PS[:, 4 + kb, :],
                                     after=(mt,), chain=False)
        T.wait(V.last(), bank_free[6], bank_free[7])
        for h in range(4):
            for kb in range(2):
                ins = mm(PS[:, 6 + h // 2, (h % 2) * 256:(h % 2) * 256 + 256], PTM[:, kb, h, :],
                         VM[:, kb, 256 * h:256 * h + 256], start=(kb == 0), stop=(kb == 1))
        m = T.mark(ins)
        for i in range(2):
            d = V.op(V.eng.tensor_tensor, Y[:, b, 512 * i:512 * i + 512].rearrange("p (h d) -> p h d", h=2),
                     PS[:, 6 + i, :].rearrange("p (h d) -> p h d", h=2),
                     rl[:, 2 * i:2 * i + 2].rearrange("p (n o) -> p n o", o=1).broadcast_to((P, 2, 256)), ALU.mult,
                     after=(m, rec))
            bank_free[6 + i] = d
    ready = transposed(Y, None, HT, (V.last(),))
    add_product(ready)
    if dbg == "x2":
        return finish_debug(nc, S, X, V, out)

    m = norm(X, Y)
    ht_ready = transposed(Y, g_ffn2, HT, (m,))
    QP = DS[:, 0:4096].rearrange("p (j t) -> p j t", j=16)
    SC = DS[:, 4096:8192].rearrange("p (b j n) -> p b j n", b=2, j=16)
    features_to(HT, QP, 4, 1.0, ht_ready)
    tile, landed = ring.take()
    SK = tile[:, 0:2048].rearrange("p (j n) -> p j n", j=16)
    q_ready = V.last()
    for b in range(2):
        for q in range(4):
            bank = 4 * b + q
            T.wait(bank_free[bank], q_ready, landed)
            for j in range(4 * q, 4 * q + 4):
                ins = mm(PS[:, bank, (j % 4) * P:(j % 4 + 1) * P], QP[:, j, b * P:(b + 1) * P], SK[:, j, :],
                         start=True, stop=True)
            m = T.mark(ins)
            bank_free[bank] = A.op(A.eng.activation, SC[:, b, 4 * q:4 * q + 4, :].rearrange("p j n -> p (j n)"),
                                   PS[:, bank, :], ACT.Copy, after=(m,), chain=False)
    ring.free(m)
    sc_ready = A.last()

    xkeep = nc.dram_tensor("xkeep", (P, 2 * D), F32, kind="Internal").ap()
    xf = X[:, :, :].rearrange("p b n -> p (b n)")
    l_k = Load(nc, "l_k")
    x_kept = l_k.start(A, xkeep, xf, after=(V.last(),))
    halves.bufs.append(xf)
    halves.used.append(x_kept)
    halves.n = len(halves.bufs) - 1

    W = BIG[:, :].rearrange("p (n t) -> p n t", n=128)
    keys = (tig[:, 0:256], tig[:, 256:512], tig[:, 512:768])
    steps = routing(nc, V, A, T, SC, DS, Y, iota, ident, keys, PS, bank_free, sm, sc_ready)
    going = True

    def split_next():
        tile, landed = ring.take()
        return halves.split(tile, landed)

    cur = split_next()
    for i in range(64):
        nxt = split_next() if i < 63 else None
        for _ in range(8):
            if going:
                going = next(steps, "end") != "end"
        assert i < 48 or not going
        hi, lo, ready, buf = cur
        bank = 4 + i % 2
        T.wait(ready, *ht_ready, bank_free[bank])
        for j in range(2):
            for k in range(8):
                at = 1024 * j + 128 * k
                ins = pass3(PS[:, bank, 256 * j:256 * j + 256], [x[:, at:at + P] for x in (hi, lo)],
                            [x[:, k, :] for x in HT], k == 0, k == 7)
        m = T.mark(ins)
        halves.free(buf, m)
        ring.free(m)
        bank_free[bank] = A.op(A.eng.activation, W[:, 2 * i:2 * i + 2, :].rearrange("p n t -> p (n t)"), PS[:, bank, :],
                               ACT.Gelu_apprx_tanh, after=(m, V.last() if i == 48 else None), chain=False)
        cur = nxt
    act_ready, u_done, routed = A.last(), T.last(), V.last()

    cur = split_next()
    I1T, I2T, GTT = keys
    EB = [x[:, :, :].rearrange("p k t -> p (k t)") for x in (HH, HL)]
    E1 = [EB[i // 2][:, 1024 * (i % 2):1024 * (i % 2) + 512] for i in range(4)]
    E2 = [EB[i // 2][:, 1024 * (i % 2) + 512:1024 * (i % 2) + 1024] for i in range(4)]
    used = [u_done] * 4

    def weigh(q, ready):
        bank = 4 + q % 4
        w = W[:, :, 4 * q:4 * q + 4]
        bank_free[bank] = V.op(V.eng.tensor_tensor, w, PS[:, bank, :].rearrange("p (t n) -> p n t", t=4), w, ALU.mult,
                               after=(ready, act_ready), chain=False)

    ready = []
    G.wait(routed)
    for q in range(64):
        i, bank = q % 4, 4 + q % 4
        for t in range(4):
            tt = 4 * q + t
            lane = G if t == 3 else V
            g = lane.op(lane.eng.tensor_scalar, E1[i][:, t * P:(t + 1) * P], iota, I1T[:, tt:tt + 1], None,
                        ALU.is_equal, after=(used[i],), chain=False)
        for t in range(4):
            tt = 4 * q + t
            v = V.op(V.eng.tensor_scalar, E2[i][:, t * P:(t + 1) * P], iota, I2T[:, tt:tt + 1],
                     GTT[:, tt:tt + 1], ALU.is_equal, ALU.mult, after=(used[i],), chain=False)
        T.wait(g, v, bank_free[bank])
        for t in range(4):
            ins = mm(PS[:, bank, t * P:(t + 1) * P], E1[i][:, t * P:(t + 1) * P], E2[i][:, t * P:(t + 1) * P],
                     start=True, stop=True)
        used[i] = T.mark(ins)
        ready.append(used[i])
        if q:
            weigh(q - 1, ready[q - 1])
    weigh(63, ready[63])
    w_ready = V.last()

    yflat = Y[:, :, :].rearrange("p b n -> p (b n)")
    WH = [yflat[:, 512 * i:512 * i + 512] for i in range(3)]
    wh_used = [None] * 3

    def split_w(i):
        w = W[:, 2 * i:2 * i + 2, :].rearrange("p n t -> p (n t)")
        h = WH[i % 3]
        ma = A.op(A.eng.activation, fr(h), w, ACT.Copy, after=(w_ready, wh_used[i % 3]), chain=False)
        mv = V.op(V.eng.tensor_tensor, fr(w), w, fr(h).bitcast(F32), ALU.subtract, after=(ma,), chain=False)
        return [fr(x).rearrange("p (n t) -> p n t", n=2) for x in (h, w)], mv

    wcur = split_w(0)
    for i in range(64):
        if i < 63:
            nxt, wnxt = split_next(), split_w(i + 1)
        hi, lo, r1, buf = cur
        w, r2 = wcur
        T.wait(r1, r2, *[bank_free[q] for q in range(4)])
        for j in range(2):
            for b in range(2):
                for half in range(2):
                    at = 1024 * j + 512 * half
                    o = PS[:, 2 * b + half, :]
                    l = [x[:, j, b * P:(b + 1) * P] for x in w]
                    r = [x[:, at:at + 512] for x in (hi, lo)]
                    mm(o, l[0], r[0], start=(i + j == 0), stop=False, skip_group_check=True)
                    mm(o, l[0], r[1], start=False, stop=False, skip_group_check=True)
                    ins = mm(o, l[1], r[0], start=False, stop=(i == 63 and j == 1), skip_group_check=True)
        m = T.mark(ins)
        halves.free(buf, m)
        wh_used[i % 3] = m
        ring.free(m)
        cur, wcur = nxt, wnxt
    gf = BIG[:, 0:1024]
    l_f = Load(nc, "l_f")
    l_f.start(A, gf, a["norm_final_2"].rearrange("(o n) -> o n", o=1).broadcast_to((P, D)), after=(m, V.last()))
    x_back = l_k.start(A, xf, xkeep, after=(m, x_kept))
    for b in range(2):
        for half in range(2):
            xb = X[:, b, 512 * half:512 * half + 512]
            V.op(V.eng.tensor_tensor, xb, xb, PS[:, 2 * b + half, :], ALU.add, after=(m, x_back), chain=False)
    norm(X, Y)
    for b in range(2):
        V.op(V.eng.tensor_tensor, Y[:, b, :], Y[:, b, :], gf, ALU.mult, after=(l_f.mark(),))
    l_o = Load(nc, "l_o")
    for b in range(2):
        l_o.start(S, out[0, b * P:(b + 1) * P, :], Y[:, b, :], after=(V.last(),))
    S.wait(l_o.mark())


def finish_debug(nc, S, X, V, out):
    l_o = Load(nc, "l_o")
    for b in range(2):
        l_o.start(S, out[0, b * P:(b + 1) * P, :], X[:, b, :], after=(V.last(),))
    S.wait(l_o.mark())


def overflow(nc, a, lanes, flag, flag_ready, X, HT, OV, ACTS, PS):
    mains = lanes
    for lane in mains:
        lane.wait(flag_ready, *[o.last() for o in mains])
    V, A, T = (Lane(nc, o.eng, f"{o.name}_ov") for o in mains)
    WG, WU, WD = (ACTS[:, 4096 * i:4096 * i + 4096] for i in range(3))
    wg, wu = (w.rearrange("p (k n) -> p k n", k=8) for w in (WG, WU))
    wd = WD.rearrange("p (c n) -> p c n", c=4)
    HU = ACTS[:, 12288:13312].rearrange("p (c t) -> p c t", c=4)
    parts = [x.bitcast(F32).rearrange("p k t -> p (k t)") for x in HT]
    HF = ACTS[:, 13312:15360]
    HT = HF.rearrange("p (k t) -> p k t", k=8)
    l_w = Load(nc, "l_ov")

    per_t, per_a, per_v = 4 * 2 + 2, 4, 4 + 4

    def t_mark(e, i):
        return (T.sem, per_t * e + i + 1)

    def a_mark(e, i):
        return (A.sem, per_a * e + i + 1)

    def v_mark(e, i):
        return (V.sem, per_v * e + i + 2)

    def body_tensor():
        for e in range(32):
            T.wait((l_w.sem, 48 * (e + 1)), (V.sem, 1))
            for c in range(4):
                for s, w in enumerate((wg, wu)):
                    bank = 2 * (c % 2) + s
                    if c >= 2:
                        T.wait(v_mark(e, c - 2))
                    elif e:
                        T.wait(v_mark(e - 1, 2 + c))
                    for k in range(8):
                        ins = nc.tensor.matmul(
                            PS[:, bank, 0:256],
                            w.rearrange("p k (f c) -> p k c f", c=4)[:, k, c, :], HT[:, k, :],
                            start=(k == 0), stop=(k == 7))
                    T.mark(ins)
            T.wait(v_mark(e, 3))
            if e:
                T.wait(v_mark(e - 1, 7))
            for b in range(2):
                for half in range(2):
                    for c in range(4):
                        ins = nc.tensor.matmul(PS[:, 4 + 2 * b + half, :], HU[:, c, b * P:(b + 1) * P],
                                               wd[:, c, 512 * half:512 * half + 512], start=(c == 0), stop=(c == 3))
                T.mark(ins)

    def body_scalar():
        for e in range(32):
            if e:
                A.wait(t_mark(e - 1, 9))
            for dst, n, k in ((WG, "w_gate", 8), (WU, "w_up", 8), (WD, "w_down", 4)):
                l_w.start(A, dst, a[n][0, e].rearrange("(p k) n -> p (k n)", k=k))
            for c in range(4):
                A.wait(t_mark(e, 2 * c))
                A.mark(nc.scalar.activation(HU[:, c, :], PS[:, 2 * (c % 2), 0:256], ACT.Silu))

    def body_vector():
        V.mark(nc.vector.tensor_tensor(HF, parts[0], parts[1], ALU.add))
        for e in range(32):
            for c in range(4):
                V.wait(a_mark(e, c), t_mark(e, 2 * c + 1))
                V.mark(nc.vector.tensor_tensor(HU[:, c, :], HU[:, c, :], PS[:, 2 * (c % 2) + 1, 0:256], ALU.mult))
            for b in range(2):
                V.wait(t_mark(e, 8 + b))
                if e:
                    V.wait(v_mark(e - 1, 4 + 2 * b + 1))
                for half in range(2):
                    xb = X[:, b, 512 * half:512 * half + 512]
                    V.mark(nc.vector.scalar_tensor_tensor(xb, PS[:, 4 + 2 * b + half, :], OV[:, b, e:e + 1], xb,
                                                          ALU.mult, ALU.add))
        V.wait(V.last(), (A.sem, per_a * 32), (T.sem, per_t * 32))

    value = nc.values_load(flag[0:1, 0:1], min_val=0, max_val=8192)
    with nc.If(value > 0):
        body_tensor()
        body_scalar()
        body_vector()


def routing(nc, V, A, T, SC, DS, Y, iota, ident, keys, PS, bank_free, sm, sc_ready):
    HK = 128
    at = [0]
    yf = Y[:, :, :].rearrange("p b n -> p (b n)")

    def part(n):
        s = yf[:, at[0]:at[0] + n]
        at[0] += n
        return s

    v, ixf, tv, pa, pb_, i1s, i2s, gg = (part(n) for n in (256, 256, 128, 128, 128, 128, 128, 128))
    ix = part(256).bitcast(U32)
    S2 = DS[:, 0:2048].rearrange("p (j n) -> p j n", j=16)
    CAND = DS[:, 0:2048].rearrange("p (h n) -> p h n", h=8)
    TMP = DS[:, 2048:4096]
    hm, hs = sm(8), sm(8)
    pos = pa.bitcast(U32)
    posb = pb_.bitcast(U32)

    if True:
        V.wait(sc_ready, T.last())
        for b in range(2):
            for j in range(16):
                s, s2 = SC[:, b, j, :], S2[:, j, :]
                vj, ij = v[:, 16 * j:16 * j + 16], ix[:, 16 * j:16 * j + 16]
                V.op(V.eng.max, vj[:, 0:8], s)
                yield
                V.op(V.eng.match_replace, s2, vj[:, 0:8], s, -3.0e38)
                yield
                V.op(V.eng.max, vj[:, 8:16], s2)
                yield
                V.op(V.eng.max_index, ij[:, 0:8], vj[:, 0:8], s, chain=False)
                yield
                V.op(V.eng.max_index, ij[:, 8:16], vj[:, 8:16], s2)
                yield
            V.op(V.eng.tensor_copy, ixf, ix)
            yield
            vv = v.rearrange("p (h s n) -> p h s n", h=8, s=2)
            for h in range(8):
                V.op(V.eng.tensor_tensor, CAND[:, h, :].rearrange("p (x y) -> p x y", x=16),
                     vv[:, h, 0, :].rearrange("p (n o) -> p n o", o=1).broadcast_to((P, 16, 16)),
                     vv[:, h, 1:2, :].broadcast_to((P, 16, 16)), ALU.add)
                yield
            C2 = SC[:, b, :, :].rearrange("p (h j) n -> p h (j n)", h=8)
            for h in range(8):
                th, ph = tv[:, 16 * h:16 * h + 16], pos[:, 16 * h:16 * h + 16]
                V.op(V.eng.max, th[:, 0:8], CAND[:, h, :])
                yield
                V.op(V.eng.match_replace, C2[:, h, :], th[:, 0:8], CAND[:, h, :], -3.0e38)
                yield
                V.op(V.eng.max, th[:, 8:16], C2[:, h, :])
                yield
                V.op(V.eng.max_index, ph[:, 0:8], th[:, 0:8], CAND[:, h, :], chain=False)
                yield
                V.op(V.eng.max_index, ph[:, 8:16], th[:, 8:16], C2[:, h, :])
                yield
            t8 = tv.rearrange("p (h k) -> p h k", h=8)
            g8 = gg.rearrange("p (h k) -> p h k", h=8)
            V.op(V.eng.tensor_tensor, g8, t8, t8[:, :, 0:1].broadcast_to((P, 8, 16)), ALU.subtract)
            yield
            m = A.op(A.eng.activation, gg, gg, ACT.Exp, after=(V.last(),))
            V.op(V.eng.tensor_scalar, posb, pos, 15, None, ALU.bitwise_and)
            yield
            V.op(V.eng.tensor_scalar, pos, pos, 4, None, ALU.logical_shift_right)
            yield
            V.op(V.eng.tensor_copy, i1s, pos)
            yield
            V.op(V.eng.tensor_copy, i2s, posb)
            yield
            xf = ixf.rearrange("p (h s n) -> p h s n", h=8, s=2)
            T4 = TMP.rearrange("p (h k n) -> p h k n", h=8, k=16)
            i16 = iota[:, 0:16].rearrange("p (o n) -> p o n", o=1).broadcast_to((P, HK, 16))
            for s, sel in enumerate((i1s, i2s)):
                V.op(V.eng.tensor_tensor, TMP.rearrange("p (k n) -> p k n", n=16), i16,
                     sel.rearrange("p (k o) -> p k o", o=1).broadcast_to((P, HK, 16)), ALU.is_equal)
                yield
                for h in range(8):
                    V.op(V.eng.tensor_tensor, T4[:, h], T4[:, h], xf[:, h, s:s + 1, :].broadcast_to((P, 16, 16)),
                         ALU.mult, chain=(h == 0))
                    yield
                V.op(V.eng.tensor_reduce, sel, TMP.rearrange("p (k n) -> p k n", n=16), AX, ALU.add)
                yield
            V.op(V.eng.tensor_reduce, hs, g8, AX, ALU.add, after=(m,))
            yield
            V.op(V.eng.reciprocal, hs, hs)
            yield
            mg = V.op(V.eng.tensor_tensor, g8, g8, hs.rearrange("p (h o) -> p h o", o=1).broadcast_to((P, 8, 16)), ALU.mult)
            yield
            T.wait(mg, bank_free[6])
            for i, src in enumerate((i1s, i2s, gg)):
                ins = nc.tensor.transpose(PS[:, 6, i * P:(i + 1) * P], src, ident)
            mt = T.mark(ins)
            for i, dst in enumerate(keys):
                d = V.op(V.eng.tensor_copy, dst[:, b * P:(b + 1) * P], PS[:, 6, i * P:(i + 1) * P], after=(mt,))
                yield
            bank_free[6] = d


_RAW = ["x", "w_in", "w_out", "w_gate", "w_up", "w_down", "mem_2", "w_in_2", "w_out_2", "w_q_mem_2",
        "w_kv_mem_2", "w_o_mem_2", "w_query_2", "norm_final_2"]


def _constants():
    t = np.arange(256)
    q, k = t[:, None], t[None, :]
    by_tile = lambda m: np.ascontiguousarray(m.reshape(2, 128, -1).transpose(1, 0, 2), dtype=np.float32)
    causal = k <= q
    count = (causal & (q - k <= 128)).astype(int) + (causal & ((q - k) % 4 == 0)) + (causal & ((q - k) % 16 == 0))
    inv = 1.0 / (np.float32(10000.0) ** (np.arange(0, 64, 2, dtype=np.float32) / np.float32(64)))
    ang = t.astype(np.float32)[:, None] * inv.astype(np.float32)[None, :]
    rope = np.stack([by_tile(np.cos(ang)), by_tile(np.sin(ang))], axis=1)
    sel = np.zeros((8, 8, 128), np.float32)
    for h in range(8):
        sel[h, h] = 1.0
    return {
        "c_ii": np.ascontiguousarray(np.stack([np.eye(128, dtype=np.float32), np.tile(np.arange(128, dtype=np.float32), (128, 1))], axis=1)),
        "c_tri": by_tile((q <= k).astype(np.float32)),
        "c_fox": by_tile(np.where(causal, 0.0, NEG)),
        "c_dil": by_tile(np.where(count > 0, np.log(np.maximum(count, 1)), NEG)),
        "c_rope": np.ascontiguousarray(rope, dtype=np.float32),
        "c_sel": sel,
    }


def _laid_out(i):
    c = np.ascontiguousarray
    out = {n: c(i[n]) for n in _RAW}
    k = _constants()
    out |= {n: k[n] for n in ("c_ii", "c_tri", "c_sel")}
    vec = lambda v: v.reshape(128, 8)
    every = lambda v: np.broadcast_to(v.reshape(1, -1), (128, v.size))
    chunks = lambda v: v.reshape(4, 128).T
    pack = [vec(i["norm_mix"]), vec(np.concatenate([i["out_norm_fox"][0], i["out_norm_dil"][0]])),
            vec(i["norm_ffn"]), vec(i["norm_mix_2"]), vec(i["norm_cross_2"]), vec(i["norm_mem_2"]),
            vec(i["norm_ffn_2"]), vec(np.concatenate([i["norm_grp_a_2"][0], i["norm_grp_b_2"][0]])),
            np.tile(i["q_norm_fox"][0], 2)[:, None], np.tile(i["k_norm_fox"][0], 2)[:, None],
            every(i["b_forget"]), every(i["b_router_group"]), every(i["b_router_expert"]),
            i["conv_w_2"][0].reshape(4, 4, 128).transpose(2, 1, 0).reshape(128, 16),
            chunks(i["conv_b_2"][0]), chunks(i["gate_a_b_2"][0]), chunks(i["gate_x_b_2"][0]),
            chunks(i["lru_lambda_2"][0])]
    out["pack"] = c(np.concatenate(pack, axis=1))
    we = i["w_router_expert"][0].transpose(1, 0, 2).reshape(1024, 32)
    wr = np.concatenate([i["w_router_group"][0], we], axis=1)
    flat = lambda v: v.reshape(128, -1)
    out["pack_acts"] = c(np.concatenate(
        [flat(k["c_fox"]), flat(k["c_dil"]), flat(k["c_rope"]), every(i["q_norm_dil"]), every(i["k_norm_dil"]),
         flat(c(i["w_in"][0][:, 3072:3080])), flat(wr)], axis=1))
    for n in ("gate_a_w_2", "gate_x_w_2"):
        out[n] = c(i[n][0].reshape(4, 2, 64, 64).transpose(1, 2, 0, 3).reshape(128, 4, 64))
    t = np.arange(256)
    rel = np.clip(t[:, None] - t[None, :], -128, 128) + 128
    rel = np.where(t[None, :] // 64 <= t[:, None] // 64, rel, 257)
    ext = np.concatenate([i["rel_bias_2"][0], np.full((8, 1), NEG, np.float32)], axis=1)
    slots = [2 * (s % 4) + s // 4 for s in range(8)]
    bias = ext[slots][:, rel].transpose(1, 0, 2)
    out["bias_2"] = c(np.concatenate([bias[:128, :, :128].reshape(128, -1), bias[128:].reshape(128, -1)], axis=1))
    out["sub_keys_2"] = c(i["sub_keys_2"][0].transpose(3, 0, 1, 2).reshape(128, 2048))
    u = i["expert_u_2"][0].reshape(128, 32, 4, 128, 8)
    out["expert_u_2"] = c(u.transpose(1, 3, 2, 4, 0).reshape(32, 128, 4096))
    v = i["expert_v_2"][0].reshape(128, 32, 4096)
    out["expert_v_2"] = c(v.transpose(1, 0, 2))
    return out


def kernel(**inputs):
    import concourse.bacc as _bacc
    from concourse.bass_utils import run_bass_kernel_spmd as _run

    nc = _bacc.Bacc("TRN2", target_bir_lowering=False, num_devices=1)
    arrays = _laid_out({k: np.asarray(v) for k, v in inputs.items()})
    aps, send = {}, {}
    for name, v in arrays.items():
        send[f"in_{name}"] = v
        aps[name] = nc.dram_tensor(f"in_{name}", v.shape, mybir.dt.from_np(v.dtype), kind="ExternalInput").ap()
    out = nc.dram_tensor("out_0", (1, 256, 1024), F32, kind="ExternalOutput").ap()
    program(nc, aps, out)
    r = _run(nc, [send], core_ids=[0])
    return r.results[0]["out_0"]
```

```python
import math

import numpy as np

import concourse.bass as bass
from concourse import mybir

F32 = mybir.dt.float32
FR = mybir.dt.float32r
U32 = mybir.dt.uint32
I32 = mybir.dt.int32
ALU = mybir.AluOpType
ACT = mybir.ActivationFunctionType
AX = mybir.AxisListType.X

EPS = 1e-6
NEG = -1e30
P = 128
D = 1024
CAP = 64
NPACK = 142
SHARE = 1536
ROUTING_SHARE = 2800


class Lane:

    def __init__(self, nc, eng, name):
        self.eng, self.name = eng, name
        self.sem = nc.alloc_semaphore(name)
        self.n = 0
        self.seen = {}

    def wait(self, *marks):
        for m in marks:
            if m is None:
                continue
            if isinstance(m, list):
                self.wait(*m)
                continue
            sem, v = m
            if self.seen.get(sem.name, 0) < v:
                self.eng.wait_ge(sem, v)
                self.seen[sem.name] = v

    def mark(self, ins):
        self.n += 1
        ins.then_inc(self.sem, 1)
        return (self.sem, self.n)

    def last(self):
        return (self.sem, self.n)

    def op(self, build, *args, after=(), chain=True, **kw):
        self.wait(*after)
        if chain and self.n:
            self.wait(self.last())
        return self.mark(build(*args, **kw))


class Load:

    def __init__(self, nc, name):
        self.sem, self.n = nc.alloc_semaphore(name), 0

    def start(self, lane, dst, src, after=()):
        lane.wait(*after)
        lane.eng.dma_start(dst, src).then_inc(self.sem, 16)
        self.n += 16
        return (self.sem, self.n)

    def mark(self):
        return (self.sem, self.n)


class Ring:

    def __init__(self, nc, lane, slots, plan, slot_of):
        self.lane, self.slots, self.plan, self.slot_of = lane, slots, plan, slot_of
        self.sems = [nc.alloc_semaphore(f"s_ring{i}") for i in range(len(slots))]
        self.before, self.turn, last, count = [], [], {}, {}
        for i, s in enumerate(slot_of):
            self.before.append(last.get(s))
            count[s] = count.get(s, 0) + 1
            self.turn.append(count[s])
            last[s] = i
        self.issued = self.taken = self.freed = 0
        self.marks = {}
        self._issue()

    def _issue(self):
        while self.issued < len(self.plan):
            i = self.issued
            before = self.before[i]
            if before is not None and before not in self.marks:
                return
            n, pat, kw, src = self.plan[i]
            dst = self.slots[self.slot_of[i]][:, 0:n]
            if pat:
                dst = dst.rearrange(pat, **kw)
            if before is not None:
                self.lane.wait(*self.marks[before])
            self.lane.eng.dma_start(dst, src).then_inc(self.sems[self.slot_of[i]], 16)
            self.issued += 1

    def take(self):
        i = self.taken
        self.taken += 1
        assert i < self.issued
        return self.slots[self.slot_of[i]], (self.sems[self.slot_of[i]], 16 * self.turn[i])

    def hold(self, n):
        held = list(range(self.freed, self.freed + n))
        self.freed += n
        return held

    def free_held(self, i, *marks):
        self.marks[i] = marks
        self._issue()

    def free(self, *marks):
        self.marks[self.freed] = marks
        self.freed += 1
        self._issue()


class Halves:

    def __init__(self, V, A, G, bufs, fr, ring, of):
        self.V, self.A, self.G, self.bufs, self.fr = V, A, G, bufs, fr
        self.ring, self.of, self.early = ring, of, []
        self.used = [None] * len(bufs)
        self.n = 0

    def split(self, tile, landed, n=2048, after=()):
        V, A = self.V, self.A
        i = self.n % len(self.bufs)
        self.n += 1
        hi = self.bufs[i][:, 0:n]
        raw = tile[:, 0:n]
        m = A.op(A.eng.activation, self.fr(hi), raw, ACT.Copy, after=(landed, self.used[i], *after), chain=False)
        ready = []
        for lane, lo, end in ((V, 0, SHARE), (self.G, SHARE, n)):
            x, h = raw[:, lo:end], self.fr(hi[:, lo:end]).bitcast(F32)
            ready.append(lane.op(lane.eng.tensor_tensor, self.fr(x), x, h, ALU.subtract, after=(m, landed), chain=False))
        return self.fr(hi), self.fr(raw), ready, i

    def free(self, i, mark):
        self.used[i] = mark

    def ahead(self):
        if not self.early and self.ring.taken in self.of:
            self.early.append(self.split(*self.ring.take()))

    def next(self):
        self.ahead()
        return self.early.pop()


class Beside:

    def __init__(self):
        self.width = 1
        self.waiting, self.places = [], [None] * 4

    def add(self, chain, may_start=lambda: True):
        self.waiting.append((chain, may_start))

    def step(self):
        for i in range(self.width):
            able = [w for w in self.waiting if w[1]()]
            if self.places[i] is None and able:
                self.waiting.remove(able[0])
                self.places[i] = able[0][0](i)
            if self.places[i] is not None and next(self.places[i], "done") == "done":
                self.places[i] = None

    def finish(self):
        while self.waiting or any(self.places):
            self.step()


def program(nc, a, out, dbg=None):
    sb = lambda name, shape, dt=F32: nc.alloc_sbuf_tensor(name, shape, dt)
    twins = {}

    def twin(name, shape, piece=None):
        t = sb(name, shape)
        row = math.prod(shape[1:])
        piece = piece or row
        start = nc.sbuf_base - 4 * row
        twins[name] = piece, [nc.alloc_sbuf_tensor_at(f"{name}_parts{i}", [P, piece], FR, offset=start + 4 * piece * i)
                              for i in range(row // piece)]
        return t

    def fr(x):
        piece, names = twins[x.tensor.name]
        (_, rows), *rest = x.ap
        assert rows == P
        return bass.AP(names[x.offset // piece], x.offset % piece, [[piece, P], *rest])

    V = Lane(nc, nc.vector, "s_dve")
    A = Lane(nc, nc.scalar, "s_act")
    T = Lane(nc, nc.tensor, "s_pe")
    G = Lane(nc, nc.gpsimd, "s_pool")
    S = Lane(nc, nc.sync, "s_sp")
    mm = nc.tensor.matmul

    BIG = twin("big", [P, 32768], 8192)
    FIX = twin("fix", [P, 5, 2048])
    ACTS, DS = BIG[:, 0:16384], BIG[:, 24576:32768]
    X = twin("x", [P, 2, D])
    HH = twin("hh", [P, 8, 256])
    HL = twin("hl", [P, 8, 256])
    HT = (fr(HH[:, :, :]), fr(HL[:, :, :]))
    Y = twin("y", [P, 2, D])
    ii = sb("ii", [P, 2, P])
    ident, iota = ii[:, 0, :], ii[:, 1, :]
    tig = sb("tig", [P, 768])
    tri = tig[:, 0:512].rearrange("p (b k) -> p b k", b=2)
    small = sb("small", [P, 952])
    PS = nc.alloc_psum_tensor("ps", [P, 8, 512], F32)
    bank_free = [None] * 8
    small_at = [0]

    def sm(n):
        s = small[:, small_at[0]:small_at[0] + n]
        small_at[0] += n
        return s

    def cols(w, n0, n=512):
        w = w.rearrange("(p k) n -> p k n", k=8)
        return [(4 * n, "p (k n) -> p k n", dict(k=4), w[:, 4 * h:4 * h + 4, n0:n0 + n]) for h in range(2)]

    def whole(src):
        return [(2048, None, None, src[:, 2048 * h:2048 * h + 2048]) for h in range(2)]

    def product(w, n):
        return [t for i in range(n) for t in cols(w, 512 * i)]

    plan = product(a["w_in"][0], 6) + product(a["w_out"][0], 2)
    split_tiles = set(range(len(plan)))
    for e in range(0, 32, 2):
        for w, k in (("w_gate", 8), ("w_up", 8), ("w_down", 4)):
            one, two = (whole(a[w][0, i].rearrange("(p k) n -> p (k n)", k=k)) for i in (e, e + 1))
            plan += [one[0], two[0], one[1], two[1]]
    w_in_2 = lambda *at: [t for n0 in at for t in cols(a["w_in_2"][0], n0)]
    before = len(plan)
    plan += w_in_2(1024, 1536, 2048)
    split_tiles |= set(range(before, len(plan)))
    plan += [(1024, None, None, a["bias_2"][:, 0:1024]), (2048, None, None, a["bias_2"][:, 1024:3072])]
    before = after_bias = len(plan)
    plan += w_in_2(0, 512) + product(a["w_kv_mem_2"][0], 4) + product(a["w_out_2"][0], 2)
    plan += product(a["w_q_mem_2"][0], 2) + product(a["w_o_mem_2"][0], 2)
    plan += product(a["w_query_2"][0], 4)
    split_tiles |= set(range(before, len(plan)))
    plan.append((2048, None, None, a["sub_keys_2"]))
    slot_of = [i % 7 for i in range(after_bias)]
    for i in range(after_bias, len(plan)):
        recent = slot_of[-3 if i == len(plan) - 1 else -6:] if i >= after_bias + 16 else slot_of[after_bias - 2:after_bias] + slot_of[max(after_bias, i - 4):]
        slot_of.append(min((s for s in range(3 if i == len(plan) - 1 else 0, 7) if s not in recent),
                           key=lambda s: max(k for k, x in enumerate(slot_of) if x == s)))
    for w in ("expert_u_2", "expert_v_2"):
        for i in range(32):
            plan += whole(a[w][i])
    slot_of += [i % 3 for i in range(128)]
    slots = [FIX[:, i, :] for i in range(3)] + [BIG[:, 16384 + 2048 * i:18432 + 2048 * i] for i in range(4)]
    split_bufs = [FIX[:, 3, :], FIX[:, 4, :]]

    l_x = Load(nc, "l_x")
    for b in range(2):
        l_x.start(S, X[:, b, :], a["x"][0, b * P:(b + 1) * P, :])
    l_c = Load(nc, "l_c")
    l_c.start(A, ii[:, :, :], a["c_ii"])
    l_c.start(A, small[:, 0:NPACK], a["pack"])
    S.wait(l_x.mark())
    l_s = Load(nc, "l_s")
    l_s.start(S, ACTS[:, 14336:15968], a["pack_acts"])
    l_s.start(S, tri, a["c_tri"])
    for o in (0, 64):
        l_s.start(S, DS[o:o + 8, 3072:4096], a["c_sel"].rearrange("h a q -> h (a q)"))
    ring = Ring(nc, S, slots, plan, slot_of)
    PROJ = ACTS[:, 0:6144].rearrange("p (b n) -> p b n", b=2)
    QK = ACTS[:, 6144:10240].rearrange("p (j c t) -> p j c t", j=4, c=4)
    PB = [ACTS[:, o:o + 1024] for o in (10240, 11264)]
    PT = [ACTS[:, o:o + 1024] for o in (12288, 13312)]
    for x in (HH, HL):
        PB.append(x[:, 0:4, :].rearrange("p k t -> p (k t)"))
        PT.append(x[:, 4:8, :].rearrange("p k t -> p (k t)"))
    MEM = ACTS[:, 10240:12288].rearrange("p (b n) -> p b n", b=2)
    MN = ACTS[:, 12288:14336].rearrange("p (b n) -> p b n", b=2)
    MT = [fr(DS[:, o:o + 2048]).rearrange("p (k t) -> p k t", k=8) for o in (4096, 6144)]
    MF = ACTS[:, 14336:14848].rearrange("p (b k) -> p b k", b=2)
    MD = ACTS[:, 14848:15360].rearrange("p (b k) -> p b k", b=2)
    ROPE = ACTS[:, 15360:15488].rearrange("p (s b f) -> p s b f", s=2, b=2)
    GDIL = ACTS[:, 15488:15616].rearrange("p (s d) -> p s d", s=2)
    CT = ACTS[:, 15968:16224]
    SEL = DS[:, 3072:4096].rearrange("p (h q) -> p h q", h=8)

    def packed(n):
        small_at[0] += n
        return small[:, small_at[0] - n:small_at[0]]

    g_mix, g_out, g_ffn, g_mix2, g_cross, g_mem, g_ffn2, g_grp = (packed(8) for _ in range(8))
    gq, gk, bf, br, cw, cb, gab, gxb, lam = (packed(n) for n in (1, 1, 8, 36, 16, 4, 4, 4, 4))
    cw = cw.rearrange("p (c w) -> p c w", c=4)
    assert small_at[0] == NPACK
    consts = [l_c.mark()]
    beside = Beside()
    halves = Halves(V, A, G, split_bufs, fr, ring, split_tiles)

    warm = sm(1)

    def root_ahead():
        A.op(A.eng.activation, warm, iota[:, 1:2], ACT.Sqrt)

    def rstd_of(ss, width):
        V.op(V.eng.tensor_scalar, ss, ss, 1.0 / width, EPS, ALU.mult, ALU.add, after=(A.last(),))
        root_ahead()
        A.op(A.eng.activation, ss, ss, ACT.Sqrt, after=(V.last(),))
        return V.op(V.eng.reciprocal, ss, ss, after=(A.last(),))

    def turned_chain(xs, gain, dst, after, turned):
        hi, lo = dst
        marks = []
        for bank in range(4):
            T.wait(bank_free[bank], *after)
            for k in (2 * bank, 2 * bank + 1):
                for b in range(2):
                    ins = nc.tensor.transpose(
                        PS[:, bank, (k % 2) * 256 + b * P:(k % 2) * 256 + (b + 1) * P],
                        xs[:, b, :].rearrange("p (c k) -> p k c", k=8)[:, k, :], ident)
            marks.append(T.mark(ins))
        yield
        for bank, m in enumerate(marks):
            for k in (2 * bank, 2 * bank + 1):
                src = PS[:, bank, (k % 2) * 256:(k % 2) * 256 + 256]
                ma = A.op(A.eng.activation, hi[:, k, :], src, ACT.Copy,
                          scale=1.0 if gain is None else gain[:, k:k + 1], after=(m,), chain=False)
            for k in (2 * bank, 2 * bank + 1):
                src = PS[:, bank, (k % 2) * 256:(k % 2) * 256 + 256]
                mv = V.op(V.eng.scalar_tensor_tensor, lo[:, k, :], src, 1.0 if gain is None else gain[:, k:k + 1],
                          hi[:, k, :].bitcast(F32), ALU.mult, ALU.subtract, after=(ma,), chain=False)
            bank_free[bank] = mv
            turned[bank] = mv
            yield

    def transposed(xs, gain, dst, after):
        turned = [None] * 4
        for _ in turned_chain(xs, gain, dst, after, turned):
            pass
        return turned

    ss = sm(4)

    def norm_chain(src, xs, ss, after=()):
        for b in range(2):
            A.op(A.eng.activation, xs[:, b, :], src[:, b, :], ACT.Square, accum_out=ss[:, b:b + 1], after=after)
        yield
        rstd_of(ss, D)
        yield
        for b in range(2):
            V.op(V.eng.tensor_scalar, xs[:, b, :], src[:, b, :], ss[:, b:b + 1], None, ALU.mult)

    def norm(src, xs, after=()):
        root_ahead()
        for b in range(2):
            A.op(A.eng.activation, xs[:, b, :], src[:, b, :], ACT.Square, accum_out=ss[:, b:b + 1],
                 after=(*after, V.last(), T.last()))
        rstd_of(ss[:, 0:2], D)
        for b in range(2):
            V.op(V.eng.tensor_scalar, xs[:, b, :], src[:, b, :], ss[:, b:b + 1], None, ALU.mult)
        return V.last()

    def pass3(o, l, r, first, last):
        mm(o, l[0], r[0], start=first, stop=False)
        mm(o, l[0], r[1], start=False, stop=False)
        return mm(o, l[1], r[0], start=False, stop=last)

    def tokens_by(w, ht, b, bank, n, after, turned, k0=0, k_of=8):
        T.wait(bank_free[bank], after)
        for k in range(k_of):
            T.wait(turned[(k0 + k) // 2])
            ins = pass3(PS[:, bank, 0:n], [x[:, k0 + k, b * P:(b + 1) * P] for x in ht], [x[:, k, 0:n] for x in w],
                        k0 + k == 0, k0 + k == 7)
        return T.mark(ins)

    def by_k(x, n=512, k=4):
        return x[:, 0:k * n].rearrange("p (k n) -> p k n", k=k)

    def tokens_product(ht, banks, turned):
        for h in range(2):
            hi, lo, m, i = halves.next()
            for b in range(2):
                mt = tokens_by((by_k(hi), by_k(lo)), ht, b, banks[b], 512, m, turned, 4 * h, 4)
                if b == 0:
                    beside.step()
                if h and b == 0:
                    first = mt
            halves.free(i, mt)
            ring.free(mt)
            halves.ahead()
            beside.step()
        return first, mt

    def features_product(ht, turned, put):
        banks = (4, 5, 6, 7)
        marks = []
        for h in range(2):
            hi, lo, m, i = halves.next()
            T.wait(m)
            for c in range(4):
                T.wait(bank_free[banks[c]])
                for k in range(4):
                    T.wait(turned[2 * h + k // 2])
                    ins = pass3(PS[:, banks[c], 0:256], [by_k(x)[:, k, c * P:(c + 1) * P] for x in (hi, lo)],
                                [x[:, 4 * h + k, :] for x in ht], h + k == 0, h == 1 and k == 3)
                mt = T.mark(ins)
                if h:
                    marks.append(mt)
                if c == 1:
                    beside.step()
            halves.free(i, mt)
            ring.free(mt)
            halves.ahead()
            if h:
                for c, m in enumerate(marks):
                    bank_free[banks[c]] = put(c, PS[:, banks[c], 0:256], m)
            beside.step()

    T.wait(*consts)
    V.wait(*consts)
    A.wait(*consts)
    m = norm(X, Y, after=(l_x.mark(),))
    l_m = Load(nc, "l_m")
    for b in range(2):
        l_m.start(A, ACTS[:, 10240 + D * b:11264 + D * b], a["mem_2"][0, b * P:(b + 1) * P, :])
    ht_ready = transposed(Y, g_mix, HT, (m,))

    def project(n_tiles, dst, ready, ht=HT, bank0=4):
        for i in range(n_tiles):
            banks = [bank0 + 2 * (i % 2), bank0 + 2 * (i % 2) + 1]
            m = tokens_product(ht, banks, ready)
            bank_free[banks[0]] = V.op(V.eng.tensor_copy, dst(i, 0), PS[:, banks[0], :], after=(m[0],), chain=False)
            bank_free[banks[1]] = A.op(A.eng.activation, dst(i, 1), PS[:, banks[1], :], ACT.Copy, after=(m[1],),
                                       chain=False)
        return [V.last(), A.last()]

    logf, cum = sm(16), sm(16)
    V.wait(l_s.mark())
    A.wait(l_s.mark())
    T.wait(l_s.mark())
    WS = ACTS[:, 15616:15968]
    WSH, WSL = DS[:, 2048:2400], DS[:, 2432:2784]
    m = A.op(A.eng.activation, fr(WSH), WS, ACT.Copy)
    ws_ready = V.op(V.eng.tensor_tensor, fr(WSL), WS, fr(WSH).bitcast(F32), ALU.subtract, after=(m,))
    WF = [fr(x[:, 0:64]).rearrange("p (k n) -> p k n", k=8) for x in (WSH, WSL)]
    WR = [fr(x[:, 64:352]).rearrange("p (k n) -> p k n", k=8) for x in (WSH, WSL)]
    def narrow_product(w, n, bias, dst, place, after, turned):
        zt = place[0:n, :]
        T.wait(after, bank_free[4])
        for k in range(8):
            T.wait(turned[k // 2])
            ins = pass3(PS[0:n, 4, 0:256], [x[:, k, :] for x in w], [x[:, k, :] for x in HT], k == 0, k == 7)
        m = T.mark(ins)
        m = V.op(V.eng.tensor_copy, zt, PS[0:n, 4, 0:256], after=(m,))
        T.wait(m, bank_free[5])
        for b in range(2):
            ins = nc.tensor.transpose(PS[:, 5, b * n:b * n + n], zt[:, b * P:(b + 1) * P], ident[0:n, 0:n])
        m = T.mark(ins)
        for b in range(2):
            d = V.op(V.eng.tensor_tensor, dst(b), PS[:, 5, b * n:b * n + n], bias, ALU.add, after=(m,), chain=False)
        bank_free[4] = bank_free[5] = d

    halves.ahead()
    narrow_product(WF, 8, bf, lambda b: logf[:, 8 * b:8 * b + 8], ACTS[:, 0:256], ws_ready, ht_ready)
    t0, t1, t2, t3 = (sm(16) for _ in range(4))

    def log1p_exp_neg_abs(x, n, e, s, s2, q):
        V.op(V.eng.tensor_scalar, e[:, 0:n], x, -1.0, None, ALU.mult)
        V.op(V.eng.tensor_tensor, e[:, 0:n], e[:, 0:n], x, ALU.min)
        A.op(A.eng.activation, e[:, 0:n], e[:, 0:n], ACT.Exp, after=(V.last(),))
        V.op(V.eng.tensor_scalar, s[:, 0:n], e[:, 0:n], 2.0, None, ALU.add, after=(A.last(),))
        V.op(V.eng.reciprocal, s[:, 0:n], s[:, 0:n])
        V.op(V.eng.tensor_tensor, s[:, 0:n], s[:, 0:n], e[:, 0:n], ALU.mult)
        V.op(V.eng.tensor_tensor, s2[:, 0:n], s[:, 0:n], s[:, 0:n], ALU.mult)
        V.op(V.eng.tensor_scalar, q[:, 0:n], s2[:, 0:n], 1.0 / 17, 1.0 / 15, ALU.mult, ALU.add)
        for c in (13, 11, 9, 7, 5, 3, 1):
            V.op(V.eng.tensor_tensor, q[:, 0:n], q[:, 0:n], s2[:, 0:n], ALU.mult)
            V.op(V.eng.tensor_scalar, q[:, 0:n], q[:, 0:n], 1.0 / c, None, ALU.add)
        V.op(V.eng.tensor_tensor, e[:, 0:n], q[:, 0:n], s[:, 0:n], ALU.mult)
        return V.op(V.eng.tensor_scalar, e[:, 0:n], e[:, 0:n], 2.0, None, ALU.mult)

    ct_ready = []

    def forget_chain(place):
        b0 = 2 * place
        log1p_exp_neg_abs(logf, 16, t0, t1, t2, t3)
        V.op(V.eng.tensor_scalar, logf, logf, 0.0, None, ALU.min)
        m = V.op(V.eng.tensor_tensor, logf, logf, t0, ALU.subtract)
        yield
        T.wait(m, bank_free[b0], bank_free[b0 + 1])
        mm(PS[:, b0, 0:8], tri[:, 0, 0:P], logf[:, 0:8], start=True, stop=True)
        mm(PS[:, b0, 8:16], tri[:, 0, P:256], logf[:, 0:8], start=True, stop=False)
        mm(PS[:, b0, 8:16], tri[:, 1, P:256], logf[:, 8:16], start=False, stop=True)
        for o in (0, 64):
            for b in range(2):
                ins = mm(PS[o:o + 8, b0 + 1, 0:256], logf[:, 8 * b:8 * b + 8], tri[:, b, :], start=(b == 0),
                         stop=(b == 1))
        m = T.mark(ins)
        yield
        V.op(V.eng.tensor_copy, cum, PS[:, b0, 0:16], after=(m,))
        for o in (0, 64):
            d = V.op(V.eng.tensor_scalar, CT[o:o + 8, :], PS[o:o + 8, b0 + 1, 0:256], -1.0, None, ALU.mult)
        bank_free[b0] = bank_free[b0 + 1] = d
        ct_ready.append(d)

    beside.add(forget_chain)

    mss, mt_ready = sm(2), [None] * 4

    def memory_chain(_):
        yield from norm_chain(MEM, MN, mss, (l_m.mark(), *ht_ready))
        yield
        yield from turned_chain(MN, g_mem, MT, (V.last(),), mt_ready)

    nrm = sm(64).rearrange("p (j b n) -> p j b n", b=2, j=2)
    SQ = DS[:, 0:2048].rearrange("p (b n d) -> p b n d", b=2, d=64)
    qk_ready, v_ready = [None, None], [None, None]

    def qk_chain(place, j, proj_ready):
        qks = [PROJ[:, b, 1536 * j:1536 * j + 1024].rearrange("p (n d) -> p n d", d=64) for b in range(2)]
        for b in range(2):
            mq = A.op(A.eng.activation, SQ[:, b], qks[b], ACT.Square, after=(proj_ready, V.last(), G.last()), chain=False)
            yield
            V.op(V.eng.tensor_reduce, nrm[:, j, b, :], SQ[:, b], AX, ALU.add, after=(mq,), chain=False)
        rstd_of(nrm[:, j].rearrange("p b n -> p (b n)"), 64)
        V.op(V.eng.tensor_scalar, nrm[:, j, :, 0:8], nrm[:, j, :, 0:8], 0.125, None, ALU.mult)
        yield
        for b in range(2):
            qk = qks[b]
            V.op(V.eng.tensor_tensor, qk, qk, nrm[:, j, b, :].rearrange("p (n o) -> p n o", o=1).broadcast_to((P, 16, 64)),
                 ALU.mult, after=(proj_ready,))
            if j:
                q4 = qk.rearrange("p (s n) d -> p s n d", s=2)
                for s in range(2):
                    V.op(V.eng.tensor_tensor, q4[:, s], q4[:, s], GDIL[:, s:s + 1, :].broadcast_to((P, 8, 64)), ALU.mult)
                yield
                cos = ROPE[:, 0, b:b + 1, :].broadcast_to((P, 16, 32))
                sin = ROPE[:, 1, b:b + 1, :].broadcast_to((P, 16, 32))
                x1, x2 = qk[:, :, 0:32], qk[:, :, 32:64]
                tmp = [DS[:, 512 * i:512 + 512 * i].rearrange("p (n d) -> p n d", d=32) for i in range(4)]
                G.op(G.eng.tensor_tensor, tmp[0], x1, sin, ALU.mult, after=(V.last(),))
                g1 = G.op(G.eng.tensor_tensor, tmp[1], x2, sin, ALU.mult)
                V.op(V.eng.tensor_tensor, tmp[2], x1, cos, ALU.mult)
                V.op(V.eng.tensor_tensor, tmp[3], x2, cos, ALU.mult)
                yield
                V.op(V.eng.tensor_tensor, x1, tmp[2], tmp[1], ALU.subtract, after=(g1,))
                V.op(V.eng.tensor_tensor, x2, tmp[3], tmp[0], ALU.add)
            yield
        normed = V.last()
        for i in range(2):
            off = 1536 * j + 512 * i
            marks = []
            for half in range(2):
                bank = 2 * place + half
                T.wait(bank_free[bank], normed)
                for c in (2 * half, 2 * half + 1):
                    for b in range(2):
                        ins = nc.tensor.transpose(PS[:, bank, (c % 2) * 256 + b * P:(c % 2) * 256 + (b + 1) * P],
                                                  PROJ[:, b, off + c * P:off + (c + 1) * P], ident)
                marks.append(T.mark(ins))
            yield
            for half, m in enumerate(marks):
                bank = 2 * place + half
                dst = QK[:, 2 * j + i, 2 * half:2 * half + 2, :].rearrange("p c t -> p (c t)")
                scale = 1.0 if j else (gq, gk)[i]
                if half:
                    d = A.op(A.eng.activation, dst, PS[:, bank, :], ACT.Copy, scale=scale, after=(m,), chain=False)
                else:
                    d = V.op(V.eng.tensor_scalar, dst, PS[:, bank, :], scale, None, ALU.mult, after=(m,), chain=False)
                bank_free[bank] = d
        qk_ready[j] = [V.last(), A.last()]

    mxs, nms, lsums, rls = ([sm(4) for _ in range(4)] for _ in range(4))
    pb_read, pt_read = [None] * 4, [None] * 4

    def attend(place, pbs, pts, scratch, qt, kt, bias, v, b, g, dst, oss, ready, v_ready, decay=None, bias_landed=None,
               bias_read=None):
        K, o = P * (b + 1), 64 * g
        b0 = 2 * place
        S = PS[:, b0:b0 + 2, :].rearrange("p a (c k) -> p (a c) k", k=256)
        pb = pbs[place][:, 0:4 * K].rearrange("p (h k) -> p h k", h=4)
        pt = pts[place].rearrange("p (b n) -> p b n", b=2)
        mx, nm, lsum, rl = mxs[place], nms[place], lsums[place], rls[place]
        T.wait(bank_free[b0], bank_free[b0 + 1], *ready())
        for i in range(4):
            if decay is not None:
                mm(S[:, i, 0:K], SEL[o:o + 8, 2 * i + g, :], CT[o:o + 8, 0:K], start=True, stop=False)
            ins = mm(S[:, i, 0:K], qt[o:o + 64, i, b * P:(b + 1) * P], kt[o:o + 64, i, 0:K],
                     start=decay is None, stop=True)
        m = T.mark(ins)
        yield
        m = V.op(V.eng.tensor_tensor, pb, S[:, :, 0:K], bias[:, :, 0:K].broadcast_to((P, 4, K)), ALU.add,
                 after=(m, pb_read[place], bias_landed))
        if bias_read is not None:
            bias_read(m)
        bank_free[b0] = bank_free[b0 + 1] = m
        V.op(V.eng.tensor_reduce, mx, pb, AX, ALU.max)
        if decay is None:
            V.op(V.eng.tensor_scalar, nm, mx, -1.0, None, ALU.mult)
        else:
            V.op(V.eng.tensor_tensor, mx, mx, decay, ALU.add)
            V.op(V.eng.tensor_tensor, nm, decay, mx, ALU.subtract)
        ready_e = V.last()
        for i in range(4):
            e = A.op(A.eng.activation, pb[:, i, :], pb[:, i, :], ACT.Exp, bias=nm[:, i:i + 1],
                     accum_out=lsum[:, i:i + 1], after=(ready_e,), chain=False)
        yield
        rec = V.op(V.eng.reciprocal, rl, lsum, after=(e,))
        marks = []
        for kb in range(b + 1):
            T.wait(bank_free[b0 + kb], e)
            for i in range(4):
                ins = nc.tensor.transpose(PS[:, b0 + kb, i * P:(i + 1) * P], pb[:, i, kb * P:(kb + 1) * P], ident)
            marks.append(T.mark(ins))
        pb_read[place] = marks[-1]
        yield
        copied = []
        for kb, m in enumerate(marks):
            if kb:
                m = A.op(A.eng.activation, pt[:, kb, :], PS[:, b0 + kb, :], ACT.Copy, after=(m, pt_read[place]), chain=False)
            else:
                m = V.op(V.eng.tensor_copy, pt[:, kb, :], PS[:, b0 + kb, :], after=(m, pt_read[place]), chain=False)
            bank_free[b0 + kb] = m
            copied.append(m)
        yield
        T.wait(copied, v_ready())
        for i in range(4):
            for kb in range(b + 1):
                ins = mm(PS[:, b0, i * 64:(i + 1) * 64], pt[:, kb, i * P:(i + 1) * P], v(kb, 2 * i + g),
                         start=(kb == 0), stop=(kb == b))
        m = T.mark(ins)
        pt_read[place] = m
        yield
        m = V.op(V.eng.tensor_tensor, dst, PS[:, b0, 0:256].rearrange("p (h d) -> p h d", h=4),
                 rl.rearrange("p (n o) -> p n o", o=1).broadcast_to((P, 4, 64)), ALU.mult, after=(m, rec))
        bank_free[b0] = m
        A.op(A.eng.activation, scratch.rearrange("p (h d) -> p h d", h=4), dst, ACT.Square, accum_out=oss, after=(m,))

    oss8 = sm(8)
    Y6 = Y[:, :, :].rearrange("p b (j h i d) -> p b j i h d", j=2, h=4, i=2)
    memory_done = []

    def memory_then(place):
        yield from memory_chain(place)
        memory_done.extend([V.last(), A.last()])

    beside.add(memory_then)
    for j in range(2):
        for b in (1, 0):
            for g in range(2):
                n = 4 * j + 2 * b + g
                beside.add(lambda place, j=j, b=b, g=g, n=n: attend(
                    place, PB, PT, DS[:, 2800:3056], QK[:, 2 * j], QK[:, 2 * j + 1], (MF, MD)[j][:, b:b + 1, :],
                    lambda kb, h: PROJ[:, kb, 1536 * j + 1024 + 64 * h:1536 * j + 1088 + 64 * h], b, g,
                    Y6[:, b, j, g], oss8[:, n:n + 1], lambda: (qk_ready[j], ct_ready), lambda: v_ready[j],
                    decay=None if j else cum[:, 8 * b:8 * b + 8].rearrange("p (i g) -> p g i", g=2)[:, g, :]),
                    lambda j=j: bool(memory_done and qk_ready[j] and v_ready[j]))
    for i in range(6):
        proj_ready = project(1, lambda _, b: PROJ[:, b, 512 * i:512 * i + 512], ht_ready, bank0=4 + 2 * (i % 2))
        j, part = divmod(i, 3)
        if part == 1:
            beside.waiting.insert(0, (lambda place, j=j, r=proj_ready: qk_chain(place, j, r), lambda: bool(memory_done)))
        if part == 2:
            v_ready[j] = proj_ready
            beside.width = 2
    beside.width = 4
    beside.finish()
    beside.width = 2

    def summed(oss8):
        oss = sm(4)
        V.op(V.eng.tensor_reduce, oss, oss8.rearrange("p (n g) -> p n g", g=2), AX, ALU.add, after=(A.last(),))
        return oss.rearrange("p (j b) -> p j b", j=2)

    oss = summed(oss8)

    def group_norm_out(oss, gain):
        rstd_of(oss.rearrange("p j b -> p (j b)"), 512)
        for b in range(2):
            for j in range(2):
                V.op(V.eng.tensor_scalar, Y[:, b, 512 * j:512 * j + 512], Y[:, b, 512 * j:512 * j + 512],
                     oss[:, j, b:b + 1], None, ALU.mult)
        ready = transposed(Y, gain, HT, (V.last(),))
        return add_product(ready)

    def add_product(ready):
        for i in range(2):
            m = tokens_product(HT, [4 + 2 * i, 5 + 2 * i], ready)
            for b in range(2):
                xb = X[:, b, 512 * i:512 * i + 512]
                bank_free[4 + 2 * i + b] = V.op(V.eng.tensor_tensor, xb, xb, PS[:, 4 + 2 * i + b, :], ALU.add,
                                                after=(m[b],), chain=False)
        return V.last()

    group_norm_out(oss, g_out)
    if dbg == "h":
        return finish_debug(nc, S, X, V, out)

    m = norm(X, Y)
    ht_ready = transposed(Y, g_ffn, HT, (m,))
    Z = sm(72).rearrange("p (b n) -> p b n", b=2)
    XSH = ACTS[:, 14336:16384].rearrange("p (b n) -> p b n", b=2)
    for b in range(2):
        m = A.op(A.eng.activation, fr(XSH[:, b, :]), Y[:, b, :], ACT.Copy, after=(V.last(), T.last()))
        xs_ready = G.op(G.eng.tensor_tensor, fr(Y[:, b, :]), Y[:, b, :], fr(XSH[:, b, :]).bitcast(F32), ALU.subtract,
                        after=(m, V.last(), T.last()))
    narrow_product(WR, 36, br, lambda b: Z[:, b, :], DS[:, 3072:3328], ws_ready, ht_ready)
    gmx, gsum, ge, goh, gidx = sm(2), sm(2), sm(8), sm(8), sm(2)
    b2 = lambda x: x.rearrange("p (b n) -> p b n", b=2)
    ge, goh = b2(ge), b2(goh)
    col = lambda x, n: x.rearrange("p (b o) -> p b o", o=1).broadcast_to((P, 2, n))
    V.op(V.eng.tensor_reduce, gmx, Z[:, :, 0:4], AX, ALU.max)
    V.op(V.eng.tensor_tensor, ge, Z[:, :, 0:4], col(gmx, 4), ALU.subtract)
    m = A.op(A.eng.activation, ge, ge, ACT.Exp, after=(V.last(),))
    V.op(V.eng.tensor_tensor, goh, Z[:, :, 0:4], col(gmx, 4), ALU.is_equal)
    iota4 = iota[:, 0:4].rearrange("p (o n) -> p o n", o=1).broadcast_to((P, 2, 4))
    V.op(V.eng.scalar_tensor_tensor, goh, goh, -1000.0, iota4, ALU.mult, ALU.add)
    V.op(V.eng.tensor_reduce, gidx, goh, AX, ALU.min)
    V.op(V.eng.tensor_scalar, gidx, gidx, 1000.0, None, ALU.add)
    V.op(V.eng.tensor_tensor, goh, iota4, col(gidx, 4), ALU.is_equal)
    V.op(V.eng.tensor_reduce, gsum, ge, AX, ALU.add, after=(m,))
    V.op(V.eng.reciprocal, gsum, gsum)
    zsel, prod, top8 = b2(sm(16)), DS[:, 2816:2880].rearrange("p (b e g) -> p b e g", b=2, e=8), b2(sm(16))
    for b in range(2):
        V.op(V.eng.tensor_tensor, prod[:, b], Z[:, b, 4:36].rearrange("p (g e) -> p e g", g=4),
             goh[:, b:b + 1, :].broadcast_to((P, 8, 4)), ALU.mult)
    V.op(V.eng.tensor_reduce, zsel.rearrange("p b e -> p (b e)"), prod.rearrange("p b e g -> p (b e) g"), AX, ALU.add)
    ti = nc.alloc_sbuf_tensor("ti", [P, 16], U32)
    tf = b2(sm(16))
    for b in range(2):
        V.op(V.eng.max, top8[:, b, :], zsel[:, b, :])
        V.op(V.eng.max_index, ti[:, 8 * b:8 * b + 8], top8[:, b, :], zsel[:, b, :])
    V.op(V.eng.tensor_copy, tf.rearrange("p b e -> p (b e)"), ti[:, :])
    w1, w2, wt = sm(2), sm(2), sm(2)
    V.op(V.eng.tensor_tensor, w2, top8[:, :, 1], top8[:, :, 0], ALU.subtract)
    A.op(A.eng.activation, w2, w2, ACT.Exp, after=(V.last(),))
    V.op(V.eng.tensor_scalar, wt, w2, 1.0, None, ALU.add, after=(A.last(),))
    V.op(V.eng.reciprocal, wt, wt)
    V.op(V.eng.tensor_tensor, w1, wt, gsum, ALU.mult)
    V.op(V.eng.tensor_tensor, w2, w2, w1, ALU.mult)
    e1, e2 = b2(sm(16)), b2(sm(16))
    iota8 = iota[:, 0:8].rearrange("p (o n) -> p o n", o=1).broadcast_to((P, 2, 8))
    V.op(V.eng.tensor_tensor, e1, iota8, tf[:, :, 0:1].broadcast_to((P, 2, 8)), ALU.is_equal)
    V.op(V.eng.tensor_tensor, e2, iota8, tf[:, :, 1:2].broadcast_to((P, 2, 8)), ALU.is_equal)
    MK, CB, RM = b2(sm(64)), b2(sm(64)), b2(sm(64))
    ee, ew = b2(sm(16)), b2(sm(16))
    V.op(V.eng.tensor_tensor, ee, e1, e2, ALU.add)
    V.op(V.eng.tensor_tensor, e1, e1, col(w1, 8), ALU.mult)
    V.op(V.eng.tensor_tensor, e2, e2, col(w2, 8), ALU.mult)
    V.op(V.eng.tensor_tensor, ew, e1, e2, ALU.add)
    for b in range(2):
        g4 = goh[:, b, :].rearrange("p (g o) -> p g o", o=1).broadcast_to((P, 4, 8))
        for dst, src in ((MK, ee), (CB, ew)):
            V.op(V.eng.tensor_tensor, dst[:, b, :].rearrange("p (g e) -> p g e", g=4), g4,
                 src[:, b:b + 1, :].broadcast_to((P, 4, 8)), ALU.mult)
    T.wait(V.last(), bank_free[6])
    mm(PS[:, 6, 0:32], tri[:, 0, 0:P], MK[:, 0, :], start=True, stop=True)
    mm(PS[:, 6, 32:64], tri[:, 0, P:256], MK[:, 0, :], start=True, stop=False)
    m = T.mark(mm(PS[:, 6, 32:64], tri[:, 1, P:256], MK[:, 1, :], start=False, stop=True))
    V.op(V.eng.tensor_tensor, RM.rearrange("p b e -> p (b e)"), MK.rearrange("p b e -> p (b e)"), PS[:, 6, 0:64],
         ALU.mult, after=(m,))
    bank_free[6] = V.last()
    OV, ovn = b2(sm(64)), sm(1)
    V.op(V.eng.tensor_scalar, OV.rearrange("p b e -> p (b e)"), RM.rearrange("p b e -> p (b e)"), float(CAP) + 0.5, None, ALU.is_gt)
    V.op(V.eng.tensor_reduce, ovn, OV.rearrange("p b e -> p (b e)"), AX, ALU.add)
    V.op(V.eng.tensor_tensor, OV.rearrange("p b e -> p (b e)"), OV.rearrange("p b e -> p (b e)"),
         CB.rearrange("p b e -> p (b e)"), ALU.mult)
    T.wait(V.last(), bank_free[7])
    m = T.mark(mm(PS[0:1, 7, 0:1], ovn, tri[:, 0, 127:128], start=True, stop=True))
    flag = nc.alloc_sbuf_tensor("flag", [1, 1], I32)
    flag_ready = V.op(V.eng.tensor_copy, flag[:, :], PS[0:1, 7, 0:1], after=(m,))
    bank_free[7] = flag_ready

    two = lambda o, n: [ACTS[:, o + n * i:o + n * i + n] for i in range(2)]
    XGS = [x.rearrange("p (g k s) -> p g k s", g=4, k=8) for x in two(0, 4096)]
    SDS = [x.rearrange("p (b e s) -> p b e s", b=2, e=8) for x in two(8192, 1024)]
    DWS = [x.rearrange("p (b e s) -> p b e s", b=2, e=8) for x in two(10240, 1024)]
    SCS = [x.rearrange("p (g t) -> p g t", g=4) for x in two(12288, 1024)]
    iota_s = iota[:, 1:1 + CAP].rearrange("p (o s) -> p o s", o=1).broadcast_to((P, 8, CAP))
    moe_marks = {}

    def slots_of(q):
        sd, dw = SDS[q % 2], DWS[q % 2]
        wide = lambda x, b: x[:, b, 8 * q:8 * q + 8].rearrange("p (e o) -> p e o", o=1).broadcast_to((P, 8, CAP))
        for b in range(2):
            V.op(V.eng.tensor_tensor, fr(sd[:, b]), iota_s, wide(RM, b), ALU.is_equal,
                 after=(moe_marks.get(("gathered", q - 2)),))
        sd_ready = V.last()
        for b in range(2):
            V.op(V.eng.tensor_tensor, dw[:, b], fr(sd[:, b]).bitcast(F32), wide(CB, b), ALU.mult, after=(moe_marks.get(("turned", q - 2)),))
        return sd_ready, V.last()

    def gather(q, ready, banks=(6, 7)):
        sd, xg = SDS[q % 2], XGS[q % 2]
        for k in range(8):
            bank = banks[k % len(banks)]
            T.wait(bank_free[bank], ready[0], xs_ready)
            for b in range(2):
                r = fr(sd[:, b].rearrange("p e s -> p (e s)"))
                for i, x in enumerate((XSH, Y)):
                    ins = mm(PS[:, bank, :], fr(x[:, b, :].rearrange("p (c k) -> p k c", k=8)[:, k, :]), r,
                             start=(b + i == 0), stop=(b + i == 2))
            mt = T.mark(ins)
            src = PS[:, bank, :].rearrange("p (g s) -> p g s", g=4)
            done = (moe_marks.get(("pairs", q - 2)),)
            if k % 2:
                d = A.op(A.eng.activation, xg[:, :, k, :], src, ACT.Copy, scale=g_ffn[:, k:k + 1],
                         after=(mt, *done), chain=False)
            else:
                d = V.op(V.eng.tensor_scalar, xg[:, :, k, :], src, g_ffn[:, k:k + 1], None, ALU.mult,
                         after=(mt, *done), chain=False)
            bank_free[bank] = d
        moe_marks[("gathered", q)] = mt
        return [V.last(), A.last()]

    def turn(q, ready):
        dw = DWS[q % 2]
        for c in range(2):
            bank = 6 + c
            T.wait(bank_free[bank], ready[1])
            for g in (2 * c, 2 * c + 1):
                for b in range(2):
                    ins = nc.tensor.transpose(PS[:, bank, (g % 2) * 256 + b * P:(g % 2) * 256 + (b + 1) * P],
                                              dw[:, b, 2 * g:2 * g + 2, :].rearrange("p e s -> p (e s)"), ident)
            mt = T.mark(ins)
            dst = SCS[q % 2][:, 2 * c:2 * c + 2, :].rearrange("p g t -> p (g t)")
            done = (moe_marks.get(("scattered", q - 2)),)
            if c:
                d = A.op(A.eng.activation, dst, PS[:, bank, :], ACT.Copy, after=(mt, *done), chain=False)
            else:
                d = V.op(V.eng.tensor_copy, dst, PS[:, bank, :], after=(mt, *done), chain=False)
            bank_free[bank] = d
        moe_marks[("turned", q)] = mt
        moe_marks[("gates", q)] = [V.last(), A.last()]

    HB = [DS[:, 0:512], DS[:, 512:1024]]
    HTB = DS[:, 1024:1536].rearrange("p (c s) -> p c s", c=4)
    YG = [DS[:, 2048:3072], DS[:, 3072:4096]]
    y_last = [None, None]
    yg_ready = None

    def scatter(g, ready):
        T.wait(ready, moe_marks[("gates", g // 4)], *[bank_free[i] for i in range(4)])
        sc = SCS[(g // 4) % 2]
        for b in range(2):
            for half in range(2):
                ins = mm(PS[:, 2 * b + half, :], sc[:, g % 4, b * P:(b + 1) * P],
                         YG[g % 2][:, 512 * half:512 * half + 512],
                         start=(g == 0), stop=(g == 15), skip_group_check=True)
        m = T.mark(ins)
        if g % 4 == 3:
            moe_marks[("scattered", g // 4)] = m
        return m

    def pair_product(lhs, banks_of, view, k_of):
        for h in range(2):
            (t0_, l0), (t1_, l1) = ring.take(), ring.take()
            T.wait(l0, l1)
            for k in range(k_of // 2):
                for bank, c0 in banks_of:
                    for i, t in enumerate((t0_, t1_)):
                        ins = mm(PS[64 * i:64 * i + 64, bank, :], lhs(h * k_of // 2 + k, i), view(t)[:, k, c0:c0 + 512],
                                 start=(h + k == 0), stop=(h == 1 and k == k_of // 2 - 1), skip_group_check=True)
            m = T.mark(ins)
            ring.free(m)
            ring.free(m)
        return m

    sp, u0, u1, u2 = (sm(4) for _ in range(4))
    sd_ready = slots_of(0)
    xg_ready = gather(0, sd_ready, (6, 7, 0, 1, 2, 3))
    for g in range(16):
        xg = XGS[(g // 4) % 2]
        hb = HB[g % 2]
        T.wait(*xg_ready)
        T.wait(bank_free[4])
        lhs = lambda k, i: xg[:, g % 4, k, 64 * i:64 * i + 64]
        m4 = pair_product(lhs, [(4, 0)], by_k, 8)
        T.wait(bank_free[5])
        m = pair_product(lhs, [(5, 0)], by_k, 8)
        if g == 0:
            turn(0, sd_ready)
        if g == 2:
            log1p_exp_neg_abs(lam, 4, sp, u0, u1, u2)
            V.op(V.eng.tensor_scalar, u0, lam, -1.0, 0.0, ALU.mult, ALU.max)
            V.op(V.eng.tensor_tensor, sp, sp, u0, ALU.add)
            V.op(V.eng.tensor_scalar, sp, sp, 4.0, None, ALU.mult)
        if g % 4 == 3:
            moe_marks[("pairs", g // 4)] = m
        mh = A.op(A.eng.activation, hb, PS[:, 4, :], ACT.Silu, after=(m4, T.last() if g < 2 else None))
        mh = V.op(V.eng.tensor_tensor, hb, hb, PS[:, 5, :], ALU.mult, after=(mh, m))
        bank_free[5] = mh
        if g:
            y_last[(g - 1) % 2] = scatter(g - 1, yg_ready)
        if g % 4 == 1 and g < 12:
            sd_ready = slots_of(g // 4 + 1)
        T.wait(mh)
        for c in range(4):
            ins = nc.tensor.transpose(PS[:, 4, c * P:(c + 1) * P],
                                      hb.rearrange("p (f c) -> p c f", c=4)[:, c, :], ident)
        m = T.mark(ins)
        m = V.op(V.eng.tensor_copy, HTB.rearrange("p c s -> p (c s)"), PS[:, 4, :], after=(m,))
        bank_free[4] = m
        T.wait(m, bank_free[6], bank_free[7])
        md = pair_product(lambda c, i: HTB[:, c, 64 * i:64 * i + 64], [(6, 0), (7, 512)],
                          lambda t: by_k(t, 1024, 2), 4)
        yg = YG[g % 2]
        d0 = V.op(V.eng.tensor_copy, yg[:, 0:512], PS[:, 6, :], after=(md, y_last[g % 2]))
        d1 = A.op(A.eng.activation, yg[:, 512:1024], PS[:, 7, :], ACT.Copy, after=(md, y_last[g % 2]))
        bank_free[6], bank_free[7] = d0, d1
        yg_ready = [d0, d1]
        if g % 4 == 1 and g < 12:
            xg_ready = gather(g // 4 + 1, sd_ready)
            turn(g // 4 + 1, sd_ready)
    m = scatter(15, yg_ready)
    for b in range(2):
        for half in range(2):
            xb = X[:, b, 512 * half:512 * half + 512]
            bank_free[2 * b + half] = V.op(V.eng.tensor_tensor, xb, xb, PS[:, 2 * b + half, :], ALU.add, after=(m,),
                                           chain=False)

    for lane in (G, S):
        lane.wait(flag_ready)
    overflow(nc, a, (V, A, T), flag, flag_ready, X, HT, OV, ACTS, PS)
    joined = V.op(V.eng.tensor_scalar, ss[:, 0:2], ss[:, 0:2], 1.0, None, ALU.mult)
    for lane in (A, T, G, S):
        lane.wait(joined)
    for i in range(8):
        bank_free[i] = None
    if dbg == "h2":
        return finish_debug(nc, S, X, V, out)

    R = lambda i: ACTS[:, 1024 * i:1024 * i + 1024].rearrange("p (c t) -> p c t", c=4)
    XR, XC, GT, RR, II, AA, BB, HS, QT, KT = (R(i) for i in range(10))
    VT = ACTS[:, 10240:11264].rearrange("p (b n) -> p b n", b=2)
    PB2 = [ACTS[:, o:o + 1024] for o in (11264, 12288)]
    PT2 = [ACTS[:, o:o + 1024] for o in (13312, 14336)]
    GW = ACTS[:, 15360:15872].rearrange("p (s c j) -> p s c j", s=2, c=4)
    l_g = Load(nc, "l_g")
    l_g.start(A, GW[:, 0], a["gate_a_w_2"])
    l_g.start(A, GW[:, 1], a["gate_x_w_2"])
    KM = DS[:, 0:2048].rearrange("p (c t) -> p c t", c=8)
    VM = DS[:, 2048:4096].rearrange("p (b n) -> p b n", b=2)
    SCR = ACTS[:, 15872:16384]
    halves.ahead()
    m = norm(X, Y)
    ht_ready = transposed(Y, g_mix2, HT, (m,))

    def features(ht, after, *puts):
        for put in puts:
            features_product(ht, after, put)

    def scaled(dst, scale):
        return lambda c, src, m: V.op(V.eng.tensor_scalar, dst[:, c, :], src, scale, None, ALU.mult, after=(m,), chain=False)

    features(HT, ht_ready, scaled(QT, 0.125), scaled(KT, 1.0))
    att_ready = V.last()
    att_v_ready = project(1, lambda i, b: VT[:, b, :], ht_ready)
    biases = [ring.take(), ring.take()]
    held = ring.hold(2)
    readers = [[], []]
    oss8 = sm(8)
    Y6 = Y[:, :, :].rearrange("p b (j h i d) -> p b j i h d", j=2, h=4, i=2)

    def bias_read(b):
        def note(m):
            readers[b].append(m)
            if len(readers[b]) == 2:
                ring.free_held(held[b], m)
        return note

    for b in (1, 0):
        tile, landed = biases[b]
        bias = tile[:, 0:8 * P * (b + 1)].rearrange("p (s k) -> p s k", s=8)
        for g in range(2):
            beside.add(lambda place, b=b, g=g, bias=bias, landed=landed: attend(
                place, PB2, PT2, SCR[:, 0:256], QT, KT, bias[:, 4 * g:4 * g + 4, :],
                lambda kb, h: VT[:, kb, 64 * h:64 * h + 64], b, g, Y6[:, b, 1, g], oss8[:, 4 + 2 * b + g:5 + 2 * b + g],
                lambda: (att_ready,), lambda: att_v_ready, bias_landed=landed, bias_read=bias_read(b)))

    gate_ready = []

    def recurrence(place):
        b0 = 2 * place
        for c in range(4):
            V.op(V.eng.tensor_scalar, XC[:, c, :], XR[:, c, :], cw[:, c, 3:4], cb[:, c:c + 1], ALU.mult, ALU.add)
            for w in (2, 1, 0):
                s = 3 - w
                V.op(V.eng.scalar_tensor_tensor, XC[:, c, s:256], XR[:, c, 0:256 - s], cw[:, c, w:w + 1],
                     XC[:, c, s:256], ALU.mult, ALU.add)
            if c % 2:
                yield
        conv = V.last()
        for s, (dst, bias) in enumerate(((RR, gab), (II, gxb))):
            T.wait(conv, bank_free[b0], bank_free[b0 + 1], l_g.mark())
            for c in range(4):
                at = 256 * (c % 2)
                for o in (0, 64):
                    ins = mm(PS[o:o + 64, b0 + c // 2, at:at + 256], GW[o:o + 64, s, c, :],
                             XC[o:o + 64, c, :], start=True, stop=True, skip_group_check=True)
            mt = T.mark(ins)
            yield
            for c in range(4):
                at = 256 * (c % 2)
                d = A.op(A.eng.activation, dst[:, c, :], PS[:, b0 + c // 2, at:at + 256], ACT.Sigmoid,
                         bias=bias[:, c:c + 1], after=(mt,), chain=False)
            bank_free[b0] = bank_free[b0 + 1] = d
        for c in range(4):
            A.op(A.eng.activation, RR[:, c, :], RR[:, c, :], ACT.Tanh, scale=sp[:, c:c + 1], after=(V.last(),))
        rdone = A.last()
        yield
        rf, aaf, bbf = (x.rearrange("p c t -> p (c t)") for x in (RR, AA, BB))
        hhf, xcf, iif = (x.rearrange("p c t -> p (c t)") for x in (HS, XC, II))
        V.op(V.eng.tensor_scalar, bbf, rf, 1.3e-35, None, ALU.max, after=(rdone,))
        ms = A.op(A.eng.activation, bbf, bbf, ACT.Sqrt, after=(V.last(),))
        V.op(V.eng.tensor_scalar, hhf, rf, 1.0, None, ALU.add)
        yield
        V.op(V.eng.reciprocal, hhf, hhf)
        yield
        V.op(V.eng.tensor_scalar, aaf, rf, -1.0, 1.0, ALU.mult, ALU.add)
        V.op(V.eng.tensor_tensor, aaf, aaf, hhf, ALU.mult)
        yield
        V.op(V.eng.tensor_tensor, xcf, xcf, iif, ALU.mult)
        V.op(V.eng.scalar_tensor_tensor, xcf, xcf, 2.0, hhf, ALU.mult, ALU.mult)
        yield
        V.op(V.eng.tensor_tensor, bbf, bbf, xcf, ALU.mult, after=(ms,))
        for c in range(4):
            V.op(V.eng.tensor_tensor_scan, HS[:, c, :], AA[:, c, :], BB[:, c, :], 0.0, ALU.mult, ALU.add)
            if c == 1:
                yield
        m = V.op(V.eng.tensor_tensor, hhf, hhf, GT.rearrange("p c t -> p (c t)"), ALU.mult, after=(gate_ready,))
        yield
        marks = []
        for b in range(2):
            T.wait(m, bank_free[b0 + b])
            for c in range(4):
                ins = nc.tensor.transpose(PS[:, b0 + b, c * P:(c + 1) * P], HS[:, c, b * P:(b + 1) * P], ident)
            marks.append(T.mark(ins))
        yield
        for b in range(2):
            d = V.op(V.eng.tensor_copy, Y[:, b, 0:512], PS[:, b0 + b, :], after=(marks[b],))
            bank_free[b0 + b] = d
            A.op(A.eng.activation, SCR, Y[:, b, 0:512], ACT.Square, accum_out=oss8[:, 2 * b:2 * b + 1], after=(d,))

    for b in range(2):
        V.op(V.eng.tensor_scalar, oss8[:, 2 * b + 1:2 * b + 2], iota[:, 0:1], 0.0, None, ALU.mult)
    features(HT, ht_ready, scaled(XR, 1.0))
    beside.waiting.insert(0, (recurrence, lambda: True))
    features(HT, ht_ready, lambda c, src, m: A.op(A.eng.activation, GT[:, c, :], src, ACT.Gelu_apprx_tanh, after=(m,),
                                                  chain=False))
    gate_ready.append(A.last())
    features(MT, mt_ready, scaled(KM[:, 0:4], 1.0), scaled(KM[:, 4:8], 1.0))
    project(2, lambda i, b: VM[:, b, 512 * i:512 * i + 512], mt_ready, ht=MT)
    kv_ready = [V.last(), A.last()]
    beside.finish()
    group_norm_out(summed(oss8), g_grp)
    if dbg == "x1":
        return finish_debug(nc, S, X, V, out)

    QM = ACTS[:, 6144:8192].rearrange("p (c t) -> p c t", c=8)
    PMS = [ACTS[:, o:o + 1024].rearrange("p (h k) -> p h k", h=4) for o in (8192, 10240)]
    PTMS = [ACTS[:, o:o + 1024].rearrange("p (b n) -> p b n", b=2) for o in (9216, 11264)]
    m = norm(X, Y)
    ht_ready = transposed(Y, g_cross, HT, (m,))
    features(HT, ht_ready, scaled(QM[:, 0:4], 1.0 / 16), scaled(QM[:, 4:8], 1.0 / 16))
    q_ready = V.last()

    def attend_memory(place, b):
        b0 = 2 * place
        S4 = PS[:, b0:b0 + 2, :].rearrange("p a (c k) -> p (a c) k", k=256)
        pm, pt = PMS[place], PTMS[place]
        mx, nm, lsum, rl = mxs[place], nms[place], lsums[place], rls[place]
        T.wait(q_ready, kv_ready, bank_free[b0], bank_free[b0 + 1])
        for h in range(4):
            for c in range(2):
                ins = mm(S4[:, h, :], QM[:, 2 * h + c, b * P:(b + 1) * P], KM[:, 2 * h + c, :],
                         start=(c == 0), stop=(c == 1))
        m = T.mark(ins)
        yield
        V.op(V.eng.tensor_reduce, mx, S4, AX, ALU.max, after=(m,))
        ready_e = V.op(V.eng.tensor_scalar, nm, mx, -1.0, None, ALU.mult)
        for h in range(4):
            e = A.op(A.eng.activation, pm[:, h, :], S4[:, h, :], ACT.Exp, bias=nm[:, h:h + 1],
                     accum_out=lsum[:, h:h + 1], after=(ready_e,), chain=False)
        bank_free[b0] = bank_free[b0 + 1] = e
        yield
        rec = V.op(V.eng.reciprocal, rl, lsum, after=(e,))
        marks = []
        for kb in range(2):
            T.wait(bank_free[b0 + kb])
            for h in range(4):
                ins = nc.tensor.transpose(PS[:, b0 + kb, h * P:(h + 1) * P], pm[:, h, kb * P:(kb + 1) * P], ident)
            marks.append(T.mark(ins))
        yield
        copied = [V.op(V.eng.tensor_copy, pt[:, 0, :], PS[:, b0, :], after=(marks[0],), chain=False),
                  A.op(A.eng.activation, pt[:, 1, :], PS[:, b0 + 1, :], ACT.Copy, after=(marks[1],), chain=False)]
        yield
        T.wait(copied)
        for h in range(4):
            for kb in range(2):
                ins = mm(PS[:, b0 + h // 2, (h % 2) * 256:(h % 2) * 256 + 256], pt[:, kb, h * P:(h + 1) * P],
                         VM[:, kb, 256 * h:256 * h + 256], start=(kb == 0), stop=(kb == 1))
        m = T.mark(ins)
        yield
        for i in range(2):
            d = V.op(V.eng.tensor_tensor, Y[:, b, 512 * i:512 * i + 512].rearrange("p (h d) -> p h d", h=2),
                     PS[:, b0 + i, :].rearrange("p (h d) -> p h d", h=2),
                     rl[:, 2 * i:2 * i + 2].rearrange("p (n o) -> p n o", o=1).broadcast_to((P, 2, 256)), ALU.mult,
                     after=(m, rec))
            bank_free[b0 + i] = d

    for b in range(2):
        beside.add(lambda place, b=b: attend_memory(place, b))
    beside.finish()
    ready = transposed(Y, None, HT, (V.last(),))
    add_product(ready)
    if dbg == "x2":
        return finish_debug(nc, S, X, V, out)

    m = norm(X, Y)
    ht_ready = transposed(Y, g_ffn2, HT, (m,))
    QP = DS[:, 0:4096].rearrange("p (j t) -> p j t", j=16)
    SC = DS[:, 4096:8192].rearrange("p (b j n) -> p b j n", b=2, j=16)

    def split_next():
        return halves.split(*ring.take())

    features(HT, ht_ready, *(scaled(QP[:, 4 * i:4 * i + 4], 1.0) for i in range(4)))
    tile, landed = ring.take()
    cur = split_next()
    SK = tile[:, 0:2048].rearrange("p (j n) -> p j n", j=16)
    q_ready = V.last()
    for b in range(2):
        for q in range(4):
            bank = 4 * b + q
            T.wait(bank_free[bank], q_ready, landed)
            for j in range(4 * q, 4 * q + 4):
                ins = mm(PS[:, bank, (j % 4) * P:(j % 4 + 1) * P], QP[:, j, b * P:(b + 1) * P], SK[:, j, :],
                         start=True, stop=True)
            m = T.mark(ins)
            bank_free[bank] = A.op(A.eng.activation, SC[:, b, 4 * q:4 * q + 4, :].rearrange("p j n -> p (j n)"),
                                   PS[:, bank, :], ACT.Copy, after=(m,), chain=False)
    ring.free(m)
    sc_ready = A.last()

    xkeep = nc.dram_tensor("xkeep", (P, 2 * D), F32, kind="Internal").ap()
    xf = X[:, :, :].rearrange("p b n -> p (b n)")
    l_k = Load(nc, "l_k")
    x_kept = l_k.start(A, xkeep, xf, after=(V.last(),))
    halves.bufs.append(xf)
    halves.used.append(x_kept)
    halves.n = len(halves.bufs) - 1

    W = BIG[:, :].rearrange("p (n t) -> p n t", n=128)
    keys = (tig[:, 0:256], tig[:, 256:512], tig[:, 512:768])
    steps = routing(nc, V, A, T, SC, DS, Y, iota, ident, keys, PS, bank_free, sm, sc_ready)
    rest = ROUTING_SHARE

    for i in range(64):
        nxt = split_next() if i < 63 else None
        while rest >= 0:
            cost = next(steps, None)
            if cost is None:
                break
            rest -= cost
        assert i < 48 or cost is None
        rest += ROUTING_SHARE
        hi, lo, ready, buf = cur
        bank = 4 + i % 2
        T.wait(ready, *ht_ready, bank_free[bank])
        for j in range(2):
            for k in range(8):
                at = 1024 * j + 128 * k
                ins = pass3(PS[:, bank, 256 * j:256 * j + 256], [x[:, at:at + P] for x in (hi, lo)],
                            [x[:, k, :] for x in HT], k == 0, k == 7)
        m = T.mark(ins)
        halves.free(buf, m)
        ring.free(m)
        bank_free[bank] = A.op(A.eng.activation, W[:, 2 * i:2 * i + 2, :].rearrange("p n t -> p (n t)"), PS[:, bank, :],
                               ACT.Gelu_apprx_tanh, after=(m, V.last() if i == 48 else None), chain=False)
        cur = nxt
    act_ready, u_done, routed = A.last(), T.last(), V.last()

    cur = split_next()
    I1T, I2T, GTT = keys
    EB = [x[:, :, :].rearrange("p k t -> p (k t)") for x in (HH, HL)]
    E1 = [EB[i // 2][:, 1024 * (i % 2):1024 * (i % 2) + 512] for i in range(4)]
    E2 = [EB[i // 2][:, 1024 * (i % 2) + 512:1024 * (i % 2) + 1024] for i in range(4)]
    used = [u_done] * 4

    def weigh(q, ready):
        bank = 4 + q % 4
        w = W[:, :, 4 * q:4 * q + 4]
        bank_free[bank] = V.op(V.eng.tensor_tensor, w, PS[:, bank, :].rearrange("p (t n) -> p n t", t=4), w, ALU.mult,
                               after=(ready, act_ready), chain=False)

    yflat = Y[:, :, :].rearrange("p b n -> p (b n)")
    NG = yflat[:, 1536:1792]
    SQS = [[yflat[:, 256 * j + 128 * i:256 * j + 128 * i + 128] for i in range(2)] for j in range(2)]
    squared = [None] * 2
    ng_ready = V.op(V.eng.tensor_scalar, NG, GTT, -1.0, None, ALU.mult)
    ready = []
    G.wait(routed)
    for q in range(64):
        i, bank = q % 4, 4 + q % 4
        by = (A, A, G, V if q % 2 else G)
        built = []
        scalars = [t for t in range(4) if by[t] is A]
        SQ = SQS[q % 2]
        sq = [A.op(A.eng.activation, SQ[t], iota, ACT.Square, scale=-1.0, bias=I2T[:, 4 * q + t:4 * q + t + 1],
                   after=(used[i], ng_ready, squared[q % 2]), chain=False) for t in scalars]
        for t in scalars:
            tt = 4 * q + t
            built.append(A.op(A.eng.activation, E2[i][:, t * P:(t + 1) * P], SQ[t], ACT.Relu, scale=NG[:, tt:tt + 1],
                              bias=GTT[:, tt:tt + 1], after=(sq[t],), chain=False))
        squared[q % 2] = A.last()
        for t in range(4):
            tt, lane = 4 * q + t, by[t]
            if lane is not A:
                built.append(lane.op(lane.eng.tensor_scalar, E2[i][:, t * P:(t + 1) * P], iota, I2T[:, tt:tt + 1],
                                     GTT[:, tt:tt + 1], ALU.is_equal, ALU.mult, after=(used[i],), chain=False))
        built.append(V.op(V.eng.tensor_tensor, E1[i].rearrange("p (t n) -> p t n", t=4),
                          iota.rearrange("p (o n) -> p o n", o=1).broadcast_to((P, 4, P)),
                          I1T[:, 4 * q:4 * q + 4].rearrange("p (t o) -> p t o", o=1).broadcast_to((P, 4, P)),
                          ALU.is_equal, after=(used[i],), chain=False))
        T.wait(built, bank_free[bank])
        for t in range(4):
            ins = mm(PS[:, bank, t * P:(t + 1) * P], E1[i][:, t * P:(t + 1) * P], E2[i][:, t * P:(t + 1) * P],
                     start=True, stop=True)
        used[i] = T.mark(ins)
        ready.append(used[i])
        if q:
            weigh(q - 1, ready[q - 1])
    weigh(63, ready[63])
    w_ready = V.last()

    XB, gf = HH[:, :, :].rearrange("p k t -> p (k t)").rearrange("p (b n) -> p b n", b=2), EB[1][:, 0:1024]
    l_f = Load(nc, "l_f")
    l_f.start(A, XB, xkeep.rearrange("p (b n) -> p b n", b=2), after=(used, x_kept))
    l_f.start(A, gf, a["norm_final_2"].rearrange("(o n) -> o n", o=1).broadcast_to((P, D)))

    WH = [yflat[:, 512 * i:512 * i + 512] for i in range(3)]
    wh_used = [None] * 3

    def split_w(i):
        w = W[:, 2 * i:2 * i + 2, :].rearrange("p n t -> p (n t)")
        h = WH[i % 3]
        ma = A.op(A.eng.activation, fr(h), w, ACT.Copy, after=(w_ready, wh_used[i % 3], squared), chain=False)
        mv = V.op(V.eng.tensor_tensor, fr(w), w, fr(h).bitcast(F32), ALU.subtract, after=(ma,), chain=False)
        return [fr(x).rearrange("p (n t) -> p n t", n=2) for x in (h, w)], mv

    wcur = split_w(0)
    for i in range(64):
        if i < 63:
            nxt, wnxt = split_next(), split_w(i + 1)
        hi, lo, r1, buf = cur
        w, r2 = wcur
        T.wait(r1, r2, *[bank_free[q] for q in range(4)])
        for j in range(2):
            for b in range(2):
                for half in range(2):
                    at = 1024 * j + 512 * half
                    o = PS[:, 2 * b + half, :]
                    l = [x[:, j, b * P:(b + 1) * P] for x in w]
                    r = [x[:, at:at + 512] for x in (hi, lo)]
                    mm(o, l[0], r[0], start=(i + j == 0), stop=False, skip_group_check=True)
                    mm(o, l[0], r[1], start=False, stop=False, skip_group_check=True)
                    ins = mm(o, l[1], r[0], start=False, stop=(i == 63 and j == 1), skip_group_check=True)
        m = T.mark(ins)
        halves.free(buf, m)
        wh_used[i % 3] = m
        ring.free(m)
        cur, wcur = nxt, wnxt
    root_ahead()
    for b in range(2):
        for half in range(2):
            xb = XB[:, b, 512 * half:512 * half + 512]
            V.op(V.eng.tensor_tensor, xb, xb, PS[:, 2 * b + half, :], ALU.add, after=(m, l_f.mark()), chain=False)
        A.op(A.eng.activation, Y[:, b, :], XB[:, b, :], ACT.Square, accum_out=ss[:, b:b + 1], after=(V.last(), m))
    rstd_of(ss[:, 0:2], D)
    l_o = Load(nc, "l_o")
    for b in range(2):
        V.op(V.eng.scalar_tensor_tensor, Y[:, b, :], XB[:, b, :], ss[:, b:b + 1], gf, ALU.mult, ALU.mult)
        l_o.start(S, out[0, b * P:(b + 1) * P, :], Y[:, b, :], after=(V.last(),))
    S.wait(l_o.mark())


def finish_debug(nc, S, X, V, out):
    l_o = Load(nc, "l_o")
    for b in range(2):
        l_o.start(S, out[0, b * P:(b + 1) * P, :], X[:, b, :], after=(V.last(),))
    S.wait(l_o.mark())


def overflow(nc, a, lanes, flag, flag_ready, X, HT, OV, ACTS, PS):
    mains = lanes
    for lane in mains:
        lane.wait(flag_ready, *[o.last() for o in mains])
    V, A, T = (Lane(nc, o.eng, f"{o.name}_ov") for o in mains)
    WG, WU, WD = (ACTS[:, 4096 * i:4096 * i + 4096] for i in range(3))
    wg, wu = (w.rearrange("p (k n) -> p k n", k=8) for w in (WG, WU))
    wd = WD.rearrange("p (c n) -> p c n", c=4)
    HU = ACTS[:, 12288:13312].rearrange("p (c t) -> p c t", c=4)
    parts = [x.bitcast(F32).rearrange("p k t -> p (k t)") for x in HT]
    HF = ACTS[:, 13312:15360]
    HT = HF.rearrange("p (k t) -> p k t", k=8)
    l_w = Load(nc, "l_ov")

    per_t, per_a, per_v = 4 * 2 + 2, 4, 4 + 4

    def t_mark(e, i):
        return (T.sem, per_t * e + i + 1)

    def a_mark(e, i):
        return (A.sem, per_a * e + i + 1)

    def v_mark(e, i):
        return (V.sem, per_v * e + i + 2)

    def body_tensor():
        for e in range(32):
            T.wait((l_w.sem, 48 * (e + 1)), (V.sem, 1))
            for c in range(4):
                for s, w in enumerate((wg, wu)):
                    bank = 2 * (c % 2) + s
                    if c >= 2:
                        T.wait(v_mark(e, c - 2))
                    elif e:
                        T.wait(v_mark(e - 1, 2 + c))
                    for k in range(8):
                        ins = nc.tensor.matmul(
                            PS[:, bank, 0:256],
                            w.rearrange("p k (f c) -> p k c f", c=4)[:, k, c, :], HT[:, k, :],
                            start=(k == 0), stop=(k == 7))
                    T.mark(ins)
            T.wait(v_mark(e, 3))
            if e:
                T.wait(v_mark(e - 1, 7))
            for b in range(2):
                for half in range(2):
                    for c in range(4):
                        ins = nc.tensor.matmul(PS[:, 4 + 2 * b + half, :], HU[:, c, b * P:(b + 1) * P],
                                               wd[:, c, 512 * half:512 * half + 512], start=(c == 0), stop=(c == 3))
                T.mark(ins)

    def body_scalar():
        for e in range(32):
            if e:
                A.wait(t_mark(e - 1, 9))
            for dst, n, k in ((WG, "w_gate", 8), (WU, "w_up", 8), (WD, "w_down", 4)):
                l_w.start(A, dst, a[n][0, e].rearrange("(p k) n -> p (k n)", k=k))
            for c in range(4):
                A.wait(t_mark(e, 2 * c))
                A.mark(nc.scalar.activation(HU[:, c, :], PS[:, 2 * (c % 2), 0:256], ACT.Silu))

    def body_vector():
        V.mark(nc.vector.tensor_tensor(HF, parts[0], parts[1], ALU.add))
        for e in range(32):
            for c in range(4):
                V.wait(a_mark(e, c), t_mark(e, 2 * c + 1))
                V.mark(nc.vector.tensor_tensor(HU[:, c, :], HU[:, c, :], PS[:, 2 * (c % 2) + 1, 0:256], ALU.mult))
            for b in range(2):
                V.wait(t_mark(e, 8 + b))
                if e:
                    V.wait(v_mark(e - 1, 4 + 2 * b + 1))
                for half in range(2):
                    xb = X[:, b, 512 * half:512 * half + 512]
                    V.mark(nc.vector.scalar_tensor_tensor(xb, PS[:, 4 + 2 * b + half, :], OV[:, b, e:e + 1], xb,
                                                          ALU.mult, ALU.add))
        V.wait(V.last(), (A.sem, per_a * 32), (T.sem, per_t * 32))

    value = nc.values_load(flag[0:1, 0:1], min_val=0, max_val=8192)
    with nc.If(value > 0):
        body_tensor()
        body_scalar()
        body_vector()


def routing(nc, V, A, T, SC, DS, Y, iota, ident, keys, PS, bank_free, sm, sc_ready):
    HK = 128
    at = [0]
    yf = Y[:, :, :].rearrange("p b n -> p (b n)")

    def part(n):
        s = yf[:, at[0]:at[0] + n]
        at[0] += n
        return s

    v, ixf, tv, pa, pb_, i1s, i2s, gg = (part(n) for n in (256, 256, 128, 128, 128, 128, 128, 128))
    ix = part(256).bitcast(U32)
    S2 = DS[:, 0:2048].rearrange("p (j n) -> p j n", j=16)
    CAND = DS[:, 0:2048].rearrange("p (h n) -> p h n", h=8)
    TMP = DS[:, 2048:4096]
    hs = sm(8)
    pos = pa.bitcast(U32)
    posb = pb_.bitcast(U32)

    V.wait(sc_ready, T.last())
    for b in range(2):
        for j in range(16):
            s, s2 = SC[:, b, j, :], S2[:, j, :]
            vj, ij = v[:, 16 * j:16 * j + 16], ix[:, 16 * j:16 * j + 16]
            V.op(V.eng.max, vj[:, 0:8], s)
            yield 270
            V.op(V.eng.match_replace, s2, vj[:, 0:8], s, -3.0e38)
            yield 270
            V.op(V.eng.max, vj[:, 8:16], s2)
            yield 270
            V.op(V.eng.max_index, ij[:, 0:8], vj[:, 0:8], s, chain=False)
            yield 270
            V.op(V.eng.max_index, ij[:, 8:16], vj[:, 8:16], s2)
            yield 270
        V.op(V.eng.tensor_copy, ixf, ix)
        yield 330
        vv = v.rearrange("p (h s n) -> p h s n", h=8, s=2)
        for h in range(8):
            V.op(V.eng.tensor_tensor, CAND[:, h, :].rearrange("p (x y) -> p x y", x=16),
                 vv[:, h, 0, :].rearrange("p (n o) -> p n o", o=1).broadcast_to((P, 16, 16)),
                 vv[:, h, 1:2, :].broadcast_to((P, 16, 16)), ALU.add)
            yield 330
        C2 = SC[:, b, :, :].rearrange("p (h j) n -> p h (j n)", h=8)
        for h in range(8):
            th, ph = tv[:, 16 * h:16 * h + 16], pos[:, 16 * h:16 * h + 16]
            V.op(V.eng.max, th[:, 0:8], CAND[:, h, :])
            yield 400
            V.op(V.eng.match_replace, C2[:, h, :], th[:, 0:8], CAND[:, h, :], -3.0e38)
            yield 400
            V.op(V.eng.max, th[:, 8:16], C2[:, h, :])
            yield 400
            V.op(V.eng.max_index, ph[:, 0:8], th[:, 0:8], CAND[:, h, :], chain=False)
            yield 400
            V.op(V.eng.max_index, ph[:, 8:16], th[:, 8:16], C2[:, h, :])
            yield 400
        t8 = tv.rearrange("p (h k) -> p h k", h=8)
        g8 = gg.rearrange("p (h k) -> p h k", h=8)
        V.op(V.eng.tensor_tensor, g8, t8, t8[:, :, 0:1].broadcast_to((P, 8, 16)), ALU.subtract)
        yield 190
        m = A.op(A.eng.activation, gg, gg, ACT.Exp, after=(V.last(),))
        V.op(V.eng.tensor_scalar, posb, pos, 15, None, ALU.bitwise_and)
        yield 190
        V.op(V.eng.tensor_scalar, pos, pos, 4, None, ALU.logical_shift_right)
        yield 190
        V.op(V.eng.tensor_copy, i1s, pos)
        yield 190
        V.op(V.eng.tensor_copy, i2s, posb)
        yield 190
        xf = ixf.rearrange("p (h s n) -> p h s n", h=8, s=2)
        T4 = TMP.rearrange("p (h k n) -> p h k n", h=8, k=16)
        i16 = iota[:, 0:16].rearrange("p (o n) -> p o n", o=1).broadcast_to((P, HK, 16))
        for s, sel in enumerate((i1s, i2s)):
            V.op(V.eng.tensor_tensor, TMP.rearrange("p (k n) -> p k n", n=16), i16,
                 sel.rearrange("p (k o) -> p k o", o=1).broadcast_to((P, HK, 16)), ALU.is_equal)
            yield 2200
            for h in range(8):
                V.op(V.eng.tensor_tensor, T4[:, h], T4[:, h], xf[:, h, s:s + 1, :].broadcast_to((P, 16, 16)),
                     ALU.mult, chain=(h == 0))
                yield 330
            V.op(V.eng.tensor_reduce, sel, TMP.rearrange("p (k n) -> p k n", n=16), AX, ALU.add)
            yield 2200
        V.op(V.eng.tensor_reduce, hs, g8, AX, ALU.add, after=(m,))
        yield 80
        V.op(V.eng.reciprocal, hs, hs)
        yield 80
        mg = V.op(V.eng.tensor_tensor, g8, g8, hs.rearrange("p (h o) -> p h o", o=1).broadcast_to((P, 8, 16)), ALU.mult)
        yield ROUTING_SHARE
        T.wait(mg, bank_free[6])
        for i, src in enumerate((i1s, i2s, gg)):
            ins = nc.tensor.transpose(PS[:, 6, i * P:(i + 1) * P], src, ident)
        mt = T.mark(ins)
        yield ROUTING_SHARE
        for i, dst in enumerate(keys):
            d = V.op(V.eng.tensor_copy, dst[:, b * P:(b + 1) * P], PS[:, 6, i * P:(i + 1) * P], after=(mt,))
            yield 190
        bank_free[6] = d


_RAW = ["x", "w_in", "w_out", "w_gate", "w_up", "w_down", "mem_2", "w_in_2", "w_out_2", "w_q_mem_2",
        "w_kv_mem_2", "w_o_mem_2", "w_query_2", "norm_final_2"]


def _constants():
    t = np.arange(256)
    q, k = t[:, None], t[None, :]
    by_tile = lambda m: np.ascontiguousarray(m.reshape(2, 128, -1).transpose(1, 0, 2), dtype=np.float32)
    causal = k <= q
    count = (causal & (q - k <= 128)).astype(int) + (causal & ((q - k) % 4 == 0)) + (causal & ((q - k) % 16 == 0))
    inv = 1.0 / (np.float32(10000.0) ** (np.arange(0, 64, 2, dtype=np.float32) / np.float32(64)))
    ang = t.astype(np.float32)[:, None] * inv.astype(np.float32)[None, :]
    rope = np.stack([by_tile(np.cos(ang)), by_tile(np.sin(ang))], axis=1)
    sel = np.zeros((8, 8, 128), np.float32)
    for h in range(8):
        sel[h, h] = 1.0
    return {
        "c_ii": np.ascontiguousarray(np.stack([np.eye(128, dtype=np.float32), np.tile(np.arange(128, dtype=np.float32), (128, 1))], axis=1)),
        "c_tri": by_tile((q <= k).astype(np.float32)),
        "c_fox": by_tile(np.where(causal, 0.0, NEG)),
        "c_dil": by_tile(np.where(count > 0, np.log(np.maximum(count, 1)), NEG)),
        "c_rope": np.ascontiguousarray(rope, dtype=np.float32),
        "c_sel": sel,
    }


def _laid_out(i):
    c = np.ascontiguousarray
    out = {n: c(i[n]) for n in _RAW}
    k = _constants()
    out |= {n: k[n] for n in ("c_ii", "c_tri", "c_sel")}
    vec = lambda v: v.reshape(128, 8)
    every = lambda v: np.broadcast_to(v.reshape(1, -1), (128, v.size))
    chunks = lambda v: v.reshape(4, 128).T
    pack = [vec(i["norm_mix"]), vec(np.concatenate([i["out_norm_fox"][0], i["out_norm_dil"][0]])),
            vec(i["norm_ffn"]), vec(i["norm_mix_2"]), vec(i["norm_cross_2"]), vec(i["norm_mem_2"]),
            vec(i["norm_ffn_2"]), vec(np.concatenate([i["norm_grp_a_2"][0], i["norm_grp_b_2"][0]])),
            np.tile(i["q_norm_fox"][0], 2)[:, None], np.tile(i["k_norm_fox"][0], 2)[:, None],
            every(i["b_forget"]), every(i["b_router_group"]), every(i["b_router_expert"]),
            i["conv_w_2"][0].reshape(4, 4, 128).transpose(2, 1, 0).reshape(128, 16),
            chunks(i["conv_b_2"][0]), chunks(i["gate_a_b_2"][0]), chunks(i["gate_x_b_2"][0]),
            chunks(i["lru_lambda_2"][0])]
    out["pack"] = c(np.concatenate(pack, axis=1))
    we = i["w_router_expert"][0].transpose(1, 0, 2).reshape(1024, 32)
    wr = np.concatenate([i["w_router_group"][0], we], axis=1)
    flat = lambda v: v.reshape(128, -1)
    out["pack_acts"] = c(np.concatenate(
        [flat(k["c_fox"]), flat(k["c_dil"]), flat(k["c_rope"]), every(i["q_norm_dil"]), every(i["k_norm_dil"]),
         flat(c(i["w_in"][0][:, 3072:3080])), flat(wr)], axis=1))
    for n in ("gate_a_w_2", "gate_x_w_2"):
        out[n] = c(i[n][0].reshape(4, 2, 64, 64).transpose(1, 2, 0, 3).reshape(128, 4, 64))
    t = np.arange(256)
    rel = np.clip(t[:, None] - t[None, :], -128, 128) + 128
    rel = np.where(t[None, :] // 64 <= t[:, None] // 64, rel, 257)
    ext = np.concatenate([i["rel_bias_2"][0], np.full((8, 1), NEG, np.float32)], axis=1)
    slots = [2 * (s % 4) + s // 4 for s in range(8)]
    bias = ext[slots][:, rel].transpose(1, 0, 2)
    out["bias_2"] = c(np.concatenate([bias[:128, :, :128].reshape(128, -1), bias[128:].reshape(128, -1)], axis=1))
    out["sub_keys_2"] = c(i["sub_keys_2"][0].transpose(3, 0, 1, 2).reshape(128, 2048))
    u = i["expert_u_2"][0].reshape(128, 32, 4, 128, 8)
    out["expert_u_2"] = c(u.transpose(1, 3, 2, 4, 0).reshape(32, 128, 4096))
    v = i["expert_v_2"][0].reshape(128, 32, 4096)
    out["expert_v_2"] = c(v.transpose(1, 0, 2))
    return out


def kernel(**inputs):
    import concourse.bacc as _bacc
    from concourse.bass_utils import run_bass_kernel_spmd as _run

    nc = _bacc.Bacc("TRN2", target_bir_lowering=False, num_devices=1)
    arrays = _laid_out({k: np.asarray(v) for k, v in inputs.items()})
    aps, send = {}, {}
    for name, v in arrays.items():
        send[f"in_{name}"] = v
        aps[name] = nc.dram_tensor(f"in_{name}", v.shape, mybir.dt.from_np(v.dtype), kind="ExternalInput").ap()
    out = nc.dram_tensor("out_0", (1, 256, 1024), F32, kind="ExternalOutput").ap()
    program(nc, aps, out)
    r = _run(nc, [send], core_ids=[0])
    return r.results[0]["out_0"]
```
